# Optimizing a Trainium2 kernel written in Bass

```python
import math
import jax, jax.numpy as jnp
from jax import lax
import numpy as np

D_MODEL = 1024
BATCH = 1
SEQ = 1024
DEPTH = 1

N_META = 16
SSM_WIDTH = 1024
SSM_GROUP = 16
SSM_GROUPS = SSM_WIDTH // SSM_GROUP
SSM_STATE = 64
DT_MIN = 1e-3
DT_MAX = 1e-1
HGRN_WIDTH = 1024
HGRN_HEAD_DIM = 128
HGRN_HEADS = HGRN_WIDTH // HGRN_HEAD_DIM
HGRN_CHUNK = 16
D_FF = 2816
CONV_WIDTH = 3
EPS = 1e-6
IN_COLS = SSM_WIDTH + 4 * HGRN_WIDTH + 2 * D_MODEL


def rmsnorm(x, g):
    xf = x.astype(jnp.float32)
    y = xf * lax.rsqrt(jnp.mean(xf * xf, axis=-1, keepdims=True) + EPS)
    return (y * g.astype(jnp.float32)).astype(x.dtype)

def _complex_affine_combine(e1, e2):
    a1r, a1i, b1r, b1i = e1
    a2r, a2i, b2r, b2i = e2
    ar = a1r * a2r - a1i * a2i
    ai = a1r * a2i + a1i * a2r
    br = a2r * b1r - a2i * b1i + b2r
    bi = a2r * b1i + a2i * b1r + b2i
    return ar, ai, br, bi

def s5_mixer(u, lam_re, lam_im, log_dt, b_re, b_im, c_re, c_im, d_skip, w_glu):
    bsz, L, _ = u.shape
    uf = u.astype(jnp.float32).reshape(bsz, L, SSM_GROUPS, SSM_GROUP)
    lr = lam_re.astype(jnp.float32)
    li = lam_im.astype(jnp.float32)
    dt = jnp.exp(log_dt.astype(jnp.float32))[:, None]
    mag = jnp.exp(lr * dt)
    ab_re = mag * jnp.cos(li * dt)
    ab_im = mag * jnp.sin(li * dt)
    den = lr * lr + li * li
    nr = ab_re - 1.0
    coef_re = (nr * lr + ab_im * li) / den
    coef_im = (ab_im * lr - nr * li) / den
    br = b_re.astype(jnp.float32)
    bi = b_im.astype(jnp.float32)
    bb_re = coef_re[..., None] * br - coef_im[..., None] * bi
    bb_im = coef_re[..., None] * bi + coef_im[..., None] * br
    v_re = jnp.einsum('blgh,gph->blgp', uf, bb_re)
    v_im = jnp.einsum('blgh,gph->blgp', uf, bb_im)
    a_re = jnp.broadcast_to(ab_re[None, None], (1, L, SSM_GROUPS, SSM_STATE))
    a_im = jnp.broadcast_to(ab_im[None, None], (1, L, SSM_GROUPS, SSM_STATE))
    _, _, s_re, s_im = lax.associative_scan(_complex_affine_combine, (a_re, a_im, v_re, v_im), axis=1)
    y = (jnp.einsum('blgp,ghp->blgh', s_re, c_re.astype(jnp.float32))
         - jnp.einsum('blgp,ghp->blgh', s_im, c_im.astype(jnp.float32))
         + d_skip.astype(jnp.float32).reshape(SSM_GROUPS, SSM_GROUP) * uf)
    y = jax.nn.gelu(y.reshape(bsz, L, SSM_WIDTH)).astype(u.dtype)
    return y * jax.nn.sigmoid(y @ w_glu)

def hgrn2_mixer(q, f_logit, i_in, og, lb, norm_g):
    bsz, L, _ = q.shape
    n_chunks = L // HGRN_CHUNK

    def heads(t):
        return t.reshape(bsz, n_chunks, HGRN_CHUNK, HGRN_HEADS, HGRN_HEAD_DIM).transpose(1, 0, 3, 2, 4)

    lbf = lb.astype(jnp.float32)
    f = lbf + (1.0 - lbf) * jax.nn.sigmoid(f_logit.astype(jnp.float32))
    log_f = jnp.log(f)
    qh = heads(q.astype(jnp.float32))
    kh = heads(1.0 - f)
    vh = heads(i_in.astype(jnp.float32))
    cum = jnp.cumsum(heads(log_f), axis=3)
    q_in = qh * jnp.exp(cum)
    k_in = kh * jnp.exp(-cum)
    k_out = kh * jnp.exp(cum[..., -1:, :] - cum)
    chunk_decay = jnp.exp(cum[..., -1, :])
    causal = jnp.tril(jnp.ones((HGRN_CHUNK, HGRN_CHUNK), dtype=bool))

    def chunk_step(state, xs):
        qi, ki, ko, v, dec = xs
        scores = jnp.where(causal, jnp.einsum('bhtd,bhsd->bhts', qi, ki), 0.0)
        o = jnp.einsum('bhts,bhsv->bhtv', scores, v) + jnp.einsum('bhtd,bhdv->bhtv', qi, state)
        state = dec[..., None] * state + jnp.einsum('bhsd,bhsv->bhdv', ko, v)
        return state, o

    init = jnp.zeros((bsz, HGRN_HEADS, HGRN_HEAD_DIM, HGRN_HEAD_DIM), jnp.float32)
    _, o = lax.scan(chunk_step, init, (q_in, k_in, k_out, vh, chunk_decay))
    o = o.transpose(1, 0, 3, 2, 4).reshape(bsz, L, HGRN_HEADS, HGRN_HEAD_DIM)
    o = o * lax.rsqrt(jnp.mean(o * o, axis=-1, keepdims=True) + EPS) * norm_g.astype(jnp.float32)
    o = o.reshape(bsz, L, HGRN_WIDTH).astype(q.dtype)
    return o * jax.nn.silu(og)

def causal_dwconv(u, w, b):
    L = u.shape[1]
    up = jnp.pad(u, ((0, 0), (CONV_WIDTH - 1, 0), (0, 0)))
    out = b
    for j in range(CONV_WIDTH):
        out = out + up[:, j:j + L, :] * w[j]
    return out

def first_inputs(seed: int = 0) -> dict:
    key = jax.random.key(seed)
    ks = jax.random.split(key, 24)
    f32 = jnp.float32

    def nrm(k, shape, scale):
        return jax.random.normal(k, shape, f32) * scale

    n_idx = jnp.arange(SSM_STATE, dtype=f32)
    return {
        'x': nrm(ks[0], (BATCH, SEQ, D_MODEL), 1.0),
        'meta_tokens': nrm(ks[1], (N_META, D_MODEL), 1.0),
        'mix_norm_g': 1.0 + nrm(ks[2], (DEPTH, D_MODEL), 0.02),
        'w_in': nrm(ks[3], (DEPTH, D_MODEL, IN_COLS), D_MODEL ** -0.5),
        'ssm_lambda_re': -0.5 + nrm(ks[4], (DEPTH, SSM_GROUPS, SSM_STATE), 0.01),
        'ssm_lambda_im': math.pi * n_idx + nrm(ks[5], (DEPTH, SSM_GROUPS, SSM_STATE), 0.01),
        'ssm_log_dt': jax.random.uniform(ks[6], (DEPTH, SSM_GROUPS), f32, math.log(DT_MIN), math.log(DT_MAX)),
        'ssm_b_re': nrm(ks[7], (DEPTH, SSM_GROUPS, SSM_STATE, SSM_GROUP), (2 * SSM_GROUP) ** -0.5),
        'ssm_b_im': nrm(ks[8], (DEPTH, SSM_GROUPS, SSM_STATE, SSM_GROUP), (2 * SSM_GROUP) ** -0.5),
        'ssm_c_re': nrm(ks[9], (DEPTH, SSM_GROUPS, SSM_GROUP, SSM_STATE), SSM_STATE ** -0.5),
        'ssm_c_im': nrm(ks[10], (DEPTH, SSM_GROUPS, SSM_GROUP, SSM_STATE), SSM_STATE ** -0.5),
        'ssm_d': nrm(ks[11], (DEPTH, SSM_WIDTH), 1.0),
        'ssm_w_glu': nrm(ks[12], (DEPTH, SSM_WIDTH, SSM_WIDTH), SSM_WIDTH ** -0.5),
        'w_ssm_proj': nrm(ks[13], (DEPTH, SSM_WIDTH, D_MODEL), SSM_WIDTH ** -0.5),
        'hgrn_lb_logits': nrm(ks[14], (DEPTH + 1, HGRN_WIDTH), 0.1),
        'hgrn_norm_g': 1.0 + nrm(ks[15], (DEPTH, HGRN_HEAD_DIM), 0.02),
        'w_hgrn_proj': nrm(ks[16], (DEPTH, HGRN_WIDTH, D_MODEL), HGRN_WIDTH ** -0.5),
        'w_out': nrm(ks[17], (DEPTH, D_MODEL, D_MODEL), D_MODEL ** -0.5),
        'ffn_norm_g': 1.0 + nrm(ks[18], (DEPTH, D_MODEL), 0.02),
        'w_up': nrm(ks[19], (DEPTH, D_MODEL, 2 * D_FF), D_MODEL ** -0.5),
        'conv_w': nrm(ks[20], (DEPTH, CONV_WIDTH, 2 * D_FF), CONV_WIDTH ** -0.5),
        'conv_b': nrm(ks[21], (DEPTH, 2 * D_FF), 0.01),
        'w_down': nrm(ks[22], (DEPTH, D_FF, D_MODEL), D_FF ** -0.5),
        'final_norm_g': 1.0 + nrm(ks[23], (D_MODEL,), 0.02),
    }

def first_block(x, meta_tokens, mix_norm_g, w_in, ssm_lambda_re, ssm_lambda_im, ssm_log_dt,
              ssm_b_re, ssm_b_im, ssm_c_re, ssm_c_im, ssm_d, ssm_w_glu, w_ssm_proj,
              hgrn_lb_logits, hgrn_norm_g, w_hgrn_proj, w_out, ffn_norm_g, w_up, conv_w,
              conv_b, w_down, final_norm_g):
    bsz = x.shape[0]
    meta = jnp.broadcast_to(meta_tokens.astype(x.dtype)[None], (bsz, N_META, D_MODEL))
    h = jnp.concatenate([meta, x], axis=1)
    lower_bounds = jnp.cumsum(jax.nn.softmax(hgrn_lb_logits.astype(jnp.float32), axis=0), axis=0)
    o1 = SSM_WIDTH
    o2 = o1 + HGRN_WIDTH
    o3 = o2 + HGRN_WIDTH
    o4 = o3 + HGRN_WIDTH
    o5 = o4 + HGRN_WIDTH
    o6 = o5 + D_MODEL
    for l in range(DEPTH):
        z = rmsnorm(h, mix_norm_g[l])
        p = z @ w_in[l]
        y_a = s5_mixer(p[..., :o1], ssm_lambda_re[l], ssm_lambda_im[l], ssm_log_dt[l],
                       ssm_b_re[l], ssm_b_im[l], ssm_c_re[l], ssm_c_im[l], ssm_d[l], ssm_w_glu[l])
        y_b = hgrn2_mixer(p[..., o1:o2], p[..., o2:o3], p[..., o3:o4], p[..., o4:o5],
                          lower_bounds[l], hgrn_norm_g[l])
        merged = (jax.nn.sigmoid(p[..., o5:o6]) * (y_a @ w_ssm_proj[l])
                  + jax.nn.sigmoid(p[..., o6:]) * (y_b @ w_hgrn_proj[l]))
        h = h + merged @ w_out[l]
        z = rmsnorm(h, ffn_norm_g[l])
        u = causal_dwconv(z @ w_up[l], conv_w[l], conv_b[l])
        h = h + (jax.nn.silu(u[..., :D_FF]) * u[..., D_FF:]) @ w_down[l]
    return rmsnorm(h[:, N_META:], final_norm_g)


DEPTH_2 = 2

GRID_W = 64
CTX_LEN = 256
POOL_WINDOWS = (2, 4, 8, 16)
POOL_GROUPS = len(POOL_WINDOWS)
POOL_GROUP_DIM = D_MODEL // 8
POOL_WIDTH = POOL_GROUPS * POOL_GROUP_DIM
SGU_HEADS = 4
SGU_HEAD_DIM = D_MODEL // 8
SGU_WIDTH = SGU_HEADS * SGU_HEAD_DIM
CHUNK = 128
AB_IN = 2 * POOL_WIDTH + 3 * SGU_WIDTH
AB_MIX = POOL_WIDTH + SGU_WIDTH
FNET_HEADS = 4
FNET_HEAD_DIM = D_MODEL // 8
FNET_WIDTH = FNET_HEADS * FNET_HEAD_DIM
MLA_HEADS = 8
QK_NOPE = 64
QK_ROPE = 32
V_DIM = 64
Q_LORA = D_MODEL // 4
KV_LORA = D_MODEL // 8
MLA_WIDTH = MLA_HEADS * V_DIM
CD_IN = 2 * FNET_WIDTH + Q_LORA + KV_LORA + QK_ROPE + MLA_WIDTH
CD_MIX = FNET_WIDTH + MLA_WIDTH
ROPE_AXIS = QK_ROPE // 2
ROPE_BASE = 10000.0
Q_BLOCK = 128
ALPHA = (2 * DEPTH_2) ** 0.25
BETA = (8 * DEPTH_2) ** -0.25
N_EVEN = (DEPTH_2 + 1) // 2
N_ODD = DEPTH_2 // 2


def _layer_norm(x, g, b):
    xf = x.astype(jnp.float32)
    mu = jnp.mean(xf, axis=-1, keepdims=True)
    var = jnp.mean(jnp.square(xf - mu), axis=-1, keepdims=True)
    return ((xf - mu) * lax.rsqrt(var + EPS) * g + b).astype(x.dtype)

def _rms_norm(x, g):
    xf = x.astype(jnp.float32)
    y = xf * lax.rsqrt(jnp.mean(jnp.square(xf), axis=-1, keepdims=True) + EPS)
    return (y * g).astype(x.dtype)

def _adaln(cond, w_mod, b_mod):
    m = jax.nn.silu(cond) @ w_mod + b_mod
    return jnp.split(m, 3, axis=-1)

def _post_norm(x, y, gate, g, b):
    return _layer_norm(ALPHA * x + gate * y, g, b)

def _multiscale_pool(a, pool_w, pool_scale):
    bn, L, _ = a.shape
    cs = jnp.cumsum(a.astype(jnp.float32), axis=1)
    cs = jnp.pad(cs, ((0, 0), (1, 0), (0, 0)))
    t = jnp.arange(L)
    outs = []
    for g, w in enumerate(POOL_WINDOWS):
        lo = jnp.clip(t - w // 2, 0, L)
        hi = jnp.clip(t + w - w // 2, 0, L)
        seg = cs[:, :, g * POOL_GROUP_DIM:(g + 1) * POOL_GROUP_DIM]
        s = jnp.take(seg, hi, axis=1) - jnp.take(seg, lo, axis=1)
        outs.append(s / (hi - lo).astype(jnp.float32)[None, :, None])
    pooled = jnp.concatenate(outs, axis=-1).astype(a.dtype)
    d = (pooled - a).reshape(bn, L, POOL_GROUPS, POOL_GROUP_DIM)
    y = jnp.einsum('blgc,gcd->blgd', d, pool_w).reshape(bn, L, POOL_WIDTH)
    return y * pool_scale

def _chunk_sgu(u, v, w_s, b_s):
    bn, L, _ = v.shape
    nc = L // CHUNK
    vh = v.reshape(bn, L, SGU_HEADS, SGU_HEAD_DIM).astype(jnp.float32)
    mu = jnp.mean(vh, axis=-1, keepdims=True)
    var = jnp.mean(jnp.square(vh - mu), axis=-1, keepdims=True)
    vn = ((vh - mu) * lax.rsqrt(var + EPS)).astype(v.dtype)
    vn = vn.reshape(bn, nc, CHUNK, SGU_HEADS, SGU_HEAD_DIM)
    f = jnp.einsum('hij,bnjhc->bnihc', w_s, vn) + jnp.swapaxes(b_s, 0, 1)[:, :, None]
    return u * f.reshape(bn, L, SGU_WIDTH)

def _ab_mixer(h, w_in, pool_w, pool_scale, sgu_w, sgu_b, w_out):
    z = h @ w_in
    a, ga, u, v, gb = jnp.split(z, [POOL_WIDTH, 2 * POOL_WIDTH, 2 * POOL_WIDTH + SGU_WIDTH,
                                    2 * POOL_WIDTH + 2 * SGU_WIDTH], axis=-1)
    ya = _multiscale_pool(a, pool_w, pool_scale) * jax.nn.silu(ga)
    yb = _chunk_sgu(u, v, sgu_w, sgu_b) * jax.nn.silu(gb)
    return jnp.concatenate([ya, yb], axis=-1) @ w_out

def _fourier_mix(f, w_f):
    bn, L, _ = f.shape
    fh = f.reshape(bn, L, FNET_HEADS, FNET_HEAD_DIM).astype(jnp.float32)
    spec = jnp.fft.fft2(fh, axes=(1, 3), norm="ortho").real
    return spec.astype(f.dtype).reshape(bn, L, FNET_WIDTH) @ w_f

def _axial_tables(L, dtype):
    rows = L // GRID_W
    row = jnp.repeat(jnp.arange(rows), GRID_W).astype(jnp.float32)
    col = jnp.tile(jnp.arange(GRID_W), rows).astype(jnp.float32)
    inv = ROPE_BASE ** (-jnp.arange(0, ROPE_AXIS, 2, dtype=jnp.float32) / ROPE_AXIS)
    ang_r = (row[:, None] * inv)[:, None, :]
    ang_c = (col[:, None] * inv)[:, None, :]
    return (jnp.cos(ang_r).astype(dtype), jnp.sin(ang_r).astype(dtype),
            jnp.cos(ang_c).astype(dtype), jnp.sin(ang_c).astype(dtype))

def _rotate(x, cos, sin):
    half = x.shape[-1] // 2
    x1, x2 = x[..., :half], x[..., half:]
    return jnp.concatenate([x1 * cos - x2 * sin, x1 * sin + x2 * cos], axis=-1)

def _axial_rope(x, rope):
    cos_r, sin_r, cos_c, sin_c = rope
    return jnp.concatenate([_rotate(x[..., :ROPE_AXIS], cos_r, sin_r),
                            _rotate(x[..., ROPE_AXIS:], cos_c, sin_c)], axis=-1)

def _split_cd(z):
    o1 = FNET_WIDTH
    o2 = o1 + FNET_WIDTH
    o3 = o2 + Q_LORA
    o4 = o3 + KV_LORA
    o5 = o4 + QK_ROPE
    return jnp.split(z, [o1, o2, o3, o4, o5], axis=-1)

def _mla_q(cq, q_norm, w_q_up, rope):
    bn, L, _ = cq.shape
    q = (_rms_norm(cq, q_norm) @ w_q_up).reshape(bn, L, MLA_HEADS, QK_NOPE + QK_ROPE)
    if rope is not None:
        q = jnp.concatenate([q[..., :QK_NOPE], _axial_rope(q[..., QK_NOPE:], rope)], axis=-1)
    return q

def _mla_kv(ckv, kr, kv_norm, w_kv_up, rope):
    bn, L, _ = ckv.shape
    kv = (_rms_norm(ckv, kv_norm) @ w_kv_up).reshape(bn, L, MLA_HEADS, QK_NOPE + V_DIM)
    k_nope, v = kv[..., :QK_NOPE], kv[..., QK_NOPE:]
    kr = kr[:, :, None, :]
    if rope is not None:
        kr = _axial_rope(kr, rope)
    k = jnp.concatenate([k_nope, jnp.broadcast_to(kr, (bn, L, MLA_HEADS, QK_ROPE))], axis=-1)
    return k, v

def _block_attention(q, k, v):
    bn, L, H, dk = q.shape
    nb = L // Q_BLOCK
    scale = dk ** -0.5
    qb = q.reshape(bn, nb, Q_BLOCK, H, dk).transpose(1, 0, 2, 3, 4)

    def one(qi):
        s = jnp.einsum('bqhd,bkhd->bhqk', qi, k, preferred_element_type=jnp.float32) * scale
        p = jax.nn.softmax(s, axis=-1).astype(v.dtype)
        return jnp.einsum('bhqk,bkhd->bqhd', p, v)

    o = lax.map(one, qb)
    return o.transpose(1, 0, 2, 3, 4).reshape(bn, L, H * V_DIM)

def _cd_out(f_in, f_gate, attn, d_gate, fnet_w, w_out):
    yc = _fourier_mix(f_in, fnet_w) * jax.nn.silu(f_gate)
    yd = attn * jax.nn.silu(d_gate)
    return jnp.concatenate([yc, yd], axis=-1) @ w_out

def second_inputs(seed: int = 0) -> dict:
    key = jax.random.key(seed)
    ks = jax.random.split(key, 32)

    def nrm(k, shape, scale):
        return jax.random.normal(k, shape, jnp.float32) * scale

    D = D_MODEL
    H = MLA_HEADS
    return {
        "x": nrm(ks[0], (BATCH, SEQ, D), 1.0),
        "c": nrm(ks[1], (BATCH, D), 1.0),
        "ctx": nrm(ks[2], (BATCH, CTX_LEN, D), 1.0),
        "c_ctx": nrm(ks[3], (D,), 1.0),
        "ab_w_mod": nrm(ks[4], (N_EVEN, D, 3 * D), 0.5 * D ** -0.5),
        "ab_b_mod": nrm(ks[5], (N_EVEN, 3 * D), 0.01),
        "ab_w_in": nrm(ks[6], (N_EVEN, D, AB_IN), D ** -0.5),
        "ab_pool_w": nrm(ks[7], (N_EVEN, POOL_GROUPS, POOL_GROUP_DIM, POOL_GROUP_DIM), POOL_GROUP_DIM ** -0.5),
        "ab_pool_scale": 1.0 + nrm(ks[8], (N_EVEN, POOL_WIDTH), 0.1),
        "ab_sgu_w": nrm(ks[9], (N_EVEN, SGU_HEADS, CHUNK, CHUNK), CHUNK ** -0.5),
        "ab_sgu_b": 1.0 + nrm(ks[10], (N_EVEN, SGU_HEADS, CHUNK), 0.01),
        "ab_w_out": nrm(ks[11], (N_EVEN, AB_MIX, D), BETA * AB_MIX ** -0.5),
        "ab_ln_g": 1.0 + nrm(ks[12], (N_EVEN, D), 0.1),
        "ab_ln_b": nrm(ks[13], (N_EVEN, D), 0.01),
        "cd_w_mod": nrm(ks[14], (N_ODD, D, 3 * D), 0.5 * D ** -0.5),
        "cd_b_mod": nrm(ks[15], (N_ODD, 3 * D), 0.01),
        "cd_w_in": nrm(ks[16], (N_ODD, D, CD_IN), D ** -0.5),
        "cd_fnet_w": nrm(ks[17], (N_ODD, FNET_WIDTH, FNET_WIDTH), FNET_WIDTH ** -0.5),
        "cd_q_norm": 1.0 + nrm(ks[18], (N_ODD, Q_LORA), 0.1),
        "cd_kv_norm": 1.0 + nrm(ks[19], (N_ODD, KV_LORA), 0.1),
        "cd_w_q_up": nrm(ks[20], (N_ODD, Q_LORA, H * (QK_NOPE + QK_ROPE)), Q_LORA ** -0.5),
        "cd_w_kv_up": nrm(ks[21], (N_ODD, KV_LORA, H * (QK_NOPE + V_DIM)), KV_LORA ** -0.5),
        "cd_w_out": nrm(ks[22], (N_ODD, CD_MIX, D), BETA * CD_MIX ** -0.5),
        "cd_ln_g": 1.0 + nrm(ks[23], (N_ODD, D), 0.1),
        "cd_ln_b": nrm(ks[24], (N_ODD, D), 0.01),
    }

def second_block(x, c, ctx, c_ctx,
              ab_w_mod, ab_b_mod, ab_w_in, ab_pool_w, ab_pool_scale, ab_sgu_w, ab_sgu_b,
              ab_w_out, ab_ln_g, ab_ln_b,
              cd_w_mod, cd_b_mod, cd_w_in, cd_fnet_w, cd_q_norm, cd_kv_norm, cd_w_q_up,
              cd_w_kv_up, cd_w_out, cd_ln_g, cd_ln_b):
    L = x.shape[1]
    rope = _axial_tables(L, x.dtype)
    for i in range(DEPTH_2):
        last = i == DEPTH_2 - 1
        j = i // 2
        if i % 2 == 0:
            sh, sc, gt = _adaln(c, ab_w_mod[j], ab_b_mod[j])
            h = x * (1.0 + sc[:, None]) + sh[:, None]
            y = _ab_mixer(h, ab_w_in[j], ab_pool_w[j], ab_pool_scale[j], ab_sgu_w[j], ab_sgu_b[j], ab_w_out[j])
            if not last:
                csh, csc, cgt = _adaln(c_ctx, ab_w_mod[j], ab_b_mod[j])
                hc = ctx * (1.0 + csc) + csh
                yc = _ab_mixer(hc, ab_w_in[j], ab_pool_w[j], ab_pool_scale[j], ab_sgu_w[j], ab_sgu_b[j], ab_w_out[j])
                ctx = _post_norm(ctx, yc, cgt, ab_ln_g[j], ab_ln_b[j])
            x = _post_norm(x, y, gt[:, None], ab_ln_g[j], ab_ln_b[j])
        else:
            csh, csc, cgt = _adaln(c_ctx, cd_w_mod[j], cd_b_mod[j])
            hc = ctx * (1.0 + csc) + csh
            fc_in, fc_gate, cq_c, ckv_c, kr_c, dc_gate = _split_cd(hc @ cd_w_in[j])
            k_ctx, v_ctx = _mla_kv(ckv_c, kr_c, cd_kv_norm[j], cd_w_kv_up[j], None)
            sh, sc, gt = _adaln(c, cd_w_mod[j], cd_b_mod[j])
            h = x * (1.0 + sc[:, None]) + sh[:, None]
            f_in, f_gate, cq, ckv, kr, d_gate = _split_cd(h @ cd_w_in[j])
            k_lat, v_lat = _mla_kv(ckv, kr, cd_kv_norm[j], cd_w_kv_up[j], rope)
            q = _mla_q(cq, cd_q_norm[j], cd_w_q_up[j], rope)
            attn = _block_attention(q, jnp.concatenate([k_ctx, k_lat], axis=1),
                                    jnp.concatenate([v_ctx, v_lat], axis=1))
            y = _cd_out(f_in, f_gate, attn, d_gate, cd_fnet_w[j], cd_w_out[j])
            if not last:
                qc = _mla_q(cq_c, cd_q_norm[j], cd_w_q_up[j], None)
                attn_c = _block_attention(qc, k_ctx, v_ctx)
                yc = _cd_out(fc_in, fc_gate, attn_c, dc_gate, cd_fnet_w[j], cd_w_out[j])
                ctx = _post_norm(ctx, yc, cgt, cd_ln_g[j], cd_ln_b[j])
            x = _post_norm(x, y, gt[:, None], cd_ln_g[j], cd_ln_b[j])
    return x


def setup_inputs(seed=0):
    out = dict(first_inputs(seed))
    for name, value in second_inputs(seed + 1).items():
        if name != "x":
            out[name + "_2"] = value
    return out


def reference(
    x, meta_tokens, mix_norm_g, w_in, ssm_lambda_re, ssm_lambda_im, ssm_log_dt, ssm_b_re,
    ssm_b_im, ssm_c_re, ssm_c_im, ssm_d, ssm_w_glu, w_ssm_proj, hgrn_lb_logits, hgrn_norm_g,
    w_hgrn_proj, w_out, ffn_norm_g, w_up, conv_w, conv_b, w_down, final_norm_g, c_2, ctx_2,
    c_ctx_2, ab_w_mod_2, ab_b_mod_2, ab_w_in_2, ab_pool_w_2, ab_pool_scale_2, ab_sgu_w_2,
    ab_sgu_b_2, ab_w_out_2, ab_ln_g_2, ab_ln_b_2, cd_w_mod_2, cd_b_mod_2, cd_w_in_2,
    cd_fnet_w_2, cd_q_norm_2, cd_kv_norm_2, cd_w_q_up_2, cd_w_kv_up_2, cd_w_out_2, cd_ln_g_2,
    cd_ln_b_2,
):
    x = first_block(
        x, meta_tokens, mix_norm_g, w_in, ssm_lambda_re, ssm_lambda_im, ssm_log_dt, ssm_b_re,
        ssm_b_im, ssm_c_re, ssm_c_im, ssm_d, ssm_w_glu, w_ssm_proj, hgrn_lb_logits, hgrn_norm_g,
        w_hgrn_proj, w_out, ffn_norm_g, w_up, conv_w, conv_b, w_down, final_norm_g,
    )
    return second_block(
        x, c_2, ctx_2, c_ctx_2, ab_w_mod_2, ab_b_mod_2, ab_w_in_2, ab_pool_w_2, ab_pool_scale_2,
        ab_sgu_w_2, ab_sgu_b_2, ab_w_out_2, ab_ln_g_2, ab_ln_b_2, cd_w_mod_2, cd_b_mod_2,
        cd_w_in_2, cd_fnet_w_2, cd_q_norm_2, cd_kv_norm_2, cd_w_q_up_2, cd_w_kv_up_2,
        cd_w_out_2, cd_ln_g_2, cd_ln_b_2,
    )


_drawn_inputs = setup_inputs


def setup_inputs(seed=0):
    import zlib

    import numpy as np

    out = dict(_drawn_inputs(seed))
    spreads = {}
    factors = {'mix_norm_g': 3.55,
     'ssm_lambda_re': 64.0,
     'ssm_lambda_im': 3.138,
     'ssm_log_dt': 3.21,
     'ssm_b_re': 4.493,
     'ssm_b_im': 4.443,
     'ssm_c_re': 4.468,
     'ssm_c_im': 4.458,
     'hgrn_norm_g': 8.0,
     'ffn_norm_g': 4.077,
     'conv_b': 7.816,
     'final_norm_g': 2.891,
     'ctx_2': 8.0,
     'c_ctx_2': 8.0,
     'ab_b_mod_2': 8.0,
     'ab_pool_scale_2': 8.0,
     'ab_sgu_b_2': 8.0,
     'ab_ln_b_2': 5.548,
     'cd_b_mod_2': 8.0,
     'cd_q_norm_2': 8.0,
     'cd_kv_norm_2': 8.0,
     'cd_w_q_up_2': 8.0,
     'cd_w_kv_up_2': 4.381,
     'cd_ln_b_2': 5.703,
     'cd_fnet_w_2': 2.93}
    for name, (base, spread) in spreads.items():
        noise = np.random.default_rng([zlib.crc32(name.encode()), seed]).standard_normal(out[name].shape)
        drawn = base * np.exp(spread * noise) if base else spread * noise
        out[name] = __import__('jax').numpy.asarray(drawn.astype(out[name].dtype))
    for name, factor in factors.items():
        out[name] = (out[name] * factor).astype(out[name].dtype)
    return out
```

```python
from contextlib import ExitStack, contextmanager

import numpy as np

import concourse.bass as bass
from concourse import mybir

F32 = mybir.dt.float32
F32R = mybir.dt.float32r
ACT = mybir.ActivationFunctionType
ALU = mybir.AluOpType
AX = mybir.AxisListType

P = 128
D = 1024
DT = D // P
SEQ, META = 1024, 16
T1 = 1056
EPS = 1e-6
G, SG, SS = 64, 16, 64
TAU = 8
NCH = T1 // TAU
NPAIR = G // 2
HH = 8
CH = 32
NC = T1 // CH
FF = 2816
FT = FF // P
CTX = 256
T2 = SEQ + CTX
ALPHA = 4.0 ** 0.25
POOLS = (2, 4, 8, 16)
NH, NOPE, ROPE, VD = 8, 64, 32, 64
QL, KVL = 256, 128


class Halves:

    def __init__(self, first, second):
        self.parts, self.half = (first, second), first.shape[1]

    def __getitem__(self, key):
        p, k, n = key
        return self.parts[k // self.half][p, k % self.half, n]


def pieces(n):
    if n == T1:
        return [(b, 352 * b, 352) for b in range(3)]
    return [(b, 512 * b, min(512, n - 512 * b)) for b in range((n + 511) // 512)]


def pview(ps, n):
    if n == T1:
        return ps.rearrange("p (b x) -> p b x", b=3)[:, :, 0:352]
    return ps[:, 0:n]


def sview(ap, n):
    return ap.rearrange("p (b x) -> p b x", b=3) if n == T1 else ap


class Phase:

    def __init__(self, nc, name):
        self.nc, self.name, self.ctx, self.sems = nc, name, ExitStack(), []

    def __enter__(self):
        return self

    def sb(self, name, shape, dt=F32):
        return self.ctx.enter_context(self.nc.sbuf_tensor(f"{self.name}_{name}", list(shape), dt))

    def ps(self, name, shape, dt=F32):
        return self.ctx.enter_context(self.nc.psum_tensor(f"{self.name}_{name}", list(shape), dt))

    def sem(self, name):
        s = self.nc.alloc_semaphore(f"{self.name}_{name}")
        self.sems.append(s)
        return s

    def __exit__(self, *exc):
        if exc[0] is None:
            self.nc.clear_and_free_semaphores(self.sems)
            self.nc.all_engine_barrier()
            self.ctx.close()


class Chain:

    def __init__(self, eng, sem, n=0):
        self.eng, self.sem, self.n = eng, sem, n

    def inc(self, ins):
        ins.then_inc(self.sem, 1)
        self.n = self.n + 1
        return self.n

    def do(self, ins):
        self.eng.wait_ge(self.sem, self.inc(ins))

    @contextmanager
    def loop(self, trips, per):
        base = self.n
        with self.eng.Fori(0, trips) as i:
            self.n = base + i * per
            yield i
        self.n = base + trips * per


def split_matmuls(pe, ps, wh, wl, xh, xl, kt, n):
    mm = None
    for b, c0, w in pieces(n):
        o = ps[:, 512 * b:512 * b + w]
        for k in range(kt):
            terms = ((wh, xh), (wl, xh), (wh, xl))
            for t, (a, x) in enumerate(terms):
                mm = pe.matmul(o, a[:, k * P:(k + 1) * P], x[:, k, c0:c0 + w],
                               start=(k == 0 and t == 0), stop=(k == kt - 1 and t == 2))
    return mm


def dense(nc, name, weights, mt, kt, x, n, epi, sides=(), side_at=None, store=None, extra=None, steps=(0, 0),
          off=0):
    assert mt % 2 == 0
    weights = weights[off:off + mt]
    with Phase(nc, name) as ph:
        stage = [ph.sb(f"wstage{j}", (P, kt * P)) for j in range(2)]
        wh = [ph.sb(f"whigh{j}", (P, kt * P), F32R) for j in range(2)]
        wl = [ph.sb(f"wlow{j}", (P, kt * P), F32R) for j in range(2)]
        side = [[ph.sb(f"side{s}_{j}", (P, n)) for j in range(2)] for s in range(len(sides))]
        out = [ph.sb(f"out{j}", (P, n)) for j in range(2)]
        ps = [ph.ps(f"psum{j}", (P, 1536)) for j in range(2)]
        w_landed = [ph.sem(f"weights_landed{j}") for j in range(2)]
        side_landed = [[ph.sem(f"side{s}_landed{j}") for j in range(2)] for s in range(len(sides))]
        out_stored = [ph.sem(f"out_stored{j}") for j in range(2)]
        high_ready, low_ready = ph.sem("high_ready"), ph.sem("low_ready")
        psum_full, psum_free = ph.sem("psum_full"), ph.sem("psum_free")
        out_ready = ph.sem("out_ready")
        act_step, dve_step = ph.sem("act_step"), ph.sem("dve_step")

        class E:
            pass
        e = E()
        e.ph, e.side, e.out, e.ps, e.n = ph, side, out, ps, n
        e.psum_free, e.out_ready, e.act_step, e.dve_step = psum_free, out_ready, act_step, dve_step
        e.psum_full, e.side_landed = psum_full, side_landed
        act_epi, dve_epi = epi(e)
        half = mt // 2
        ns = len(sides)

        with nc.Block() as block:
            @block.sync
            def _(sp):
                def load(m, j, i):
                    sp.dma_start(stage[j][:, :], weights[m]).then_inc(w_landed[j], 16)

                def load_sides(m, j):
                    for s in range(ns):
                        sp.dma_start(side[s][j][:, :], side_at(s, sides[s], m)).then_inc(side_landed[s][j], 16)

                def put(m, j):
                    if store is not None:
                        sp.wait_ge(out_ready, m + 1)
                        sp.dma_start(store(m), out[j][:, :]).then_inc(out_stored[j], 16)

                for j in range(2):
                    load(j, j, 0)
                    load_sides(j, j)
                if half > 1:
                    with sp.Fori(0, half - 1) as i:
                        for j in range(2):
                            sp.wait_ge(low_ready, 2 * i + j + 1)
                            load(2 * i + j + 2, j, i)
                        for j in range(2 if ns or store is not None else 0):
                            sp.wait_ge(out_ready, 2 * i + j + 1)
                            put(2 * i + j, j)
                            load_sides(2 * i + j + 2, j)
                for j in range(2):
                    put(mt - 2 + j, j)
                if store is not None:
                    for j in range(2):
                        sp.wait_ge(out_stored[j], 16 * half)

            @block.tensor
            def _(pe):
                with pe.Fori(0, half) as i:
                    for j in range(2):
                        pe.wait_ge(low_ready, 2 * i + j + 1)
                        pe.wait_ge(psum_free, 2 * i + j + 1)
                        split_matmuls(pe, ps[j], wh[j], wl[j], x[0], x[1], kt, n).then_inc(psum_full, 1)

            @block.scalar
            def _(act):
                ch = Chain(act, act_step)

                def high(m, j, i):
                    act.wait_ge(w_landed[j], 16 * (i + 1))
                    act.activation(wh[j][:, :], stage[j][:, :], ACT.Copy).then_inc(high_ready, 1)

                def one(m, j, i):
                    act.wait_ge(psum_full, m + 1)
                    act_epi(act, m, j, i, ch)

                for j in range(2):
                    high(j, j, 0)
                if half > 1:
                    with ch.loop(half - 1, int(2 * steps[0])) as i:
                        for j in range(2):
                            one(2 * i + j, j, i)
                            high(2 * i + j + 2, j, i + 1)
                for j in range(2):
                    one(mt - 2 + j, j, half - 1)

            @block.vector
            def _(dve):
                ch = Chain(dve, dve_step)

                def low(m, j, i):
                    dve.wait_ge(high_ready, m + 1)
                    dve.tensor_tensor(wl[j][:, :], stage[j][:, :], wh[j][:, :].bitcast(F32),
                                      ALU.subtract).then_inc(low_ready, 1)

                def one(m, j, i):
                    dve.wait_ge(psum_full, m + 1)
                    if store is not None and i is not None:
                        dve.wait_ge(out_stored[j], 16 * i)
                    dve_epi(dve, m, j, i, ch)

                dve.sem_inc(psum_free, 2)
                for j in range(2):
                    low(j, j, 0)
                for j in range(2):
                    dve.wait_ge(psum_full, j + 1)
                    dve_epi(dve, j, j, 0, ch)
                    if half > 1:
                        low(j + 2, j, 1)
                if half > 2:
                    base = ch.n
                    with dve.Fori(1, half - 1) as i:
                        ch.n = base + (i - 1) * int(2 * steps[1])
                        for j in range(2):
                            one(2 * i + j, j, i)
                            low(2 * i + j + 2, j, i + 1)
                    ch.n = base + (half - 2) * int(2 * steps[1])
                if half > 1:
                    for j in range(2):
                        one(mt - 2 + j, j, half - 1)

            if extra is not None:
                extra(block, e)


def split(dve, ch, hi, lo, v):
    ch.do(dve.tensor_scalar(hi, v, 1.0, None, ALU.mult))
    return dve.tensor_tensor(lo, v, hi.bitcast(F32), ALU.subtract)


def inverse_rms(nc, name, acc, out, rows, c, n):
    with Phase(nc, name) as ph:
        ps = ph.ps("sum", (P, 1536))
        root = ph.sb("root", (P, n))
        summed, rooted, done = ph.sem("summed"), ph.sem("rooted"), ph.sem("done")
        with nc.Block() as block:
            @block.tensor
            def _(pe):
                for b, c0, w in pieces(n):
                    mm = pe.matmul(ps[:, 512 * b:512 * b + w], c["ones"][:, :], acc[:, c0:c0 + w],
                                   start=True, stop=True)
                mm.then_inc(summed, 1)

            @block.scalar
            def _(act):
                act.wait_ge(summed, 1)
                act.activation(sview(root[:, :], n), pview(ps, n), ACT.Sqrt, bias=c["eps"][:, 0:1],
                               scale=1.0 / rows).then_inc(rooted, 1)

            @block.vector
            def _(dve):
                dve.wait_ge(rooted, 1)
                dve.reciprocal(out[:, :], root[:, :]).then_inc(done, 1)
                dve.wait_ge(done, 1)


def prepare_input(nc, c, x_in, x, acc):
    with Phase(nc, "pre") as ph:
        t = [ph.sb(f"t{j}", (P, T1)) for j in range(2)]
        s = [ph.sb(f"s{j}", (P, T1)) for j in range(2)]
        v = ph.sb("v", (P, T1))
        landed = [ph.sem(f"landed{j}") for j in range(2)]
        squared, used, step = ph.sem("squared"), ph.sem("used"), ph.sem("step")
        with nc.Block() as block:
            @block.sync
            def _(sp):
                for m in range(DT):
                    if m >= 2:
                        sp.wait_ge(used, m - 1)
                    sp.dma_start(t[m % 2][:, :], x_in[m]).then_inc(landed[m % 2], 16)

            @block.scalar
            def _(act):
                for m in range(DT):
                    act.wait_ge(landed[m % 2], 16 * (m // 2 + 1))
                    if m >= 2:
                        act.wait_ge(used, m - 1)
                    act.activation(s[m % 2][:, :], t[m % 2][:, :], ACT.Square).then_inc(squared, 1)

            @block.vector
            def _(dve):
                ch = Chain(dve, step)
                for m in range(DT):
                    dve.wait_ge(landed[m % 2], 16 * (m // 2 + 1))
                    ch.do(dve.tensor_scalar(v[:, :], t[m % 2][:, :], c["mix_g"][:, m:m + 1], None, ALU.mult))
                    ch.do(split(dve, ch, x[0][:, m, :], x[1][:, m, :], v[:, :]))
                    dve.wait_ge(squared, m + 1)
                    if m == 0:
                        ins = dve.tensor_copy(acc[:, :], s[0][:, :])
                    else:
                        ins = dve.tensor_tensor(acc[:, :], acc[:, :], s[m % 2][:, :], ALU.add)
                    ins.then_inc(used, 1)
                    dve.wait_ge(used, m + 1)


def epi_scale_store(scale):
    def epi(e):
        def act(eng, m, j, i, ch):
            pass

        def dve(eng, m, j, i, ch):
            o = sview(e.out[j][:, :], e.n)
            if scale is None:
                ins = eng.tensor_copy(o, pview(e.ps[j], e.n))
            else:
                ins = eng.tensor_tensor(o, pview(e.ps[j], e.n), sview(scale[:, :], e.n), ALU.mult)
            ch.do(ins)
            eng.sem_inc(e.psum_free, 1)
            eng.sem_inc(e.out_ready, 1)
        return act, dve
    return epi, (0, 1)


def epi_gate(add):
    def epi(e):
        gate = [e.ph.sb(f"gate{j}", (P, e.n)) for j in range(2)]
        gate_ready = e.ph.sem("gate_ready")

        def act(eng, m, j, i, ch):
            eng.wait_ge(e.side_landed[0][j], 16 * (i + 1))
            eng.activation(gate[j][:, :], e.side[0][j][:, :], ACT.Sigmoid).then_inc(gate_ready, 1)

        def dve(eng, m, j, i, ch):
            eng.wait_ge(gate_ready, m + 1)
            ch.do(eng.tensor_tensor(sview(e.out[j][:, :], e.n), pview(e.ps[j], e.n),
                                    sview(gate[j][:, :], e.n), ALU.mult))
            eng.sem_inc(e.psum_free, 1)
            if add is None:
                eng.sem_inc(e.out_ready, 1)
                return
            eng.wait_ge(e.side_landed[1][j], 16 * (i + 1))
            ch.do(eng.tensor_tensor(e.out[j][:, :], e.out[j][:, :], e.side[1][j][:, :], ALU.add))
            ch.do(split(eng, ch, add[0][:, m, :], add[1][:, m, :], e.out[j][:, :]))
            eng.sem_inc(e.out_ready, 1)
        return act, dve
    return epi, ((0, 1) if add is None else (0, 4))


def epi_glu(x):
    def epi(e):
        gate = [e.ph.sb(f"gate{j}", (P, e.n)) for j in range(2)]
        gate_ready = e.ph.sem("gate_ready")

        def act(eng, m, j, i, ch):
            eng.activation(sview(gate[j][:, :], e.n), pview(e.ps[j], e.n), ACT.Sigmoid).then_inc(gate_ready, 1)

        def dve(eng, m, j, i, ch):
            eng.wait_ge(gate_ready, m + 1)
            eng.sem_inc(e.psum_free, 1)
            eng.wait_ge(e.side_landed[0][j], 16 * (i + 1))
            ch.do(eng.tensor_tensor(gate[j][:, :], e.side[0][j][:, :], gate[j][:, :], ALU.mult))
            ch.do(split(eng, ch, x[0][:, m, :], x[1][:, m, :], gate[j][:, :]))
            eng.sem_inc(e.out_ready, 1)
        return act, dve
    return epi, (0, 3)


def epi_residual_norm(x, g, acc):
    def epi(e):
        sq = [e.ph.sb(f"sq{j}", (P, e.n)) for j in range(2)]
        v = e.ph.sb("v", (P, e.n))
        sum_ready, squared = e.ph.sem("sum_ready"), e.ph.sem("squared")

        def act(eng, m, j, i, ch):
            eng.wait_ge(sum_ready, m + 1)
            eng.activation(sq[j][:, :], e.out[j][:, :], ACT.Square).then_inc(squared, 1)

        def dve(eng, m, j, i, ch):
            eng.wait_ge(e.side_landed[0][j], 16 * (i + 1))
            ch.do(eng.tensor_tensor(sview(e.out[j][:, :], e.n), pview(e.ps[j], e.n),
                                    sview(e.side[0][j][:, :], e.n), ALU.add))
            eng.sem_inc(e.psum_free, 1)
            eng.sem_inc(sum_ready, 1)
            if x is not None:
                ch.do(eng.tensor_scalar(v[:, :], e.out[j][:, :], g[:, bass.ds(m, 1)], None, ALU.mult))
                ch.do(split(eng, ch, x[0][:, m, :], x[1][:, m, :], v[:, :]))
            eng.wait_ge(squared, m + 1)
            if isinstance(m, int) and m == 0:
                ch.do(eng.tensor_copy(acc[:, :], sq[j][:, :]))
            else:
                ch.do(eng.tensor_tensor(acc[:, :], acc[:, :], sq[j][:, :], ALU.add))
            eng.sem_inc(e.out_ready, 1)
        return act, dve
    return epi, (0, 5 if x is not None else 2)


class Order:

    def __init__(self, *names):
        self.names = names

    def at(self, i, name):
        return i * len(self.names) + self.names.index(name) + 1


def hgrn(nc, c, pin, x):
    CP = NC - 1
    MID = CH // 2 - 1
    VE = Order("decay", "key", "cum", "centred", "g_a", "g_b", "q_in", "k_in", "k_out", "masked", "mask_tail",
               "inverse", "scaled", "gated", "high", "low")
    AC = Order("sigmoid", "log", "grow", "shrink", "g", "v_rows", "k_rows", "raw", "square", "root", "silu")
    PE = Order("v_turned", "scores", "k_turned", "out", "norm")
    with Phase(nc, "hgrn") as ph:
        def w(name, n=T1):
            return ph.sb(name, (P, n))
        q, f, v, og = w("q"), w("f"), w("v"), w("og")
        s, fp, k, cum, sums, so = w("s"), w("fp"), w("k"), w("cum"), w("sums"), w("so")
        e1, e2, qi, ki, ko = w("e1"), w("e2"), w("qi"), w("ki"), w("ko")
        gx, gg = w("gx", NC), w("gg", NC)
        vt = ph.sb("vt", (P, 9, P))
        kt = ph.sb("kt", (P, 8, 4, P))
        st = ph.sb("st", (P, 9, P))
        S = ph.sb("S", (P, NC, P))
        pa = ph.ps("turned_and_kv", (P, 4, 512))
        po = ph.ps("scores_and_out", (P, 1536))
        sum3, k3 = (a[:, :].rearrange("p (c t) -> p c t", t=CH) for a in (sums, ki))
        ko3 = ko[:, :].rearrange("p (c t) -> p c t", t=CH)
        landed = {n: ph.sem(f"{n}_landed") for n in "qfvo"}
        ve, ac, pe_s = ph.sem("vector_step"), ph.sem("scalar_step"), ph.sem("tensor_step")
        kv_full, kv_used, zeroed = ph.sem("kv_full"), ph.sem("kv_used"), ph.sem("zeroed")
        scores_seen = ph.sem("scores_seen")
        with nc.Block() as block:
            @block.sync
            def _(sp):
                def load(n, buf, sec, h):
                    sp.dma_start(buf[:, :], pin[h + sec * DT]).then_inc(landed[n], 16)

                def all_four(h):
                    load("f", f, 2, h)
                    load("q", q, 1, h)
                    load("v", v, 3, h)
                    load("o", og, 4, h)
                all_four(0)
                with sp.Fori(0, HH - 1) as h:
                    sp.wait_ge(ac, AC.at(h, "sigmoid"))
                    load("f", f, 2, h + 1)
                    sp.wait_ge(ve, VE.at(h, "q_in"))
                    load("q", q, 1, h + 1)
                    sp.wait_ge(pe_s, PE.at(h, "v_turned"))
                    load("v", v, 3, h + 1)
                    sp.wait_ge(ac, AC.at(h, "silu"))
                    load("o", og, 4, h + 1)

            @block.scalar
            def _(act):
                with act.Fori(0, HH) as h:
                    act.wait_ge(landed["f"], 16 * (h + 1))
                    act.activation(s[:, :], f[:, :], ACT.Sigmoid).then_inc(ac, 1)
                    act.wait_ge(ve, VE.at(h, "decay"))
                    act.activation(cum[:, :], fp[:, :], ACT.Ln).then_inc(ac, 1)
                    act.wait_ge(ve, VE.at(h, "g_b"))
                    act.activation(e1[:, :], fp[:, :], ACT.Exp).then_inc(ac, 1)
                    act.activation(e2[:, :], fp[:, :], ACT.Exp, scale=-1.0).then_inc(ac, 1)
                    act.activation(gg[:, 0:CP], gx[:, 0:CP], ACT.Exp).then_inc(ac, 1)
                    act.wait_ge(pe_s, PE.at(h, "v_turned"))
                    flat = pa[:, :, :].rearrange("p b x -> p (b x)")
                    act.activation(vt[:, 0:8, :].rearrange("p b x -> p (b x)"), flat[:, 0:1024], ACT.Copy)
                    act.activation(vt[0:CH, 8, :], flat[0:CH, 1024:1152], ACT.Copy).then_inc(ac, 1)
                    act.wait_ge(pe_s, PE.at(h, "k_turned"))
                    for u in range(4):
                        r = CH * u
                        ins = act.activation(kt[r:r + CH, :, u, :],
                                             flat[r:r + CH, 0:1024].rearrange("p (b x) -> p b x", x=P), ACT.Copy)
                    ins.then_inc(ac, 1)
                    act.wait_ge(pe_s, PE.at(h, "out"))
                    act.activation(e1[:, :], po[:, 0:T1], ACT.Copy).then_inc(ac, 1)
                    act.activation(e2[:, :], po[:, 0:T1], ACT.Square).then_inc(ac, 1)
                    act.wait_ge(pe_s, PE.at(h, "norm"))
                    act.activation(sview(k[:, :], T1), pview(flat[:, 0:1536], T1), ACT.Sqrt, bias=c["eps"][:, 0:1],
                                   scale=1.0 / P).then_inc(ac, 1)
                    act.wait_ge(landed["o"], 16 * (h + 1))
                    act.activation(so[:, :], og[:, :], ACT.Silu).then_inc(ac, 1)

            @block.tensor
            def _(pe):
                flat = pa[:, :, :].rearrange("p b x -> p (b x)")
                with pe.Fori(0, HH) as h:
                    pe.wait_ge(landed["v"], 16 * (h + 1))
                    pe.wait_ge(ac, AC.at(h, "sigmoid"))
                    for b in range(9):
                        n = min(P, T1 - b * P)
                        mm = pe.transpose(flat[0:n, b * P:(b + 1) * P], v[:, b * P:b * P + n], c["ident"][:, :])
                    mm.then_inc(pe_s, 1)
                    pe.wait_ge(ve, VE.at(h, "k_in"))
                    for b in range(9):
                        n = min(P, T1 - b * P)
                        mm = pe.matmul(po[0:n, b * P:b * P + n], ki[:, b * P:b * P + n], qi[:, b * P:b * P + n],
                                       start=True, stop=True)
                    mm.then_inc(pe_s, 1)
                    pe.wait_ge(ve, VE.at(h, "k_out"))
                    pe.wait_ge(ac, AC.at(h, "v_rows"))
                    for b in range(8):
                        mm = pe.transpose(flat[:, b * P:(b + 1) * P], ko[:, b * P:(b + 1) * P], c["ident"][:, :])
                    mm.then_inc(pe_s, 1)
                    pe.wait_ge(ac, AC.at(h, "k_rows"))
                    for i in range(CP // 4):
                        if i >= 4:
                            pe.wait_ge(kv_used, h * CP + 4 * (i - 3))
                        for u in range(4):
                            mm = pe.matmul(pa[:, i % 4, P * u:P * (u + 1)], kt[:, i, u, :], vt[:, i, :],
                                           start=True, stop=True)
                        mm.then_inc(kv_full, 1)
                    pe.wait_ge(ve, VE.at(h, "mask_tail"))
                    for i in range(NC):
                        b, u = divmod(i, 4)
                        n = min(P, T1 - b * P)
                        if u == 0:
                            mm = pe.matmul(po[:, b * P:b * P + n], vt[0:n, b, :], st[0:n, b, 0:n],
                                           start=True, stop=True, skip_group_check=True)
                        if i == 0:
                            continue
                        pe.wait_ge(kv_used, h * CP + i)
                        mm = pe.matmul(po[:, CH * i:CH * (i + 1)], S[:, i, :], qi[:, CH * i:CH * (i + 1)],
                                       start=False, stop=True, skip_group_check=True)
                    mm.then_inc(pe_s, 1)
                    pe.wait_ge(ac, AC.at(h, "square"))
                    for b, c0, n in pieces(T1):
                        mm = pe.matmul(flat[:, 512 * b:512 * b + n], c["ones"][:, :], e2[:, c0:c0 + n],
                                       start=True, stop=True)
                    mm.then_inc(pe_s, 1)

            @block.vector
            def _(dve):
                dve.memset(S[:, 0, :], 0.0).then_inc(zeroed, 1)
                dve.memset(st[:, :, :], 0.0).then_inc(zeroed, 1)
                dve.memset(kt[:, :, :, :], 0.0).then_inc(zeroed, 1)
                dve.wait_ge(zeroed, 3)
                with dve.Fori(0, HH) as h:
                    ch = Chain(dve, ve, h * len(VE.names))
                    dve.wait_ge(ac, AC.at(h, "sigmoid"))
                    ch.do(dve.tensor_scalar(fp[:, :], s[:, :], c["one_minus_lb"][:, bass.ds(h, 1)],
                                            c["lb"][:, bass.ds(h, 1)], ALU.mult, ALU.add))
                    ch.inc(dve.tensor_scalar(k[:, :], fp[:, :], -1.0, 1.0, ALU.mult, ALU.add))
                    dve.wait_ge(ac, AC.at(h, "log"))
                    ch.do(dve.tensor_tensor_scan(sums[:, :], c["chunk_mask"][:, :], cum[:, :], 0.0,
                                                 ALU.mult, ALU.add))
                    ch.inc(dve.tensor_tensor(fp[:, :].rearrange("p (c t) -> p c t", t=CH), sum3,
                                             sum3[:, :, MID:MID + 1].broadcast_to([P, NC, CH]), ALU.subtract))
                    ch.do(dve.tensor_tensor(gx[:, 0:CP], sum3[:, 0:CP, CH - 1], sum3[:, 0:CP, MID], ALU.subtract))
                    ch.do(dve.tensor_tensor(gx[:, 0:CP], gx[:, 0:CP], sum3[:, 1:NC, MID], ALU.add))
                    dve.wait_ge(landed["q"], 16 * (h + 1))
                    dve.wait_ge(ac, AC.at(h, "g"))
                    ch.inc(dve.tensor_tensor(qi[:, :], q[:, :], e1[:, :], ALU.mult))
                    ch.do(dve.tensor_tensor(ki[:, :], k[:, :], e2[:, :], ALU.mult))
                    ch.do(dve.tensor_tensor(ko3[:, 0:CP, :], k3[:, 0:CP, :],
                                            gg[:, 0:CP].unsqueeze(2).broadcast_to([P, CP, CH]), ALU.mult))
                    dve.wait_ge(pe_s, PE.at(h, "scores"))
                    dve.sem_inc(scores_seen, 1)
                    ch.inc(dve.copy_predicated(st[:, 0:8, :], c["causal"][:, 0:8, :].bitcast(mybir.dt.int32),
                                               po[:, 0:1024].rearrange("p (b t) -> p b t", t=P)))
                    ch.do(dve.copy_predicated(st[0:CH, 8, 0:CH], c["causal"][0:CH, 8, 0:CH].bitcast(mybir.dt.int32), po[0:CH, 1024:T1]))
                    for i in range(CP):
                        if i % 4 == 0:
                            dve.wait_ge(kv_full, h * (CP // 4) + i // 4 + 1)
                        dve.scalar_tensor_tensor(
                            out=S[:, i + 1, :], in0=S[:, i, :], scalar=gg[:, i:i + 1],
                            in1=pa[:, i // 4 % 4, P * (i % 4):P * (i % 4 + 1)],
                            op0=ALU.mult, op1=ALU.add).then_inc(kv_used, 1)
                        dve.wait_ge(kv_used, h * CP + i + 1)
                    dve.wait_ge(ac, AC.at(h, "root"))
                    ch.do(dve.reciprocal(cum[:, :], k[:, :]))
                    ch.do(dve.scalar_tensor_tensor(out=cum[:, :], in0=e1[:, :], scalar=c["hgrn_g"][:, 0:1],
                                                   in1=cum[:, :], op0=ALU.mult, op1=ALU.mult))
                    dve.wait_ge(ac, AC.at(h, "silu"))
                    ch.do(dve.tensor_tensor(cum[:, :], cum[:, :], so[:, :], ALU.mult))
                    ch.do(split(dve, ch, x[0][:, h, :], x[1][:, h, :], cum[:, :]))


def reorder_u(nc, pin, up):
    with Phase(nc, "reorder") as ph:
        a = [ph.sb(f"a{j}", (P, T1)) for j in range(2)]
        b = [ph.sb(f"b{j}", (P, T1)) for j in range(2)]
        landed = [ph.sem(f"landed{j}") for j in range(2)]
        stored = [ph.sem(f"stored{j}") for j in range(2)]
        moved = ph.sem("moved")
        with nc.Block() as block:
            @block.sync
            def _(sp):
                for m in range(DT):
                    if m >= 2:
                        sp.wait_ge(moved, m - 1)
                    sp.dma_start(a[m % 2][:, :], pin[m]).then_inc(landed[m % 2], 16)
                    if m >= 1:
                        sp.wait_ge(moved, m)
                        sp.dma_start(up[m - 1], b[(m - 1) % 2][:, :]).then_inc(stored[(m - 1) % 2], 16)
                sp.wait_ge(moved, DT)
                sp.dma_start(up[DT - 1], b[(DT - 1) % 2][:, :]).then_inc(stored[(DT - 1) % 2], 16)
                for j in range(2):
                    sp.wait_ge(stored[j], 16 * DT // 2)

            @block.vector
            def _(dve):
                for m in range(DT):
                    dve.wait_ge(landed[m % 2], 16 * (m // 2 + 1))
                    if m >= 2:
                        dve.wait_ge(stored[m % 2], 16 * (m // 2))
                    dve.tensor_copy(b[m % 2][:, :].rearrange("p (t c) -> p c t", t=TAU),
                                    a[m % 2][:, :].rearrange("p (c t) -> p c t", t=TAU)).then_inc(moved, 1)


def split_y(nc, yc, yt, x):
    with Phase(nc, "split_y") as ph:
        a = [ph.sb(f"a{j}", (P, T1)) for j in range(2)]
        b = [ph.sb(f"b{j}", (P, T1)) for j in range(2)]
        landed = [ph.sem(f"landed{j}") for j in range(2)]
        stored = [ph.sem(f"stored{j}") for j in range(2)]
        moved, moved_high, step = ph.sem("moved"), ph.sem("moved_high"), ph.sem("step")
        with nc.Block() as block:
            @block.sync
            def _(sp):
                for m in range(DT):
                    if m >= 2:
                        sp.wait_ge(moved, m - 1)
                    sp.dma_start(a[m % 2][:, :], yc[m]).then_inc(landed[m % 2], 16)
                    if m >= 1:
                        sp.wait_ge(moved, m)
                        sp.dma_start(yt[m - 1], b[(m - 1) % 2][:, :]).then_inc(stored[(m - 1) % 2], 16)
                sp.wait_ge(moved, DT)
                sp.dma_start(yt[DT - 1], b[(DT - 1) % 2][:, :]).then_inc(stored[(DT - 1) % 2], 16)
                for j in range(2):
                    sp.wait_ge(stored[j], 16 * DT // 2)

            @block.scalar
            def _(act):
                for m in range(DT):
                    act.wait_ge(landed[m % 2], 16 * (m // 2 + 1))
                    if m >= 2:
                        act.wait_ge(stored[m % 2], 16 * (m // 2))
                        act.wait_ge(step, m - 1)
                    act.activation(b[m % 2][:, :].rearrange("p (c t) -> p c t", t=TAU),
                                   a[m % 2][:, :].rearrange("p (t c) -> p c t", t=TAU), ACT.Copy).then_inc(moved, 1)
                    act.wait_ge(moved, m + 1)
                    act.activation(x[0][:, m, :], b[m % 2][:, :], ACT.Copy).then_inc(moved_high, 1)

            @block.vector
            def _(dve):
                for m in range(DT):
                    dve.wait_ge(moved_high, m + 1)
                    dve.tensor_tensor(x[1][:, m, :], b[m % 2][:, :], x[0][:, m, :].bitcast(F32),
                                      ALU.subtract).then_inc(step, 1)


def s5(nc, c, t, up, yc):
    NP, NQ = NPAIR, 8
    with Phase(nc, "s5") as outer:
        ca = [outer.sb(n, (P, NP, TAU + 1, SG)) for n in ("ca_re", "ca_im")]
        win = outer.sb("win", (P, 2, NP, P))
        toep = outer.sb("toeplitz", (P, 2, NP, P))
        m8 = outer.sb("m8", (P, NP))
        rot = outer.sb("rot", (P, 2, NP))
        with Phase(nc, "s5w") as ph:
            def small(n, k=1):
                return ph.sb(n, (P, NP * k))
            lr, li, dt = small("lr"), small("li"), small("dt")
            br, bi, cr, ci = (ph.sb(n, (P, NP, SG)) for n in ("br", "bi", "cr", "ci"))
            th, kk, r, ab, co, si, mag = (small(n) for n in ("th", "kk", "r", "ab", "co", "si", "mag"))
            x1, x2, x3, x4 = (small(n) for n in ("x1", "x2", "x3", "x4"))
            pw = ph.sb("powers", (P, 2, TAU + 1, NP))
            bb = [ph.sb(n, (P, NP, 3 * SG)) for n in ("bb_re", "bb_im")]
            wt = [ph.sb(n, (P, NP, TAU, SG)) for n in ("w_re", "w_im")]
            t1, t2 = (ph.sb(n, (P, NP, TAU + 1, SG)) for n in ("t1", "t2"))
            pst = ph.ps("turn", (P, 4, 512))
            psk = ph.ps("kernel", (P, 4, 512))
            landed, step, sc = ph.sem("landed"), ph.sem("vector_step"), ph.sem("scalar_step")
            zeroed, w_ready, ker_ready = ph.sem("zeroed"), ph.sem("w_ready"), ph.sem("kernel_ready")
            turned, turned_out = ph.sem("turned"), ph.sem("turned_out")
            made, made_out = ph.sem("made"), ph.sem("made_out")
            loads = ((lr, "lam_re"), (li, "lam_im"), (dt, "log_dt"), (br, "b_re"), (bi, "b_im"), (cr, "c_re"),
                     (ci, "c_im"))
            with nc.Block() as block:
                @block.sync
                def _(sp):
                    for buf, n in loads:
                        sp.dma_start(buf[:], t[n]).then_inc(landed, 16)

                @block.scalar
                def _(act):
                    act.wait_ge(landed, 16 * len(loads))
                    act.activation(dt[:, :], dt[:, :], ACT.Exp).then_inc(sc, 1)
                    act.wait_ge(step, 2)
                    act.activation(mag[:, :], x1[:, :], ACT.Exp).then_inc(sc, 1)
                    act.wait_ge(step, 11)
                    act.activation(si[:, :], r[:, :], ACT.Sin).then_inc(sc, 1)
                    act.activation(co[:, :], ab[:, :], ACT.Sin).then_inc(sc, 1)
                    act.wait_ge(w_ready, 1)
                    for n in range(16):
                        act.wait_ge(turned, n + 1)
                        part, q = divmod(n, 8)
                        act.activation(win[:, part, 4 * q:4 * q + 4, :].rearrange("p a b -> p (a b)"),
                                       pst[:, n % 4, :], ACT.Copy).then_inc(turned_out, 1)

                @block.vector
                def _(dve):
                    ch = Chain(dve, step)
                    tt, ts = dve.tensor_tensor, dve.tensor_scalar
                    dve.memset(toep[:, :, :, :], 0.0).then_inc(zeroed, 1)
                    for b in bb:
                        dve.memset(b[:, :, :], 0.0).then_inc(zeroed, 1)
                    dve.wait_ge(zeroed, 3)
                    dve.wait_ge(sc, 1)
                    ch.do(tt(th[:, :], li[:, :], dt[:, :], ALU.mult))
                    ch.do(tt(x1[:, :], lr[:, :], dt[:, :], ALU.mult))
                    big = 1.5 * 2.0 ** 23
                    ch.do(ts(kk[:, :], th[:, :], float(1 / (2 * np.pi)), big, ALU.mult, ALU.add))
                    ch.do(ts(kk[:, :], kk[:, :], big, None, ALU.subtract))
                    src = th
                    for part in (6.28125, 0.0019350051879882812, 3.019915981956752e-07):
                        ch.do(dve.scalar_tensor_tensor(out=r[:, :], in0=kk[:, :], scalar=-part, in1=src[:, :],
                                                       op0=ALU.mult, op1=ALU.add))
                        src = r
                    ch.do(ts(r[:, :], r[:, :], 3.1415925, -3.1415925, ALU.min, ALU.max))
                    ch.do(ts(ab[:, :], r[:, :], -1.0, None, ALU.mult))
                    ch.do(tt(ab[:, :], r[:, :], ab[:, :], ALU.max))
                    ch.do(ts(ab[:, :], ab[:, :], -1.0, float(np.pi / 2), ALU.mult, ALU.add))
                    assert ch.n == 11
                    dve.wait_ge(sc, 4)
                    ch.inc(dve.memset(pw[:, 0, 0, :], 1.0))
                    ch.inc(dve.memset(pw[:, 1, 0, :], 0.0))
                    ch.inc(tt(pw[:, 0, 1, :], mag[:, :], co[:, :], ALU.mult))
                    ch.do(tt(pw[:, 1, 1, :], mag[:, :], si[:, :], ALU.mult))

                    def cmul(ore, oim, are, aim, bre, bim, u, v):
                        ch.inc(tt(u, are, bre, ALU.mult))
                        ch.do(tt(v, aim, bim, ALU.mult))
                        ch.do(tt(ore, u, v, ALU.subtract))
                        ch.inc(tt(u, are, bim, ALU.mult))
                        ch.do(tt(v, aim, bre, ALU.mult))
                        ch.do(tt(oim, u, v, ALU.add))

                    a1, b1 = pw[:, 0, 1, :], pw[:, 1, 1, :]
                    for j in range(2, TAU + 1):
                        cmul(pw[:, 0, j, :], pw[:, 1, j, :], pw[:, 0, j - 1, :], pw[:, 1, j - 1, :], a1, b1,
                             x1[:, :], x2[:, :])
                    cmul(rot[:, 0, :], rot[:, 1, :], co[:, :], si[:, :], co[:, :], si[:, :], x1[:, :], x2[:, :])
                    ch.do(tt(m8[:, :], mag[:, :], mag[:, :], ALU.mult))
                    for _ in range(2):
                        cmul(x3[:, :], x4[:, :], rot[:, 0, :], rot[:, 1, :], rot[:, 0, :], rot[:, 1, :],
                             x1[:, :], x2[:, :])
                        ch.inc(dve.tensor_copy(rot[:, 0, :], x3[:, :]))
                        ch.inc(dve.tensor_copy(rot[:, 1, :], x4[:, :]))
                        ch.do(tt(m8[:, :], m8[:, :], m8[:, :], ALU.mult))
                    ch.inc(tt(x1[:, :], lr[:, :], lr[:, :], ALU.mult))
                    ch.do(tt(x2[:, :], li[:, :], li[:, :], ALU.mult))
                    ch.do(tt(x1[:, :], x1[:, :], x2[:, :], ALU.add))
                    ch.do(dve.reciprocal(r[:, :], x1[:, :]))
                    ch.inc(ts(kk[:, :], a1, -1.0, None, ALU.add))
                    ch.do(tt(x2[:, :], b1, li[:, :], ALU.mult))
                    ch.do(tt(x1[:, :], kk[:, :], lr[:, :], ALU.mult))
                    ch.do(tt(x1[:, :], x1[:, :], x2[:, :], ALU.add))
                    ch.do(tt(x3[:, :], x1[:, :], r[:, :], ALU.mult))
                    ch.inc(tt(x1[:, :], b1, lr[:, :], ALU.mult))
                    ch.do(tt(x2[:, :], kk[:, :], li[:, :], ALU.mult))
                    ch.do(tt(x1[:, :], x1[:, :], x2[:, :], ALU.subtract))
                    ch.do(tt(x4[:, :], x1[:, :], r[:, :], ALU.mult))
                    wide = lambda v, n: v.unsqueeze(2).broadcast_to([P, NP, n])
                    bre, bim = (b[:, :, SG:2 * SG] for b in bb)
                    cmul(bre, bim, wide(x3[:, :], SG), wide(x4[:, :], SG), br[:, :, :], bi[:, :, :],
                         t1[:, :, 0, :], t2[:, :, 0, :])
                    for k in range(TAU):
                        cmul(wt[0][:, :, k, :], wt[1][:, :, k, :], wide(pw[:, 0, TAU - 1 - k, :], SG),
                             wide(pw[:, 1, TAU - 1 - k, :], SG), bre, bim, t1[:, :, 0, :], t2[:, :, 0, :])
                    dve.sem_inc(w_ready, 1)
                    for k in range(TAU + 1):
                        cmul(ca[0][:, :, k, :], t1[:, :, 1, :], wide(pw[:, 0, k, :], SG), wide(pw[:, 1, k, :], SG),
                             cr[:, :, :], ci[:, :, :], t1[:, :, 0, :], t2[:, :, 0, :])
                        ch.do(ts(ca[1][:, :, k, :], t1[:, :, 1, :], -1.0, None, ALU.mult))
                    dve.sem_inc(ker_ready, 1)
                    for n in range(16):
                        par, q = divmod(n, 8)
                        dve.wait_ge(made, n + 1)
                        for j in range(4):
                            w = P - 32 * j
                            ins = dve.tensor_copy(
                                toep[32 * j:32 * j + 32, par, 4 * q:4 * q + 4, 32 * j:P],
                                psk[0:32, n % 4, :].rearrange("p (a b) -> p a b", b=P)[:, :, 0:w])
                        ins.then_inc(made_out, 1)
                        dve.wait_ge(made_out, n + 1)

                @block.tensor
                def _(pe):
                    pe.wait_ge(w_ready, 1)
                    for n in range(16):
                        part, q = divmod(n, 8)
                        if n >= 4:
                            pe.wait_ge(turned_out, n - 3)
                        for u in range(4):
                            mm = pe.transpose(pst[:, n % 4, P * u:P * u + P],
                                              wt[part][:, 4 * q + u, :, :].rearrange("p a b -> p (a b)"),
                                              c["ident"][:, :])
                        mm.then_inc(turned, 1)
                    pe.wait_ge(ker_ready, 1)
                    for n in range(16):
                        par, q = divmod(n, 8)
                        r0 = SS * par
                        if n >= 4:
                            pe.wait_ge(made_out, n - 3)
                        for u in range(4):
                            pair = 4 * q + u
                            for part in range(2):
                                b = bb[part][r0:r0 + SS, pair, :]
                                a = ca[part][r0:r0 + SS, pair, :, :].rearrange("p a b -> p (a b)")
                                o = psk[0:32, n % 4, P * u:P * u + P]
                                pe.matmul(o, b[:, SG:3 * SG], a[:, 0:P], start=part == 0, stop=False,
                                          skip_group_check=True)
                                mm = pe.matmul(o[:, SG:P], b[:, 0:2 * SG], a[:, 0:P - SG], start=False,
                                               stop=part == 1, skip_group_check=True)
                        mm.then_inc(made, 1)
        with Phase(nc, "s5m") as ph:
            U = ph.sb("u", (P, G, NCH))
            dcol = ph.sb("d", (P, G))
            wr, wi, er, ei, xr, xi, t1, t2, sr, si, dec = (
                ph.sb(n, (P, NQ, NCH)) for n in ("wr", "wi", "er", "ei", "xr", "xi", "t1", "t2", "sr", "si", "dec"))
            yv = ph.sb("yv", (P, 2, NQ, NCH))
            psv = ph.ps("v", (P, 4, 512))
            psy = ph.ps("y", (P, 4, 512))
            landed, step, zeroed = ph.sem("landed"), ph.sem("vector_step"), ph.sem("zeroed")
            v_full, v_used, states = ph.sem("v_full"), ph.sem("v_used"), ph.sem("states")
            y_full, y_used, gelu, stored = ph.sem("y_full"), ph.sem("y_used"), ph.sem("gelu"), ph.sem("stored")
            trips = ((0, 3), (3, 6), (6, 8))
            rows = yc.rearrange("m p x -> (m p) x").rearrange("(g h) (t c) -> t h g c", h=SG, t=TAU)
            urow = up.rearrange("m p x -> (m p) x").rearrange("(g h) (t c) -> t h g c", h=SG, t=TAU)
            with nc.Block() as block:
                @block.sync
                def _(sp):
                    sp.dma_start(dcol[:, :], t["ssm_d"]).then_inc(landed, 16)
                    for k in range(TAU):
                        sp.dma_start(U[SG * k:SG * k + SG, :, :], urow[k]).then_inc(landed, 16)
                    for n in range(4):
                        sp.wait_ge(gelu, n + 1)
                        for k in range(TAU):
                            for par in range(2):
                                dst = rows[k][:, 2 * NQ * n + par:2 * NQ * (n + 1):2, :]
                                sp.dma_start(dst, yv[SG * k:SG * k + SG, par, :, :]).then_inc(stored, 16)
                        sp.wait_ge(stored, 16 * 16 * (n + 1))

                @block.tensor
                def _(pe):
                    pe.wait_ge(landed, 16 * 9)
                    f = 0
                    g = 0
                    for n in range(4):
                        for a, b in trips:
                            if f >= 2:
                                pe.wait_ge(v_used, f - 1)
                            for pair in range(a, b):
                                pp = NQ * n + pair
                                for part in range(2):
                                    for par in range(2):
                                        o = psv[SS * par:SS * par + SS, 2 * (f % 2) + part,
                                                NCH * (pair - a):NCH * (pair - a + 1)]
                                        mm = pe.matmul(o, win[:, part, pp, SS * par:SS * par + SS],
                                                       U[:, 2 * pp + par, :], start=True, stop=True)
                            mm.then_inc(v_full, 1)
                            f += 1
                        pe.wait_ge(states, n + 1)
                        for par in range(2):
                            r0 = SS * par
                            for a, b in trips:
                                if g >= 4:
                                    pe.wait_ge(y_used, g - 3)
                                for pair in range(a, b):
                                    pp = NQ * n + pair
                                    o = psy[:, g % 4, NCH * (pair - a):NCH * (pair - a + 1)]
                                    pe.matmul(o, toep[:, par, pp, :], U[:, 2 * pp + par, :], start=True, stop=False)
                                    for part, s in ((0, sr), (1, si)):
                                        w = ca[part][r0:r0 + SS, pp, :, :].rearrange("p a b -> p (a b)")
                                        mm = pe.matmul(o, w[:, SG:], s[r0:r0 + SS, pair, :], start=False,
                                                       stop=part == 1)
                                mm.then_inc(y_full, 1)
                                g += 1

                @block.scalar
                def _(act):
                    for n in range(4):
                        act.wait_ge(y_used, 6 * (n + 1))
                        act.activation(yv[:, :, :, :], yv[:, :, :, :], ACT.Gelu_apprx_tanh).then_inc(gelu, 1)

                @block.vector
                def _(dve):
                    ch = Chain(dve, step)
                    tt = dve.tensor_tensor
                    dve.memset(sr[:, :, 0:1], 0.0).then_inc(zeroed, 1)
                    dve.memset(si[:, :, 0:1], 0.0).then_inc(zeroed, 1)
                    dve.wait_ge(zeroed, 2)
                    f = 0
                    g = 0
                    dve.wait_ge(landed, 16 * 9)
                    for n in range(4):
                        lo, hi = NQ * n, NQ * (n + 1)
                        ch.inc(dve.memset(wr[:, :, 0:1], 1.0))
                        ch.inc(dve.memset(wi[:, :, 0:1], 0.0))
                        ch.inc(dve.tensor_copy(wr[:, :, 1:2], rot[:, 0, lo:hi].unsqueeze(2)))
                        ch.inc(dve.tensor_copy(wi[:, :, 1:2], rot[:, 1, lo:hi].unsqueeze(2)))
                        ch.do(dve.tensor_copy(dec[:, :, :], m8[:, lo:hi].unsqueeze(2).broadcast_to([P, NQ, NCH])))
                        ch.do(dve.memset(dec[:, :, 0:1], 0.0))
                        k = 1
                        while k < NCH - 1:
                            m = min(k, NCH - 1 - k)
                            s = slice(1, m + 1)
                            d = slice(k + 1, k + 1 + m)
                            wk = [w[:, :, k:k + 1].broadcast_to([P, NQ, m]) for w in (wr, wi)]
                            u, v = t1[:, :, 0:m], t2[:, :, 0:m]
                            ch.inc(tt(u, wr[:, :, s], wk[0], ALU.mult))
                            ch.do(tt(v, wi[:, :, s], wk[1], ALU.mult))
                            ch.do(tt(wr[:, :, d], u, v, ALU.subtract))
                            ch.inc(tt(u, wr[:, :, s], wk[1], ALU.mult))
                            ch.do(tt(v, wi[:, :, s], wk[0], ALU.mult))
                            ch.do(tt(wi[:, :, d], u, v, ALU.add))
                            k *= 2
                        for a, b in trips:
                            dve.wait_ge(v_full, f + 1)
                            vr, vi = (psv[:, 2 * (f % 2) + part, 0:NCH * (b - a)].rearrange(
                                "p (a c) -> p a c", c=NCH) for part in range(2))
                            s = slice(a, b)
                            ch.inc(tt(t1[:, s, :], vr, wr[:, s, :], ALU.mult))
                            ch.inc(tt(t2[:, s, :], vi, wi[:, s, :], ALU.mult))
                            ch.inc(tt(xr[:, s, :], vi, wr[:, s, :], ALU.mult))
                            ch.do(tt(xi[:, s, :], vr, wi[:, s, :], ALU.mult))
                            dve.sem_inc(v_used, 1)
                            ch.inc(tt(er[:, s, :], t1[:, s, :], t2[:, s, :], ALU.add))
                            ch.do(tt(ei[:, s, :], xr[:, s, :], xi[:, s, :], ALU.subtract))
                            f += 1
                        for x, e in ((xr, er), (xi, ei)):
                            ins = dve.tensor_tensor_scan(*(q[:, :, :].rearrange("p a c -> p (a c)")
                                                           for q in (x, dec, e)), 0.0, ALU.mult, ALU.add)
                            ch.do(ins)
                        w = slice(0, NCH - 1)
                        ch.inc(tt(t1[:, :, w], xr[:, :, w], wr[:, :, w], ALU.mult))
                        ch.do(tt(t2[:, :, w], xi[:, :, w], wi[:, :, w], ALU.mult))
                        ch.do(tt(sr[:, :, 1:], t1[:, :, w], t2[:, :, w], ALU.subtract))
                        ch.inc(tt(t1[:, :, w], xi[:, :, w], wr[:, :, w], ALU.mult))
                        ch.do(tt(t2[:, :, w], xr[:, :, w], wi[:, :, w], ALU.mult))
                        ch.do(tt(si[:, :, 1:], t1[:, :, w], t2[:, :, w], ALU.add))
                        dve.sem_inc(states, 1)
                        if n:
                            dve.wait_ge(stored, 16 * 16 * n)
                        for par in range(2):
                            for a, b in trips:
                                dve.wait_ge(y_full, g + 1)
                                for pair in range(a, b):
                                    gr = 2 * (lo + pair) + par
                                    ins = dve.scalar_tensor_tensor(
                                        out=yv[:, par, pair, :], in0=U[:, gr, :], scalar=dcol[:, gr:gr + 1],
                                        in1=psy[:, g % 4, NCH * (pair - a):NCH * (pair - a + 1)],
                                        op0=ALU.mult, op1=ALU.add)
                                ins.then_inc(y_used, 1)
                                g += 1


def epi_conv(rms, conv, x, off):
    def epi(e):
        raw = [e.ph.sb(f"raw{j}", (P, T1 + 2)) for j in range(2)]
        cv = [e.ph.sb(f"conv{j}", (P, T1)) for j in range(2)]
        gate = e.ph.sb("gate", (P, T1))
        conv_ready, gate_ready, zeroed = e.ph.sem("conv_ready"), e.ph.sem("gate_ready"), e.ph.sem("zeroed")

        def act(eng, m, j, i, ch):
            if j == 0:
                eng.wait_ge(conv_ready, i + 1)
                eng.activation(gate[:, :], cv[0][:, :], ACT.Silu).then_inc(gate_ready, 1)

        def dve(eng, m, j, i, ch):
            if isinstance(m, int) and m == j:
                eng.memset(raw[j][:, 0:2], 0.0).then_inc(zeroed, 1)
                eng.wait_ge(zeroed, m + 1)
            ch.do(eng.tensor_tensor(sview(raw[j][:, 2:], T1), pview(e.ps[j], T1), sview(rms[:, :], T1), ALU.mult))
            eng.sem_inc(e.psum_free, 1)
            col = lambda k: conv[:, bass.ds(m + off, 1), k]
            ch.do(eng.tensor_scalar(cv[j][:, :], raw[j][:, 2:], col(2), col(3), ALU.mult, ALU.add))
            for k in (1, 0):
                ch.do(eng.scalar_tensor_tensor(out=cv[j][:, :], in0=raw[j][:, k:k + T1], scalar=col(k),
                                               in1=cv[j][:, :], op0=ALU.mult, op1=ALU.add))
            if j == 0:
                eng.sem_inc(conv_ready, 1)
            else:
                eng.wait_ge(gate_ready, i + 1)
                ch.do(eng.tensor_tensor(cv[1][:, :], gate[:, :], cv[1][:, :], ALU.mult))
                ch.do(split(eng, ch, x[0][:, i, :], x[1][:, i, :], cv[1][:, :]))
            eng.sem_inc(e.out_ready, 1)
        return act, dve
    return epi, (0, 5.5)


def epi_residual():
    def epi(e):
        def act(eng, m, j, i, ch):
            pass

        def dve(eng, m, j, i, ch):
            eng.wait_ge(e.side_landed[0][j], 16 * (i + 1))
            ch.do(eng.tensor_tensor(sview(e.out[j][:, :], e.n), pview(e.ps[j], e.n),
                                    sview(e.side[0][j][:, :], e.n), ALU.add))
            eng.sem_inc(e.psum_free, 1)
            eng.sem_inc(e.out_ready, 1)
        return act, dve
    return epi, (0, 1)


def epi_gated_residual(mod, n):
    def epi(e):
        scaled = [e.ph.sb(f"scaled{j}", (P, n)) for j in range(2)]
        scaled_ready = e.ph.sem("scaled_ready")

        def act(eng, m, j, i, ch):
            eng.wait_ge(e.side_landed[0][j], 16 * (i + 1))
            eng.activation(scaled[j][:, :], e.side[0][j][:, :], ACT.Copy, scale=ALPHA).then_inc(scaled_ready, 1)

        def dve(eng, m, j, i, ch):
            eng.wait_ge(scaled_ready, m + 1)
            for s, (a, b) in enumerate(((0, SEQ), (SEQ, n))[:1 if n == SEQ else 2]):
                ins = eng.scalar_tensor_tensor(out=e.out[j][:, a:b], in0=e.ps[j][:, a:b],
                                               scalar=mod[:, bass.ds(m + 2 * DT, 1), s],
                                               in1=scaled[j][:, a:b], op0=ALU.mult, op1=ALU.add)
                ch.do(ins)
            eng.sem_inc(e.psum_free, 1)
            eng.sem_inc(e.out_ready, 1)
        return act, dve
    return epi, (0, 1 if n == SEQ else 2)


def modulation(nc, name, t, cond, w, bias, mod):
    MT, Q = 3 * DT, 4
    with Phase(nc, name) as ph:
        raw, sc = ph.sb("cond", (P, DT, 2)), ph.sb("silu", (P, DT, 2))
        b = ph.sb("bias", (P, MT))
        wt = [ph.sb(f"w{j}", (P, Q, DT * P)) for j in range(2)]
        ps = ph.ps("mod", (P, 512))
        landed = [ph.sem(f"landed{j}") for j in range(2)]
        small, ready, used, step = ph.sem("small"), ph.sem("ready"), ph.sem("used"), ph.sem("step")

        def stream(eng, j):
            group = w.rearrange("(i j q) p x -> i j p q x", j=2, q=Q)
            eng.dma_start(wt[j][:, :, :], group[0, j]).then_inc(landed[j], 16)
            with eng.Fori(1, MT // (2 * Q)) as i:
                eng.wait_ge(used, 2 * i + j - 1)
                eng.dma_start(wt[j][:, :, :], group[i, j]).then_inc(landed[j], 16)

        with nc.Block() as block:
            @block.sync
            def _(sp):
                sp.dma_start(raw[:, :, :], cond).then_inc(small, 16)
                sp.dma_start(b[:, :], bias).then_inc(small, 16)
                stream(sp, 0)

            @block.scalar
            def _(act):
                act.wait_ge(small, 32)
                act.activation(sc[:, :, :], raw[:, :, :], ACT.Silu).then_inc(ready, 1)
                stream(act, 1)

            @block.tensor
            def _(pe):
                pe.wait_ge(ready, 1)
                with pe.Fori(0, MT // (2 * Q)) as i:
                    for j in range(2):
                        pe.wait_ge(landed[j], 16 * (i + 1))
                        for q in range(Q):
                            for k in range(DT):
                                mm = pe.matmul(ps[:, bass.ds(4 * Q * i + 2 * (Q * j + q), 2)],
                                               wt[j][:, q, k * P:(k + 1) * P], sc[:, k, :],
                                               start=k == 0, stop=k == DT - 1)
                        mm.then_inc(used, 1)

            @block.vector
            def _(dve):
                ch = Chain(dve, step)
                dve.wait_ge(used, MT // Q)
                ch.do(dve.tensor_tensor(mod[:, :, :], ps[:, 0:2 * MT].rearrange("p (m s) -> p m s", s=2),
                                        b[:, :].unsqueeze(2).broadcast_to([P, MT, 2]), ALU.add))
                ch.do(dve.tensor_scalar(mod[:, DT:2 * DT, :], mod[:, DT:2 * DT, :], 1.0, None, ALU.add))


def modulate(dve, ch, mod, m, x, v, h, n):
    for s, (a, b) in enumerate(((0, SEQ), (SEQ, n))):
        ch.do(dve.tensor_scalar(h[:, a:b], v[:, a:b], mod[:, DT + m, s:s + 1], mod[:, m, s:s + 1],
                                ALU.mult, ALU.add))
    ch.do(split(dve, ch, x[0][:, m, :], x[1][:, m, :], h[:, :]))


def finish_first(nc, c, hd, ctx, x1, rms, mod, x):
    with Phase(nc, "finish") as ph:
        a = [ph.sb(f"a{j}", (P, T1)) for j in range(2)]
        v = [ph.sb(f"v{j}", (P, T2)) for j in range(2)]
        h = ph.sb("h", (P, T2))
        landed = [ph.sem(f"landed{j}") for j in range(2)]
        stored = [ph.sem(f"stored{j}") for j in range(2)]
        normed, used, step = ph.sem("normed"), ph.sem("used"), ph.sem("step")
        with nc.Block() as block:
            @block.sync
            def _(sp):
                def load(m):
                    j = m % 2
                    sp.dma_start(a[j][:, :], hd[m]).then_inc(landed[j], 16)
                    sp.dma_start(v[j][:, SEQ:], ctx[m]).then_inc(landed[j], 16)
                load(0)
                load(1)
                for m in range(DT):
                    sp.wait_ge(normed, m + 1)
                    sp.dma_start(x1[m], v[m % 2][:, :]).then_inc(stored[m % 2], 16)
                    if m + 2 < DT:
                        sp.wait_ge(used, m + 1)
                        sp.wait_ge(stored[m % 2], 16 * (m // 2 + 1))
                        load(m + 2)
                for j in range(2):
                    sp.wait_ge(stored[j], 16 * DT // 2)

            @block.vector
            def _(dve):
                ch = Chain(dve, step)
                for m in range(DT):
                    j = m % 2
                    dve.wait_ge(landed[j], 32 * (m // 2 + 1))
                    dve.scalar_tensor_tensor(out=v[j][:, 0:SEQ], in0=a[j][:, META:META + SEQ],
                                             scalar=c["final_g"][:, m:m + 1], in1=rms[:, META:META + SEQ],
                                             op0=ALU.mult, op1=ALU.mult).then_inc(normed, 1)
                    dve.wait_ge(normed, m + 1)
                    modulate(dve, ch, mod, m, x, v[j], h, T2)
                    dve.sem_inc(used, 1)


def layer_norm(nc, name, c, vd, n, g, b, out, mod=None, x=None):
    with Phase(nc, name) as ph:
        v = ph.sb("v", (P, DT, n))
        mean, root, h = ph.sb("mean", (P, n)), ph.sb("root", (P, n)), ph.sb("h", (P, n))
        sq = [ph.sb(f"sq{j}", (P, n)) for j in range(2)]
        ps = ph.ps("mean_sum", (P, 1536))
        pq = ph.ps("square_sum", (P, 1536))
        landed = [ph.sem(f"landed{m}") for m in range(DT)]
        summed, centred, squared, sq_used, rooted = (ph.sem(s) for s in ("summed", "centred", "squared", "sq_used",
                                                                         "rooted"))
        step, done, stored = ph.sem("step"), ph.sem("done"), ph.sem("stored")
        with nc.Block() as block:
            @block.sync
            def _(sp):
                for m in range(DT):
                    sp.dma_start(v[:, m, :], vd[m]).then_inc(landed[m], 16)
                for m in range(DT):
                    sp.wait_ge(done, m + 1)
                    sp.dma_start(out[m], v[:, m, :]).then_inc(stored, 16)
                sp.wait_ge(stored, 16 * DT)

            @block.tensor
            def _(pe):
                for m in range(DT):
                    pe.wait_ge(landed[m], 16)
                    for bk, c0, w in pieces(n):
                        mm = pe.matmul(ps[:, 512 * bk:512 * bk + w], c["ones"][:, :], v[:, m, c0:c0 + w],
                                       start=m == 0, stop=m == DT - 1)
                mm.then_inc(summed, 1)
                for m in range(DT):
                    pe.wait_ge(squared, m + 1)
                    for bk, c0, w in pieces(n):
                        mm = pe.matmul(pq[:, 512 * bk:512 * bk + w], c["ones"][:, :], sq[m % 2][:, c0:c0 + w],
                                       start=m == 0, stop=m == DT - 1)
                    mm.then_inc(sq_used, 1)

            @block.scalar
            def _(act):
                act.wait_ge(summed, 1)
                act.activation(mean[:, :], ps[:, 0:n], ACT.Copy, scale=1.0 / D).then_inc(summed, 1)
                for m in range(DT):
                    act.wait_ge(centred, m + 1)
                    if m >= 2:
                        act.wait_ge(sq_used, m - 1)
                    act.activation(sq[m % 2][:, :], v[:, m, :], ACT.Square).then_inc(squared, 1)
                act.wait_ge(sq_used, DT)
                act.activation(root[:, :], pq[:, 0:n], ACT.Sqrt, bias=c["eps"][:, 0:1],
                               scale=1.0 / D).then_inc(rooted, 1)

            @block.vector
            def _(dve):
                ch = Chain(dve, step)
                dve.wait_ge(summed, 2)
                for m in range(DT):
                    dve.wait_ge(landed[m], 16)
                    dve.tensor_tensor(v[:, m, :], v[:, m, :], mean[:, :], ALU.subtract).then_inc(centred, 1)
                dve.wait_ge(rooted, 1)
                dve.wait_ge(squared, DT)
                dve.wait_ge(centred, DT)
                ch.do(dve.reciprocal(root[:, :], root[:, :]))
                for m in range(DT):
                    ch.do(dve.scalar_tensor_tensor(out=v[:, m, :], in0=v[:, m, :], scalar=g[:, m:m + 1],
                                                   in1=root[:, :], op0=ALU.mult, op1=ALU.mult))
                    ch.do(dve.tensor_scalar(v[:, m, :], v[:, m, :], b[:, m:m + 1], None, ALU.add))
                    dve.sem_inc(done, 1)
                    if x is not None:
                        modulate(dve, ch, mod, m, x, v[:, m, :], h, n)


def pool_and_gate(nc, c, t, z, x):
    NCK = T2 // P
    PAD, W = 8, 8 + SEQ + 16 + CTX + 8
    VE = Order("copied", "copied_ctx", "pair", "four", "eight", "sixteen", "average", "diff_x", "diff_ctx",
               "pooled", "high", "low")
    with Phase(nc, "pool") as ph:
        a, ga, inv = ph.sb("a", (P, T2)), ph.sb("ga", (P, T2)), ph.sb("inv", (P, T2))
        pad = ph.sb("pad", (P, W))
        s = [ph.sb(f"s{k}", (P, W)) for k in range(4)]
        d, sg = ph.sb("d", (P, T2)), ph.sb("sg", (P, T2))
        pw, scale = ph.sb("pool_w", (P, 4, P)), ph.sb("pool_scale", (P, 4))
        ps = ph.ps("pooled", (P, 1536))
        small, landed_a, landed_g, silu, made = (ph.sem(n) for n in ("small", "a_landed", "gate_landed", "silu",
                                                                     "made"))
        step, zeroed = ph.sem("step"), ph.sem("zeroed")
        seqs = ((PAD, 0, SEQ), (PAD + SEQ + 16, SEQ, CTX))
        with nc.Block() as block:
            @block.sync
            def _(sp):
                sp.dma_start(pw[:, :, :], t["pool_w"]).then_inc(small, 16)
                sp.dma_start(scale[:, :], t["pool_scale"]).then_inc(small, 16)
                for g in range(4):
                    if g:
                        sp.wait_ge(step, VE.at(g - 1, "diff_ctx"))
                    sp.dma_start(a[:, :], z[g]).then_inc(landed_a, 16)
                    sp.dma_start(inv[:, :], t["inv_count"][g]).then_inc(landed_a, 16)
                    if g:
                        sp.wait_ge(silu, g)
                    sp.dma_start(ga[:, :], z[4 + g]).then_inc(landed_g, 16)

            @block.scalar
            def _(act):
                for g in range(4):
                    act.wait_ge(landed_g, 16 * (g + 1))
                    if g:
                        act.wait_ge(step, VE.at(g - 1, "pooled"))
                    act.activation(sg[:, :], ga[:, :], ACT.Silu).then_inc(silu, 1)

            @block.tensor
            def _(pe):
                pe.wait_ge(small, 32)
                for g in range(4):
                    pe.wait_ge(step, VE.at(g, "diff_ctx"))
                    for bk, c0, w in pieces(T2):
                        mm = pe.matmul(ps[:, c0:c0 + w], pw[:, g, :], d[:, c0:c0 + w], start=True, stop=True)
                    mm.then_inc(made, 1)

            @block.vector
            def _(dve):
                ch = Chain(dve, step)
                tt = dve.tensor_tensor
                for b in [pad] + s:
                    dve.memset(b[:, :], 0.0).then_inc(zeroed, 1)
                dve.wait_ge(zeroed, 5)
                dve.wait_ge(small, 32)
                for g in range(4):
                    dve.wait_ge(landed_a, 32 * (g + 1))
                    for p0, c0, n in seqs:
                        ins = dve.tensor_copy(pad[:, p0:p0 + n], a[:, c0:c0 + n])
                        ch.do(ins)
                    ch.do(tt(s[0][:, 1:W], pad[:, 0:W - 1], pad[:, 1:W], ALU.add))
                    for k in range(1, 4):
                        q = 2 ** (k - 1)
                        lo, hi = 2 ** k, W - 2 ** k
                        ch.do(tt(s[k][:, lo:hi], s[k - 1][:, lo - q:hi - q], s[k - 1][:, lo + q:hi + q], ALU.add))
                    for u, (p0, c0, n) in enumerate(seqs):
                        ch.inc(tt(d[:, c0:c0 + n], s[g][:, p0:p0 + n], inv[:, c0:c0 + n], ALU.mult))
                    dve.wait_ge(step, ch.n)
                    ch.do(tt(d[:, :], d[:, :], a[:, :], ALU.subtract))
                    dve.wait_ge(made, g + 1)
                    dve.wait_ge(silu, g + 1)
                    ch.do(dve.scalar_tensor_tensor(out=d[:, :], in0=ps[:, 0:T2], scalar=scale[:, g:g + 1],
                                                   in1=sg[:, :], op0=ALU.mult, op1=ALU.mult))
                    ch.do(split(dve, ch, x[0][:, g, :], x[1][:, g, :], d[:, :]))
                    assert ch.n == len(VE.names) * (g + 1)

    with Phase(nc, "sgu") as ph:
        u, v, gb = ph.sb("u", (P, T2)), ph.sb("v", (P, T2)), ph.sb("gb", (P, T2))
        vt = ph.sb("vt", (P, NCK, P))
        st, mv, root = ph.sb("stats", (P, NCK, 6)), ph.sb("mean_var", (P, NCK, 2)), ph.sb("root", (P, NCK))
        sw, sb_ = ph.sb("sgu_w", (P, 4, P)), ph.sb("sgu_b", (P, 4, P))
        f, sg = ph.sb("f", (P, NCK, P)), ph.sb("sg", (P, T2))
        pt = ph.ps("turned", (P, 1536))
        pf = ph.ps("mixed", (P, 1536))
        small, landed, silu, turned, made = (ph.sem(n) for n in ("small", "landed", "silu", "turned", "made"))
        step, stats, rooted, vn, done = (ph.sem(n) for n in ("step", "stats", "rooted", "normed", "done"))
        flat = lambda a: a[:, :, :].rearrange("p a b -> p (a b)")
        with nc.Block() as block:
            @block.sync
            def _(sp):
                sp.dma_start(sw[:, :, :], t["sgu_w"]).then_inc(small, 16)
                sp.dma_start(sb_[:, :, :], t["sgu_b"]).then_inc(small, 16)
                for h in range(4):
                    if h:
                        sp.wait_ge(done, h)
                    for buf, k in ((v, 12), (u, 8), (gb, 16)):
                        sp.dma_start(buf[:, :], z[k + h]).then_inc(landed, 16)

            @block.scalar
            def _(act):
                for h in range(4):
                    act.wait_ge(landed, 48 * (h + 1))
                    act.activation(sg[:, :], gb[:, :], ACT.Silu).then_inc(silu, 1)
                    act.wait_ge(stats, h + 1)
                    act.activation(root[:, :], mv[:, :, 1], ACT.Sqrt, bias=c["eps"][:, 0:1]).then_inc(rooted, 1)

            @block.tensor
            def _(pe):
                pe.wait_ge(small, 32)
                for h in range(4):
                    pe.wait_ge(landed, 48 * (h + 1))
                    for b in range(NCK):
                        mm = pe.transpose(pt[:, P * b:P * b + P], v[:, P * b:P * b + P], c["ident"][:, :])
                    mm.then_inc(turned, 1)
                    pe.wait_ge(vn, h + 1)
                    for b in range(NCK):
                        mm = pe.matmul(pf[:, P * b:P * b + P], vt[:, b, :], sw[:, h, :], start=True, stop=True)
                    mm.then_inc(made, 1)

            @block.vector
            def _(dve):
                ch = Chain(dve, step)
                dve.wait_ge(small, 32)
                for h in range(4):
                    dve.wait_ge(turned, h + 1)
                    for b in range(NCK):
                        ch.inc(dve.bn_stats(st[:, b, :], pt[:, P * b:P * b + P]))
                    dve.wait_ge(step, ch.n)
                    for b in range(NCK):
                        ch.inc(dve.bn_aggr(mv[:, b, :], st[:, b, :]))
                    dve.wait_ge(step, ch.n)
                    dve.sem_inc(stats, 1)
                    dve.wait_ge(rooted, h + 1)
                    ch.do(dve.reciprocal(root[:, :], root[:, :]))
                    for b in range(NCK):
                        ch.inc(dve.tensor_scalar(vt[:, b, :], pt[:, P * b:P * b + P], mv[:, b, 0:1],
                                                 root[:, b:b + 1], ALU.subtract, ALU.mult))
                    dve.wait_ge(step, ch.n)
                    dve.sem_inc(vn, 1)
                    dve.wait_ge(made, h + 1)
                    ch.do(dve.tensor_tensor(f[:, :, :], pf[:, 0:T2].rearrange("p (a b) -> p a b", b=P),
                                            sb_[:, h:h + 1, :].broadcast_to([P, NCK, P]), ALU.add))
                    ch.do(dve.tensor_tensor(flat(f), flat(f), u[:, :], ALU.mult))
                    dve.wait_ge(silu, h + 1)
                    ch.do(dve.tensor_tensor(flat(f), flat(f), sg[:, :], ALU.mult))
                    ch.do(split(dve, ch, x[0][:, 4 + h, :], x[1][:, 4 + h, :], flat(f)))
                    dve.sem_inc(done, 1)


def fourier(nc, c, t, z, x):
    LT = SEQ // P
    with Phase(nc, "fnet") as ph:
        fin, fg = [ph.sb(f"f_in{j}", (P, SEQ)) for j in range(2)], [ph.sb(f"gate{j}", (P, SEQ)) for j in range(2)]
        dd = ph.sb("dft_features", (P, 2 * P))
        dl = ph.sb("dft_tokens", (P, 2, LT, SEQ))
        pq = [ph.sb(f"pq{j}", (P, LT, 2 * P)) for j in range(2)]
        sp_ = ph.sb("spectrum", (P, 4, SEQ))
        w = ph.sb("fnet_w", (P, 4, 512))
        sg = [ph.sb(f"silu{j}", (P, SEQ)) for j in range(2)]
        y = ph.sb("y", (P, SEQ))
        p1 = ph.ps("features", (P, 4, 512))
        p2 = [ph.ps(f"tokens{j}", (P, 1024)) for j in range(2)]
        const, tokens_in = ph.sem("constants"), ph.sem("dft_tokens_in")
        landed, g_landed = ([ph.sem(f"{n}{j}") for j in range(2)] for n in ("f_in_landed", "gate_landed"))
        first, first_out, second, second_out = (ph.sem(n) for n in ("first", "first_out", "second", "second_out"))
        silu, step, done = ph.sem("silu"), ph.sem("step"), ph.sem("done")
        with nc.Block() as block:
            @block.sync
            def _(sp):
                sp.dma_start(dd[:, :], t["dft_features"]).then_inc(const, 16)
                sp.dma_start(w[:, :, :], t["fnet_w"]).then_inc(const, 16)
                for h in range(2):
                    sp.dma_start(fin[h][:, :], z[h]).then_inc(landed[h], 16)
                sp.dma_start(dl[:, :, :, :], t["dft_tokens"]).then_inc(tokens_in, 16)
                for h in range(2, 4):
                    sp.wait_ge(first, 4 * (h - 1))
                    sp.dma_start(fin[h % 2][:, :], z[h]).then_inc(landed[h % 2], 16)
                for m in range(4):
                    if m >= 2:
                        sp.wait_ge(silu, m - 1)
                    sp.dma_start(fg[m % 2][:, :], z[4 + m]).then_inc(g_landed[m % 2], 16)

            @block.tensor
            def _(pe):
                pe.wait_ge(const, 32)

                def features(h):
                    pe.wait_ge(landed[h % 2], 16 * (h // 2 + 1))
                    for b in range(4):
                        if h:
                            pe.wait_ge(first_out, 4 * (h - 1) + b + 1)
                        for u in range(2):
                            q = 2 * b + u
                            mm = pe.matmul(p1[:, b, 256 * u:256 * u + 256], fin[h % 2][:, P * q:P * q + P],
                                           dd[:, :], start=True, stop=True)
                        mm.then_inc(first, 1)
                features(0)
                for h in range(4):
                    if h + 1 < 4:
                        features(h + 1)
                    pe.wait_ge(first_out, 4 * (h + 1))
                    pe.wait_ge(tokens_in, 16)
                    if h >= 2:
                        pe.wait_ge(second_out, h - 1)
                    for b in range(2):
                        for n in range(2 * LT):
                            part, q = divmod(n, LT)
                            mm = pe.matmul(p2[h % 2][:, 512 * b:512 * b + 512], pq[h % 2][:, q, P * part:P * part + P],
                                           dl[:, part, q, 512 * b:512 * b + 512], start=n == 0, stop=n == 2 * LT - 1)
                    mm.then_inc(second, 1)
                for m in range(4):
                    pe.wait_ge(second_out, 4 if m < 2 else 4 + m - 1)
                    for b in range(2):
                        for k in range(4):
                            mm = pe.matmul(p2[m % 2][:, 512 * b:512 * b + 512], w[:, k, P * m:P * m + P],
                                           sp_[:, k, 512 * b:512 * b + 512], start=k == 0, stop=k == 3)
                    mm.then_inc(second, 1)

            @block.scalar
            def _(act):
                for h in range(4):
                    for b in range(4):
                        act.wait_ge(first, 4 * h + b + 1)
                        if h >= 2:
                            act.wait_ge(second, h - 1)
                        act.activation(pq[h % 2][:, 2 * b:2 * b + 2, :].rearrange("p a b -> p (a b)"), p1[:, b, :],
                                       ACT.Copy).then_inc(first_out, 1)
                for m in range(4):
                    act.wait_ge(g_landed[m % 2], 16 * (m // 2 + 1))
                    if m >= 2:
                        act.wait_ge(done, m - 1)
                    act.activation(sg[m % 2][:, :], fg[m % 2][:, :], ACT.Silu).then_inc(silu, 1)

            @block.vector
            def _(dve):
                ch = Chain(dve, step)
                for h in range(4):
                    dve.wait_ge(second, h + 1)
                    dve.tensor_copy(sp_[:, h, :], p2[h % 2][:, :]).then_inc(second_out, 1)
                for m in range(4):
                    dve.wait_ge(second, 4 + m + 1)
                    dve.wait_ge(silu, m + 1)
                    dve.tensor_tensor(y[:, :], p2[m % 2][:, :], sg[m % 2][:, :], ALU.mult).then_inc(second_out, 1)
                    dve.wait_ge(second_out, 4 + m + 1)
                    ch.do(split(dve, ch, x[0][:, m, :], x[1][:, m, :], y[:, :]))
                    dve.sem_inc(done, 1)


def mla_operands(nc, c, t, z, zk, qc, kc, vc, room):
    QT = QL // P
    with Phase(nc, "mla") as ph:
        cq = room[0][:, 0:QT * SEQ].rearrange("p (k n) -> p k n", k=QT)
        wq = room[1][:, 0:QT * NH * P].rearrange("p (k h m) -> p k h m", k=QT, h=NH)
        ckv, kr = ph.sb("ckv", (P, T2)), ph.sb("kr", (P, T2))
        wk, wv = ph.sb("wk", (P, NH, NOPE)), ph.sb("wv", (P, NH * VD))
        qn, kn = ph.sb("q_norm", (P, QT)), ph.sb("kv_norm", (P, 1))
        turn = ph.sb("turn", (P, T2))
        sq = [ph.sb(f"sq{k}", (P, SEQ)) for k in range(QT)] + [ph.sb("sq_kv", (P, T2))]
        root, rk, tmp = sq[0], sq[2], sq[2]
        pq = [ph.ps(f"q{j}", (P, 1024)) for j in range(2)]
        pk = ph.ps("k", (P, 1536))
        pv = ph.ps("v", (P, 512))
        landed, squared, summed, rooted, normed = (ph.sem(n) for n in ("landed", "squared", "summed", "rooted",
                                                                       "normed"))
        q_made, q_low, q_high, k_made, k_out = (ph.sem(n) for n in ("q_made", "q_plain_out", "q_turned_out",
                                                                    "k_made", "k_out"))
        v_made, v_out, step, kr_done, kr_copied = (ph.sem(n) for n in ("v_made", "v_out", "step", "kr_done",
                                                                       "kr_copied"))
        loads = ((cq[:, 0, :], z[8]), (cq[:, 1, :], z[9]), (ckv[:, :], zk[0]), (kr[:, :], zk[1]),
                 (wq[:, :, :, :], t["w_q_up"]), (wk[:, :, :], t["w_k_up"]), (wv[:, :], t["w_v_up"]),
                 (qn[:, :], t["q_norm"]), (kn[:, :], t["kv_norm"]), (turn[:, :], t["rope"]))
        A, B = slice(NOPE, NOPE + ROPE), slice(NOPE + ROPE, P)
        with nc.Block() as block:
            @block.sync
            def _(sp):
                for dst, src in loads:
                    sp.dma_start(dst, src).then_inc(landed, 16)

            @block.tensor
            def _(pe):
                pe.wait_ge(squared, 3)
                for b, c0, w in pieces(SEQ):
                    for k in range(QT):
                        pe.matmul(pq[0][:, c0:c0 + w], c["ones"][:, :], sq[k][:, c0:c0 + w], start=k == 0,
                                  stop=k == QT - 1)
                for b, c0, w in pieces(T2):
                    mm = pe.matmul(pk[:, c0:c0 + w], c["ones"][:, :], sq[2][:, c0:c0 + w], start=True, stop=True)
                mm.then_inc(summed, 1)
                pe.wait_ge(normed, 3)
                for h in range(NH):
                    if h >= 2:
                        pe.wait_ge(q_low, h - 1)
                        pe.wait_ge(q_high, h - 1)
                    for b, c0, w in pieces(SEQ):
                        for k in range(QT):
                            mm = pe.matmul(pq[h % 2][:, c0:c0 + w], wq[:, k, h, :], cq[:, k, c0:c0 + w],
                                           start=k == 0, stop=k == QT - 1)
                    mm.then_inc(q_made, 1)
                    if h:
                        pe.wait_ge(k_out, h)
                    for b, c0, w in pieces(T2):
                        mm = pe.matmul(pk[0:NOPE, c0:c0 + w], wk[:, h, :], ckv[:, c0:c0 + w], start=True, stop=True)
                    mm.then_inc(k_made, 1)
                for b in range(T2 // P):
                    if b:
                        pe.wait_ge(v_out, b)
                    pe.matmul(pv[:, :], ckv[:, P * b:P * b + P], wv[:, :], start=True, stop=True).then_inc(v_made, 1)

            @block.scalar
            def _(act):
                act.wait_ge(landed, 16 * len(loads))
                for k in range(QT):
                    act.activation(sq[k][:, :], cq[:, k, :], ACT.Square).then_inc(squared, 1)
                act.activation(sq[2][:, :], ckv[:, :], ACT.Square).then_inc(squared, 1)
                act.wait_ge(summed, 1)
                act.activation(root[:, :], pq[0][:, :], ACT.Sqrt, bias=c["eps"][:, 0:1],
                               scale=1.0 / QL).then_inc(rooted, 1)
                act.activation(rk[:, :], pk[:, 0:T2], ACT.Sqrt, bias=c["eps"][:, 0:1],
                               scale=1.0 / KVL).then_inc(rooted, 1)
                for h in range(NH):
                    act.wait_ge(q_made, h + 1)
                    act.activation(qc[0:NOPE, h, :], pq[h % 2][0:NOPE, :], ACT.Copy).then_inc(q_low, 1)
                    act.wait_ge(k_made, h + 1)
                    act.activation(kc[0:NOPE, h, :], pk[0:NOPE, 0:T2], ACT.Copy).then_inc(k_out, 1)
                    if h == 0:
                        act.wait_ge(kr_done, 1)
                    act.activation(kc[A, h, :], kr[A, :], ACT.Copy).then_inc(kr_copied, 1)
                for b in range(T2 // P):
                    act.wait_ge(v_made, b + 1)
                    act.activation(vc[:, b, :].rearrange("p (h v) -> p h v", h=NH)[:, :, 0:VD],
                                   pv[:, :].rearrange("p (h v) -> p h v", h=NH), ACT.Copy).then_inc(v_out, 1)

            @block.vector
            def _(dve):
                ch = Chain(dve, step)
                tt = dve.tensor_tensor
                dve.memset(vc[:, :, :].rearrange("p b (h v) -> p (b h) v", v=VD + 1)[:, :, VD:VD + 1], 1.0)
                dve.memset(kc[NOPE + ROPE:NOPE + ROPE + 1, :, :], 1.0)
                dve.wait_ge(landed, 16 * len(loads))
                dve.wait_ge(rooted, 2)
                ch.inc(dve.reciprocal(root[:, :], root[:, :]))
                ch.do(dve.reciprocal(rk[:, :], rk[:, :]))
                for k in range(QT):
                    dve.scalar_tensor_tensor(out=cq[:, k, :], in0=cq[:, k, :], scalar=qn[:, k:k + 1], in1=root[:, :],
                                             op0=ALU.mult, op1=ALU.mult).then_inc(normed, 1)
                dve.scalar_tensor_tensor(out=ckv[:, :], in0=ckv[:, :], scalar=kn[:, 0:1], in1=rk[:, :],
                                         op0=ALU.mult, op1=ALU.mult).then_inc(normed, 1)
                dve.wait_ge(normed, 3)
                ch.inc(tt(tmp[A, :], kr[B, :], turn[B, :], ALU.mult))
                ch.do(tt(kr[A, :], kr[A, :], turn[A, :], ALU.mult))
                ch.do(tt(kr[A, :], kr[A, :], tmp[A, :], ALU.add))
                dve.sem_inc(kr_done, 1)
                for h in range(NH):
                    dve.wait_ge(q_made, h + 1)
                    ps = pq[h % 2]
                    ch.inc(tt(tmp[A, 0:SEQ], ps[B, :], turn[B, 0:SEQ], ALU.mult))
                    ch.do(tt(qc[A, h, :], ps[A, :], turn[A, 0:SEQ], ALU.mult))
                    ch.do(tt(qc[A, h, :], qc[A, h, :], tmp[A, 0:SEQ], ALU.add))
                    dve.sem_inc(q_high, 1)


def attention(nc, c, z, qc, kc, vc, x, room):
    NQT, NKT = SEQ // P, T2 // P
    KD, V1, HQ = NOPE + ROPE, VD + 1, NQT // 2
    SCORE_RING, PROB_RING = 3, 6
    scale = float(KD) ** -0.5
    with Phase(nc, "attn") as ph:
        pt = [ph.sb(f"probs{j}", (P, 512)) for j in range(PROB_RING)]
        mx = ph.sb("max", (P, KD + NH * NQT))
        rr = ph.sb("inverse_sum", (P, HQ))
        zero = ph.sb("zeros", (1, P + HQ * V1), mybir.dt.bfloat16)
        o = room[0][:, :].rearrange("p (q n) -> p q n", q=NQT)
        dg = room[1][:, :].rearrange("p (m n) -> p m n", m=4)
        y = ph.sb("y", (P, SEQ))
        pa = ph.ps("scores", (P, 1536))
        pb = [ph.ps(f"turned_scores{j}", (P, 512)) for j in range(SCORE_RING)]
        pc = [ph.ps(f"values{j}", (P, 512)) for j in range(2)]
        zeroed, scored, maxed, rows_made, rows_out = (ph.sem(n) for n in (
            "zeroed", "scored", "maxed", "rows_made", "rows_out"))
        turned, exped, used, summed, normal = (ph.sem(n) for n in ("turned", "exponentials", "probs_used", "summed",
                                                                  "normal"))
        step, landed, back, back_used, silu = (ph.sem(n) for n in ("step", "landed", "back", "back_used", "silu"))
        with nc.Block() as block:
            @block.sync
            def _(sp):
                for m in range(4):
                    sp.dma_start(dg[:, m, :], z[10 + m]).then_inc(landed, 16)

            @block.tensor
            def _(pe):
                def scores(h, q):
                    i = h * NQT + q
                    if q == 0 and h:
                        pe.wait_ge(rows_out, h)
                    elif q:
                        pe.wait_ge(maxed, i)
                    for b, c0, w in pieces(T2):
                        mm = pe.matmul(pa[:, c0:c0 + w], qc[0:KD, h, P * q:P * q + P], kc[0:KD, h, c0:c0 + w],
                                       start=True, stop=True)
                    mm.then_inc(scored, 1)

                def turn_maxima(h):
                    pe.wait_ge(maxed, NQT * (h + 1))
                    for q in range(NQT):
                        i = h * NQT + q
                        mm = pe.matmul(pa[0:KD + 1, P * q:P * q + P], mx[:, i:i + KD + 1], c["ident"][:, :],
                                       start=True, stop=True)
                    mm.then_inc(rows_made, 1)

                def turned_scores(h, k):
                    if k == 0:
                        pe.wait_ge(rows_out, h + 1)
                    for b in range(2):
                        u = 2 * (h * NKT + k) + b
                        if u >= SCORE_RING:
                            pe.wait_ge(exped, u - SCORE_RING + 1)
                        pe.matmul(pb[u % SCORE_RING][:, :], kc[0:KD + 1, h, P * k:P * k + P],
                                  qc[0:KD + 1, h, 512 * b:512 * b + 512], start=True, stop=True).then_inc(turned, 1)

                def values(h, k):
                    for b in range(2):
                        u = 2 * (h * NKT + k) + b
                        if k == 0:
                            if h:
                                pe.wait_ge(normal, 2 * (h - 1) + b + 1)
                            pe.matmul(pc[b][:, 0:HQ * V1], zero[:, 0:P], zero[:, P:P + HQ * V1],
                                      start=True, stop=False, skip_group_check=True)
                        pe.wait_ge(exped, u + 1)
                        for q in range(HQ):
                            mm = pe.matmul(pc[b][:, V1 * q:V1 * (q + 1)], pt[u % PROB_RING][:, P * q:P * q + P],
                                           vc[:, k, V1 * h:V1 * (h + 1)], start=False,
                                           stop=k == NKT - 1 and q == HQ - 1, skip_group_check=True)
                        mm.then_inc(used, 1)
                pe.wait_ge(zeroed, 2)
                for q in range(NQT):
                    scores(0, q)
                turn_maxima(0)
                for h in range(NH):
                    for k in range(NKT):
                        if h + 1 < NH and k < NQT:
                            scores(h + 1, k)
                        if h + 1 < NH and k == NQT:
                            turn_maxima(h + 1)
                        turned_scores(h, k)
                        if k:
                            values(h, k - 1)
                        elif h:
                            values(h - 1, NKT - 1)
                values(NH - 1, NKT - 1)
                for m in range(4):
                    if m == 0:
                        pe.wait_ge(normal, 2 * NH)
                    else:
                        pe.wait_ge(back_used, m)
                    for q in range(NQT):
                        mm = pe.transpose(pa[:, P * q:P * q + P], o[:, q, P * m:P * m + P], c["ident"][:, :])
                    mm.then_inc(back, 1)

            @block.scalar
            def _(act):
                def rows(h):
                    act.wait_ge(rows_made, h + 1)
                    act.activation(qc[KD:KD + 1, h, :], pa[KD:KD + 1, 0:SEQ], ACT.Copy,
                                   scale=-1.0).then_inc(rows_out, 1)
                act.wait_ge(landed, 64)
                for m in range(4):
                    act.activation(dg[:, m, :], dg[:, m, :], ACT.Silu).then_inc(silu, 1)
                rows(0)
                for h in range(NH):
                    for k in range(NKT):
                        if h + 1 < NH and k == NQT:
                            rows(h + 1)
                        for b in range(2):
                            u = 2 * (h * NKT + k) + b
                            act.wait_ge(turned, u + 1)
                            if u >= PROB_RING:
                                act.wait_ge(used, u - PROB_RING + 1)
                            act.activation(pt[u % PROB_RING][:, :], pb[u % SCORE_RING][:, :], ACT.Exp,
                                           scale=scale).then_inc(exped, 1)

            @block.vector
            def _(dve):
                ch = Chain(dve, step)

                def maximum(h, q):
                    i = h * NQT + q
                    dve.wait_ge(scored, i + 1)
                    dve.tensor_reduce(mx[:, KD + i:KD + i + 1], pa[:, 0:T2], AX.X, ALU.max).then_inc(maxed, 1)

                def normalise(h):
                    for b in range(2):
                        dve.wait_ge(used, 2 * (h * NKT + NKT - 1) + b + 1)
                        sums = pc[b][:, 0:HQ * V1].rearrange("p (q v) -> p q v", v=V1)
                        ch.do(dve.reciprocal(rr[:, :], sums[:, :, VD]))
                        ins = dve.tensor_tensor(o[:, HQ * b:HQ * (b + 1), VD * h:VD * (h + 1)], sums[:, :, 0:VD],
                                                rr[:, :].unsqueeze(2).broadcast_to([P, HQ, VD]), ALU.mult)
                        ins.then_inc(normal, 1)
                        dve.wait_ge(normal, 2 * h + b + 1)
                dve.memset(mx[:, 0:KD], 0.0).then_inc(zeroed, 1)
                dve.memset(zero[:, :], 0.0).then_inc(zeroed, 1)
                for q in range(NQT):
                    maximum(0, q)
                for h in range(NH):
                    for k in range(NKT):
                        if h + 1 < NH and k < NQT:
                            maximum(h + 1, k)
                        if h and k == 1:
                            normalise(h - 1)
                normalise(NH - 1)
                for m in range(4):
                    dve.wait_ge(back, m + 1)
                    dve.wait_ge(silu, m + 1)
                    ch.do(dve.tensor_tensor(y[:, :], pa[:, 0:SEQ], dg[:, m, :], ALU.mult))
                    dve.sem_inc(back_used, 1)
                    ch.do(split(dve, ch, x[0][:, m, :], x[1][:, m, :], y[:, :]))


def setup(nc, ph, t, c):
    shapes = {"ident": (P, P), "chunk_mask": (P, T1), "causal": (P, 9, P), "mix_g": (P, DT), "ffn_g": (P, DT),
              "final_g": (P, DT), "hgrn_g": (P, 1), "ab_g": (P, DT), "ab_b": (P, DT), "cd_g": (P, DT),
              "cd_b": (P, DT), "lb_logits": (P, 2, HH)}
    for n, sh in shapes.items():
        c[n] = ph.sb(n, sh)
    for n, sh in {"ones": (P, P), "eps": (P, 1), "lb": (P, HH), "one_minus_lb": (P, HH)}.items():
        c[n] = ph.sb(n, sh)
    with Phase(nc, "setup") as s:
        m, e0, e1 = (s.sb(n, (P, HH)) for n in ("m", "e0", "e1"))
        landed, step, ex = s.sem("landed"), s.sem("step"), s.sem("exponentials")
        with nc.Block() as block:
            @block.sync
            def _(sp):
                for n, sh in shapes.items():
                    sp.dma_start(c[n][:], t[n]).then_inc(landed, 16)
                sp.wait_ge(landed, 16 * len(shapes))

            @block.vector
            def _(dve):
                ch = Chain(dve, step)
                dve.memset(c["ones"][:, :], 1.0)
                dve.memset(c["eps"][:, :], EPS)
                dve.wait_ge(landed, 16 * len(shapes))
                l0, l1 = c["lb_logits"][:, 0, :], c["lb_logits"][:, 1, :]
                ch.do(dve.tensor_tensor(m[:, :], l0, l1, ALU.max))
                ch.inc(dve.tensor_tensor(e0[:, :], l0, m[:, :], ALU.subtract))
                ch.inc(dve.tensor_tensor(e1[:, :], l1, m[:, :], ALU.subtract))
                dve.wait_ge(ex, 2)
                ch.do(dve.tensor_tensor(e1[:, :], e0[:, :], e1[:, :], ALU.add))
                ch.do(dve.reciprocal(e1[:, :], e1[:, :]))
                ch.do(dve.tensor_tensor(c["lb"][:, :], e0[:, :], e1[:, :], ALU.mult))
                ch.do(dve.tensor_scalar(c["one_minus_lb"][:, :], c["lb"][:, :], -1.0, 1.0, ALU.mult, ALU.add))

            @block.scalar
            def _(act):
                act.wait_ge(step, 3)
                act.activation(e0[:, :], e0[:, :], ACT.Exp).then_inc(ex, 1)
                act.activation(e1[:, :], e1[:, :], ACT.Exp).then_inc(ex, 1)


def load_one(nc, name, buf, src):
    with Phase(nc, f"load_{name}") as ph:
        landed = ph.sem("landed")
        with nc.Block() as block:
            @block.sync
            def _(sp):
                sp.dma_start(buf[:], src).then_inc(landed, 16)
                sp.wait_ge(landed, 16)


def square_sum(nc, hd, acc):
    with Phase(nc, "square_sum") as ph:
        a = [ph.sb(f"a{j}", (P, T1)) for j in range(2)]
        s = [ph.sb(f"s{j}", (P, T1)) for j in range(2)]
        landed = [ph.sem(f"landed{j}") for j in range(2)]
        squared, added = ph.sem("squared"), ph.sem("added")
        with nc.Block() as block:
            @block.sync
            def _(sp):
                for m in range(DT):
                    if m >= 2:
                        sp.wait_ge(squared, m - 1)
                    sp.dma_start(a[m % 2][:, :], hd[m]).then_inc(landed[m % 2], 16)

            @block.scalar
            def _(act):
                for m in range(DT):
                    act.wait_ge(landed[m % 2], 16 * (m // 2 + 1))
                    if m >= 2:
                        act.wait_ge(added, m - 1)
                    act.activation(s[m % 2][:, :], a[m % 2][:, :], ACT.Square).then_inc(squared, 1)

            @block.vector
            def _(dve):
                for m in range(DT):
                    dve.wait_ge(squared, m + 1)
                    if m == 0:
                        ins = dve.tensor_copy(acc[:, :], s[0][:, :])
                    else:
                        ins = dve.tensor_tensor(acc[:, :], acc[:, :], s[m % 2][:, :], ALU.add)
                    ins.then_inc(added, 1)
                    dve.wait_ge(added, m + 1)


def build(nc, t):
    def scratch(name, tiles, n):
        return nc.dram_tensor(name, (tiles, P, n), F32, kind="Internal").ap()
    t["p"] = scratch("p", 7 * DT, T1)
    t["y_glu"] = scratch("y_glu", DT, T1)
    t["mb"] = scratch("mb", DT, T1)
    t["h"] = scratch("h", DT, T1)
    c = {}

    def pair(ph, name, tiles, n):
        return [ph.sb(f"{name}_{part}", (P, tiles, n), F32R) for part in ("high", "low")]

    own = lambda s, a, m: a[m]
    root = Phase(nc, "all")
    setup(nc, root, t, c)
    with Phase(nc, "mix") as outer:
        rms = outer.sb("inverse_rms", (P, T1))
        acc = outer.sb("squares", (P, T1))
        xa = pair(outer, "z", DT, T1)
        prepare_input(nc, c, t["xt"], xa, acc)
        inverse_rms(nc, "mix_rms", acc, rms, D, c, T1)
        epi, steps = epi_scale_store(rms)
        dense(nc, "w_in", t["w_in"], 7 * DT, DT, xa, T1, epi, store=lambda m: t["p"][m], steps=steps)
    with Phase(nc, "yb") as outer:
        xb = pair(outer, "yb", DT, T1)
        hgrn(nc, c, t["p"], xb)
        epi, steps = epi_gate(None)
        dense(nc, "hgrn_proj", t["w_hgrn_proj"], DT, DT, xb, T1, epi, sides=(t["p"],),
              side_at=lambda s, a, m: a[m + 6 * DT], store=lambda m: t["mb"][m], steps=steps)
    t["u_chunks"] = scratch("u_chunks", DT, T1)
    t["y_chunks"] = scratch("y_chunks", DT, T1)
    reorder_u(nc, t["p"], t["u_chunks"])
    s5(nc, c, t, t["u_chunks"], t["y_chunks"])
    with Phase(nc, "first") as outer:
        xa, xb = pair(outer, "operand_a", DT, T1), pair(outer, "operand_b", DT, T1)
        split_y(nc, t["y_chunks"], t["y_glu"], xa)
        epi, steps = epi_glu(xb)
        dense(nc, "glu", t["w_glu"], DT, DT, xa, T1, epi, sides=(t["y_glu"],), side_at=own, steps=steps)
        epi, steps = epi_gate(xa)
        dense(nc, "ssm_proj", t["w_ssm_proj"], DT, DT, xb, T1, epi, sides=(t["p"], t["mb"]),
              side_at=lambda s, a, m: a[m + 5 * DT] if s == 0 else a[m], steps=steps)
        rms = outer.sb("inverse_rms", (P, T1))
        epi, steps = epi_residual_norm(xb, c["ffn_g"], rms)
        dense(nc, "w_out", t["w_out"], DT, DT, xa, T1, epi, sides=(t["xt"],), side_at=own,
              store=lambda m: t["h"][m], steps=steps)
        inverse_rms(nc, "ffn_rms", rms, rms, D, c, T1)
        conv = outer.sb("conv", (P, 2 * FT, 4))
        load_one(nc, "conv", conv, t["conv"])
        f0 = 0
        for n, k in enumerate((8, 8, 6)):
            epi, steps = epi_conv(rms, conv, xa, 2 * f0)
            dense(nc, f"up{n}", t["w_up"], 2 * k, DT, xb, T1, epi, steps=steps, off=2 * f0)
            epi, steps = epi_residual()
            dense(nc, f"down{n}", t[f"w_down{n}"], DT, k, xa, T1, epi, sides=(t["h"],), side_at=own,
                  store=lambda m: t["h"][m], steps=steps)
            f0 += k
    t["x1"], t["x2"] = scratch("x1", DT, T2), scratch("x2", DT, T2)
    t["v"], t["abz"] = scratch("v", DT, T2), scratch("abz", 20, T2)
    t["v_out"] = scratch("v_out", DT, SEQ)
    t["cdz"], t["cdk"] = scratch("cdz", 14, SEQ), scratch("cdk", 2, T2)
    with Phase(nc, "second") as outer:
        mod, mod2 = outer.sb("mod_ab", (P, 3 * DT, 2)), outer.sb("mod_cd", (P, 3 * DT, 2))
        modulation(nc, "mod1", t, t["cond"], t["ab_w_mod"], t["ab_b_mod"], mod)
        modulation(nc, "mod2", t, t["cond"], t["cd_w_mod"], t["cd_b_mod"], mod2)
        with Phase(nc, "abx") as inner:
            xa = pair(inner, "operand", DT, T2)
            with Phase(nc, "final") as f:
                rms = f.sb("inverse_rms", (P, T1))
                square_sum(nc, t["h"], rms)
                inverse_rms(nc, "final_rms", rms, rms, D, c, T1)
                finish_first(nc, c, t["h"], t["ctx"], t["x1"], rms, mod, xa)
            epi, steps = epi_scale_store(None)
            dense(nc, "ab_in", t["ab_w_in"], 20, DT, xa, T2, epi, store=lambda m: t["abz"][m], steps=steps)
        with Phase(nc, "abm") as inner:
            xb = pair(inner, "operand", DT, T2)
            pool_and_gate(nc, c, t, t["abz"], xb)
            epi, steps = epi_gated_residual(mod, T2)
            dense(nc, "ab_out", t["ab_w_out"], DT, DT, xb, T2, epi, sides=(t["x1"],), side_at=own,
                  store=lambda m: t["v"][m], steps=steps)
        with Phase(nc, "cdx") as inner:
            xa = pair(inner, "operand", DT, T2)
            layer_norm(nc, "ab_norm", c, t["v"], T2, c["ab_g"], c["ab_b"], t["x2"], mod2, xa)
            epi, steps = epi_scale_store(None)
            dense(nc, "cd_in", t["cd_w_in"], 14, DT, xa, SEQ, epi, store=lambda m: t["cdz"][m], steps=steps)
            epi, steps = epi_scale_store(None)
            dense(nc, "cd_kv", t["cd_w_kv"], 2, DT, xa, T2, epi, store=lambda m: t["cdk"][m], steps=steps)
        with Phase(nc, "cdm") as inner:
            xv = pair(inner, "attended", 4, SEQ)
            with Phase(nc, "qkv") as q:
                qc, kc = q.sb("queries", (P, NH, SEQ)), q.sb("keys", (P, NH, T2))
                vc = q.sb("values", (P, T2 // P, NH * (VD + 1)))
                room = [q.sb(f"room{j}", (P, 4 * SEQ)) for j in range(2)]
                mla_operands(nc, c, t, t["cdz"], t["cdk"], qc, kc, vc, room)
                attention(nc, c, t["cdz"], qc, kc, vc, xv, room)
            with Phase(nc, "cdo") as o:
                xf = pair(o, "spectrum", 4, SEQ)
                fourier(nc, c, t, t["cdz"], xf)
                epi, steps = epi_gated_residual(mod2, SEQ)
                dense(nc, "cd_out", t["cd_w_out"], DT, DT, [Halves(xf[j], xv[j]) for j in range(2)], SEQ, epi,
                      sides=(t["x2"],), side_at=lambda s, a, m: a[m][:, 0:SEQ], store=lambda m: t["v_out"][m],
                      steps=steps)
        layer_norm(nc, "cd_norm", c, t["v_out"], SEQ, c["cd_g"], c["cd_b"], t["out"])


def columns(v):
    return np.ascontiguousarray(np.asarray(v).reshape(-1, P).T)


def weight_tiles(w):
    k, m = w.shape
    return np.ascontiguousarray(w.reshape(k // P, P, m // P, P).transpose(2, 1, 0, 3)).reshape(m // P, P, -1)


def layout(a):
    f = np.float32
    o = {}
    xt = np.zeros((DT, P, T1), f)
    xt[:, :, :META] = a["meta_tokens"].T.reshape(DT, P, META)
    xt[:, :, META:META + SEQ] = a["x"][0].T.reshape(DT, P, SEQ)
    o["xt"] = xt
    for n, k in (("mix_g", "mix_norm_g"), ("ffn_g", "ffn_norm_g"), ("final_g", "final_norm_g"),
                 ("hgrn_g", "hgrn_norm_g")):
        o[n] = columns(a[k])
    o["lb_logits"] = np.ascontiguousarray(a["hgrn_lb_logits"].reshape(2, HH, P).transpose(2, 0, 1))
    for n, k in (("w_in", "w_in"), ("w_hgrn_proj", "w_hgrn_proj"), ("w_glu", "ssm_w_glu"),
                 ("w_ssm_proj", "w_ssm_proj"), ("w_out", "w_out")):
        o[n] = weight_tiles(a[k][0])

    def pairs(v, lead):
        v = np.asarray(v).reshape((NPAIR, 2, SS) + lead)
        return np.ascontiguousarray(np.moveaxis(v, 0, 2)).reshape((P, NPAIR) + lead)
    o["lam_re"], o["lam_im"] = pairs(a["ssm_lambda_re"][0], ()), pairs(a["ssm_lambda_im"][0], ())
    o["log_dt"] = pairs(np.broadcast_to(a["ssm_log_dt"][0][:, None], (G, SS)), ())
    o["b_re"], o["b_im"] = pairs(a["ssm_b_re"][0], (SG,)), pairs(a["ssm_b_im"][0], (SG,))
    o["c_re"], o["c_im"] = (pairs(a[n][0].transpose(0, 2, 1), (SG,)) for n in ("ssm_c_re", "ssm_c_im"))
    o["ssm_d"] = np.ascontiguousarray(np.tile(a["ssm_d"][0].reshape(G, SG).T, (TAU, 1)))
    ctx = a["ctx_2"][0].T.reshape(DT, P, CTX)
    o["ctx"] = np.ascontiguousarray(ctx)
    order = np.arange(2 * FT).reshape(2, FT).T.reshape(-1)
    o["w_up"] = np.ascontiguousarray(weight_tiles(a["w_up"][0])[order])
    cw = np.concatenate([a["conv_w"][0], a["conv_b"][0][None]])
    o["conv"] = np.ascontiguousarray(cw.reshape(4, 2 * FT, P)[:, order].transpose(2, 1, 0))
    for n, (r0, r1) in enumerate(((0, 1024), (1024, 2048), (2048, FF))):
        o[f"w_down{n}"] = weight_tiles(a["w_down"][0][r0:r1])
    o["cond"] = np.ascontiguousarray(np.stack([columns(a["c_2"][0]), columns(a["c_ctx_2"])], -1))
    for n in ("ab", "cd"):
        o[f"{n}_w_mod"] = weight_tiles(a[f"{n}_w_mod_2"][0])
        o[f"{n}_b_mod"] = columns(a[f"{n}_b_mod_2"][0])
        o[f"{n}_g"], o[f"{n}_b"] = columns(a[f"{n}_ln_g_2"][0]), columns(a[f"{n}_ln_b_2"][0])
        o[f"{n}_w_out"] = weight_tiles(a[f"{n}_w_out_2"][0])
    o["ab_w_in"] = weight_tiles(a["ab_w_in_2"][0])
    o["pool_w"] = np.ascontiguousarray(a["ab_pool_w_2"][0].transpose(1, 0, 2))
    o["pool_scale"] = columns(a["ab_pool_scale_2"][0])
    inv = []
    for w in POOLS:
        row = []
        for n in (SEQ, CTX):
            p = np.arange(n)
            row.append(1.0 / (np.minimum(p + w - w // 2, n) - np.maximum(p - w // 2, 0)))
        inv.append(np.tile(np.concatenate(row), (P, 1)))
    o["inv_count"] = np.stack(inv).astype(f)
    o["sgu_w"] = np.ascontiguousarray(a["ab_sgu_w_2"][0].transpose(2, 0, 1))
    o["sgu_b"] = np.ascontiguousarray(np.broadcast_to(a["ab_sgu_b_2"][0][None], (P, 4, P)))
    w = a["cd_w_in_2"][0]
    swap = np.concatenate([np.arange(8, 16), np.arange(0, 8), np.arange(24, 32), np.arange(16, 24)])
    kr = w[:, 1408:1440]
    o["cd_w_in"] = weight_tiles(np.concatenate([w[:, 0:1280], w[:, 1440:]], 1))
    o["cd_w_kv"] = weight_tiles(np.concatenate([w[:, 1280:1408], kr, kr, kr, kr[:, swap]], 1))
    wq = a["cd_w_q_up_2"][0].reshape(QL // P, P, NH, NOPE + ROPE)
    o["w_q_up"] = np.ascontiguousarray(np.concatenate([wq, wq[..., NOPE + swap]], -1).transpose(1, 0, 2, 3))
    wkv = a["cd_w_kv_up_2"][0].reshape(KVL, NH, NOPE + VD)
    o["w_k_up"] = np.ascontiguousarray(wkv[..., :NOPE])
    o["w_v_up"] = np.ascontiguousarray(wkv[..., NOPE:]).reshape(KVL, NH * VD)
    o["q_norm"], o["kv_norm"] = columns(a["cd_q_norm_2"][0]), columns(a["cd_kv_norm_2"][0])
    inv_f = 10000.0 ** (-np.arange(0, 16, 2) / 16)
    pos = np.arange(SEQ)
    ang = np.concatenate([np.outer(inv_f, pos // 64)] * 2 + [np.outer(inv_f, pos % 64)] * 2)
    sign = np.where(np.arange(ROPE) % 16 < 8, -1.0, 1.0)[:, None]
    rope = np.zeros((P, T2), f)
    rope[NOPE:NOPE + ROPE] = 1.0
    rope[NOPE:NOPE + ROPE, :SEQ] = np.cos(ang)
    rope[NOPE + ROPE:, :SEQ] = np.sin(ang) * sign
    o["rope"] = rope
    p = np.outer(np.arange(P), np.arange(P)) % P * (2 * np.pi / P)
    o["dft_features"] = (np.concatenate([np.cos(p), np.sin(p)], 1) / np.sqrt(P)).astype(f)
    p = np.outer(np.arange(SEQ), np.arange(SEQ)) % SEQ * (2 * np.pi / SEQ)
    d = (np.stack([np.cos(p), -np.sin(p)]) / np.sqrt(SEQ)).astype(f)
    o["dft_tokens"] = np.ascontiguousarray(d.reshape(2, SEQ // P, P, SEQ).transpose(2, 0, 1, 3))
    o["fnet_w"] = np.ascontiguousarray(a["cd_fnet_w_2"][0].reshape(4, P, 512).transpose(1, 0, 2))
    o["ident"] = np.eye(P, dtype=f)
    o["chunk_mask"] = np.tile((np.arange(T1) % CH != 0).astype(f), (P, 1))
    s, u = np.arange(P)[:, None], np.arange(P)[None, :]
    o["causal"] = np.ascontiguousarray(np.broadcast_to(((s // CH == u // CH) & (s <= u))[:, None, :], (P, 9, P)))
    o["causal"] = o["causal"].astype(f)
    return o


def kernel(**inputs):
    import concourse.bacc as bacc
    from concourse.bass_utils import run_bass_kernel_spmd
    arrays = layout({k: np.asarray(v) for k, v in inputs.items()})
    nc = bacc.Bacc("TRN2", target_bir_lowering=False, num_devices=1)
    t = {n: nc.dram_tensor(n, v.shape, F32, kind="ExternalInput").ap() for n, v in arrays.items()}
    t["out"] = nc.dram_tensor("out", (DT, P, SEQ), F32, kind="ExternalOutput").ap()
    build(nc, t)
    r = run_bass_kernel_spmd(nc, [arrays], core_ids=[0])
    y = r.results[0]["out"]
    return np.ascontiguousarray(y.reshape(D, SEQ).T).reshape(1, SEQ, D)
```

```python
from contextlib import ExitStack, contextmanager

import numpy as np

import concourse.bass as bass
from concourse import mybir

F32 = mybir.dt.float32
F32R = mybir.dt.float32r
ACT = mybir.ActivationFunctionType
ALU = mybir.AluOpType
AX = mybir.AxisListType

P = 128
D = 1024
DT = D // P
SEQ, META = 1024, 16
T1 = 1056
EPS = 1e-6
G, SG, SS = 64, 16, 64
TAU = 8
NCH = T1 // TAU
NPAIR = G // 2
HH = 8
CH = 32
NC = T1 // CH
FF = 2816
FT = FF // P
CTX = 256
T2 = SEQ + CTX
ALPHA = 4.0 ** 0.25
POOLS = (2, 4, 8, 16)
NH, NOPE, ROPE, VD = 8, 64, 32, 64
QL, KVL = 256, 128


class Halves:

    def __init__(self, first, second):
        self.parts, self.half = (first, second), first.shape[1]

    def __getitem__(self, key):
        p, k, n = key
        return self.parts[k // self.half][p, k % self.half, n]


def pieces(n):
    if n == T1:
        return [(b, 352 * b, 352) for b in range(3)]
    return [(b, 512 * b, min(512, n - 512 * b)) for b in range((n + 511) // 512)]


def pview(ps, n):
    if n == T1:
        return ps.rearrange("p (b x) -> p b x", b=3)[:, :, 0:352]
    return ps[:, 0:n]


def sview(ap, n):
    return ap.rearrange("p (b x) -> p b x", b=3) if n == T1 else ap


class Phase:

    def __init__(self, nc, name):
        self.nc, self.name, self.ctx, self.sems = nc, name, ExitStack(), []

    def __enter__(self):
        return self

    def sb(self, name, shape, dt=F32):
        return self.ctx.enter_context(self.nc.sbuf_tensor(f"{self.name}_{name}", list(shape), dt))

    def ps(self, name, shape, dt=F32):
        return self.ctx.enter_context(self.nc.psum_tensor(f"{self.name}_{name}", list(shape), dt))

    def sem(self, name):
        s = self.nc.alloc_semaphore(f"{self.name}_{name}")
        self.sems.append(s)
        return s

    def __exit__(self, *exc):
        if exc[0] is None:
            self.nc.clear_and_free_semaphores(self.sems)
            self.nc.all_engine_barrier()
            self.ctx.close()


class Chain:

    def __init__(self, eng, sem, n=0):
        self.eng, self.sem, self.n = eng, sem, n

    def inc(self, ins):
        ins.then_inc(self.sem, 1)
        self.n = self.n + 1
        return self.n

    def do(self, ins):
        self.eng.wait_ge(self.sem, self.inc(ins))

    @contextmanager
    def loop(self, trips, per):
        base = self.n
        with self.eng.Fori(0, trips) as i:
            self.n = base + i * per
            yield i
        self.n = base + trips * per


def split_matmuls(pe, ps, wh, wl, xh, xl, kt, n):
    mm = None
    for b, c0, w in pieces(n):
        o = ps[:, 512 * b:512 * b + w]
        for k in range(kt):
            terms = ((wh, xh), (wl, xh), (wh, xl))
            for t, (a, x) in enumerate(terms):
                mm = pe.matmul(o, a[:, k * P:(k + 1) * P], x[:, k, c0:c0 + w],
                               start=(k == 0 and t == 0), stop=(k == kt - 1 and t == 2))
    return mm


def dense(nc, name, weights, mt, kt, x, n, epi, sides=(), side_at=None, store=None, extra=None, steps=(0, 0),
          off=0, stage=None, warm=False, following=None):
    assert mt % 2 == 0
    weights = weights[off:off + mt]
    with Phase(nc, name) as ph:
        places = stage or [ph.sb(f"wstage{j}", (P, kt * P)) for j in range(2)]
        stage = [s[:, 0:kt * P] for s in places]
        early = 16 if warm else 0
        wh = [ph.sb(f"whigh{j}", (P, kt * P), F32R) for j in range(2)]
        wl = [ph.sb(f"wlow{j}", (P, kt * P), F32R) for j in range(2)]
        side = [[ph.sb(f"side{s}_{j}", (P, n)) for j in range(2)] for s in range(len(sides))]
        out = [ph.sb(f"out{j}", (P, n)) for j in range(2)]
        ps = [ph.ps(f"psum{j}", (P, 1536)) for j in range(2)]
        w_landed = [ph.sem(f"weights_landed{j}") for j in range(2)]
        side_landed = [[ph.sem(f"side{s}_landed{j}") for j in range(2)] for s in range(len(sides))]
        out_stored = [ph.sem(f"out_stored{j}") for j in range(2)]
        high_ready, low_ready = ph.sem("high_ready"), ph.sem("low_ready")
        psum_full, psum_free = ph.sem("psum_full"), ph.sem("psum_free")
        out_ready = ph.sem("out_ready")
        act_step, dve_step = ph.sem("act_step"), ph.sem("dve_step")

        class E:
            pass
        e = E()
        e.ph, e.side, e.out, e.ps, e.n = ph, side, out, ps, n
        e.psum_free, e.out_ready, e.act_step, e.dve_step = psum_free, out_ready, act_step, dve_step
        e.psum_full, e.side_landed = psum_full, side_landed
        act_epi, dve_epi = epi(e)
        half = mt // 2
        ns = len(sides)

        with nc.Block() as block:
            @block.sync
            def _(sp):
                def load(m, j, i):
                    sp.dma_start(stage[j], weights[m]).then_inc(w_landed[j], 16)

                def load_sides(m, j):
                    for s in range(ns):
                        sp.dma_start(side[s][j][:, :], side_at(s, sides[s], m)).then_inc(side_landed[s][j], 16)

                def put(m, j):
                    if store is not None:
                        sp.wait_ge(out_ready, m + 1)
                        sp.dma_start(store(m), out[j][:, :]).then_inc(out_stored[j], 16)

                for j in range(2):
                    if not warm:
                        load(j, j, 0)
                    load_sides(j, j)
                if half > 1:
                    with sp.Fori(0, half - 1) as i:
                        for j in range(2):
                            sp.wait_ge(low_ready, 2 * i + j + 1)
                            load(2 * i + j + 2, j, i)
                        for j in range(2 if ns or store is not None else 0):
                            sp.wait_ge(out_ready, 2 * i + j + 1)
                            put(2 * i + j, j)
                            load_sides(2 * i + j + 2, j)
                if following is not None:
                    for j in range(2):
                        sp.wait_ge(low_ready, mt - 1 + j)
                        k = following.shape[-1]
                        sp.dma_start(places[j][:, 0:k], following[j]).then_inc(w_landed[j], 16)
                for j in range(2):
                    put(mt - 2 + j, j)
                if following is not None:
                    for j in range(2):
                        sp.wait_ge(w_landed[j], 16 * (half + 1) - early)
                if store is not None:
                    for j in range(2):
                        sp.wait_ge(out_stored[j], 16 * half)

            @block.tensor
            def _(pe):
                with pe.Fori(0, half) as i:
                    for j in range(2):
                        pe.wait_ge(low_ready, 2 * i + j + 1)
                        pe.wait_ge(psum_free, 2 * i + j + 1)
                        split_matmuls(pe, ps[j], wh[j], wl[j], x[0], x[1], kt, n).then_inc(psum_full, 1)

            @block.scalar
            def _(act):
                ch = Chain(act, act_step)

                def high(m, j, i):
                    if not (warm and isinstance(i, int) and i == 0):
                        act.wait_ge(w_landed[j], 16 * (i + 1) - early)
                    act.activation(wh[j][:, :], stage[j], ACT.Copy).then_inc(high_ready, 1)

                def one(m, j, i):
                    act.wait_ge(psum_full, m + 1)
                    act_epi(act, m, j, i, ch)

                for j in range(2):
                    high(j, j, 0)
                if half > 1:
                    with ch.loop(half - 1, int(2 * steps[0])) as i:
                        for j in range(2):
                            one(2 * i + j, j, i)
                            high(2 * i + j + 2, j, i + 1)
                for j in range(2):
                    one(mt - 2 + j, j, half - 1)

            @block.vector
            def _(dve):
                ch = Chain(dve, dve_step)

                def low(m, j, i):
                    dve.wait_ge(high_ready, m + 1)
                    dve.tensor_tensor(wl[j][:, :], stage[j], wh[j][:, :].bitcast(F32),
                                      ALU.subtract).then_inc(low_ready, 1)

                def one(m, j, i):
                    dve.wait_ge(psum_full, m + 1)
                    if store is not None and i is not None:
                        dve.wait_ge(out_stored[j], 16 * i)
                    dve_epi(dve, m, j, i, ch)

                dve.sem_inc(psum_free, 2)
                for j in range(2):
                    low(j, j, 0)
                for j in range(2):
                    dve.wait_ge(psum_full, j + 1)
                    dve_epi(dve, j, j, 0, ch)
                    if half > 1:
                        low(j + 2, j, 1)
                if half > 2:
                    base = ch.n
                    with dve.Fori(1, half - 1) as i:
                        ch.n = base + (i - 1) * int(2 * steps[1])
                        for j in range(2):
                            one(2 * i + j, j, i)
                            low(2 * i + j + 2, j, i + 1)
                    ch.n = base + (half - 2) * int(2 * steps[1])
                if half > 1:
                    for j in range(2):
                        one(mt - 2 + j, j, half - 1)

            if extra is not None:
                extra(block, e)


def split(dve, ch, hi, lo, v):
    ch.do(dve.tensor_scalar(hi, v, 1.0, None, ALU.mult))
    return dve.tensor_tensor(lo, v, hi.bitcast(F32), ALU.subtract)


def inverse_rms(nc, name, acc, out, rows, c, n):
    with Phase(nc, name) as ph:
        ps = ph.ps("sum", (P, 1536))
        summed, rooted = ph.sem("summed"), ph.sem("rooted")
        with nc.Block() as block:
            @block.tensor
            def _(pe):
                for b, c0, w in pieces(n):
                    mm = pe.matmul(ps[:, 512 * b:512 * b + w], c["ones"][:, :], acc[:, c0:c0 + w],
                                   start=True, stop=True)
                mm.then_inc(summed, 1)

            @block.scalar
            def _(act):
                act.wait_ge(summed, 1)
                inverse_root(act, sview(out[:, :], n), pview(ps, n), c["eps"][:, 0:1], 1.0 / rows, rooted)


def inverse_root(act, out, mean_square, eps, scale, sem, n=0):
    act.activation(out, mean_square, ACT.Ln, bias=eps, scale=scale).then_inc(sem, 1)
    act.wait_ge(sem, n + 1)
    act.activation(out, out, ACT.Exp, scale=-0.5).then_inc(sem, 1)


def prepare_input(nc, c, x_in, x, acc):
    with Phase(nc, "pre") as ph:
        t = [ph.sb(f"t{j}", (P, T1)) for j in range(2)]
        s = [ph.sb(f"s{j}", (P, T1)) for j in range(2)]
        v = ph.sb("v", (P, T1))
        landed = [ph.sem(f"landed{j}") for j in range(2)]
        squared, used, step = ph.sem("squared"), ph.sem("used"), ph.sem("step")
        with nc.Block() as block:
            @block.sync
            def _(sp):
                for m in range(DT):
                    if m >= 2:
                        sp.wait_ge(used, m - 1)
                    sp.dma_start(t[m % 2][:, :], x_in[m]).then_inc(landed[m % 2], 16)

            @block.scalar
            def _(act):
                for m in range(DT):
                    act.wait_ge(landed[m % 2], 16 * (m // 2 + 1))
                    if m >= 2:
                        act.wait_ge(used, m - 1)
                    act.activation(s[m % 2][:, :], t[m % 2][:, :], ACT.Square).then_inc(squared, 1)

            @block.vector
            def _(dve):
                ch = Chain(dve, step)
                for m in range(DT):
                    dve.wait_ge(landed[m % 2], 16 * (m // 2 + 1))
                    ch.do(dve.tensor_scalar(v[:, :], t[m % 2][:, :], c["mix_g"][:, m:m + 1], None, ALU.mult))
                    ch.do(split(dve, ch, x[0][:, m, :], x[1][:, m, :], v[:, :]))
                    dve.wait_ge(squared, m + 1)
                    if m == 0:
                        ins = dve.tensor_copy(acc[:, :], s[0][:, :])
                    else:
                        ins = dve.tensor_tensor(acc[:, :], acc[:, :], s[m % 2][:, :], ALU.add)
                    ins.then_inc(used, 1)
                    dve.wait_ge(used, m + 1)


def epi_scale_store(scale):
    def epi(e):
        def act(eng, m, j, i, ch):
            pass

        def dve(eng, m, j, i, ch):
            o = sview(e.out[j][:, :], e.n)
            if scale is None:
                ins = eng.tensor_copy(o, pview(e.ps[j], e.n))
            else:
                ins = eng.tensor_tensor(o, pview(e.ps[j], e.n), sview(scale[:, :], e.n), ALU.mult)
            ch.do(ins)
            eng.sem_inc(e.psum_free, 1)
            eng.sem_inc(e.out_ready, 1)
        return act, dve
    return epi, (0, 1)


def epi_gate(add):
    def epi(e):
        gate = [e.ph.sb(f"gate{j}", (P, e.n)) for j in range(2)]
        gate_ready = e.ph.sem("gate_ready")

        def act(eng, m, j, i, ch):
            eng.wait_ge(e.side_landed[0][j], 16 * (i + 1))
            eng.activation(gate[j][:, :], e.side[0][j][:, :], ACT.Sigmoid).then_inc(gate_ready, 1)

        def dve(eng, m, j, i, ch):
            eng.wait_ge(gate_ready, m + 1)
            ch.do(eng.tensor_tensor(sview(e.out[j][:, :], e.n), pview(e.ps[j], e.n),
                                    sview(gate[j][:, :], e.n), ALU.mult))
            eng.sem_inc(e.psum_free, 1)
            if add is None:
                eng.sem_inc(e.out_ready, 1)
                return
            eng.wait_ge(e.side_landed[1][j], 16 * (i + 1))
            ch.do(eng.tensor_tensor(e.out[j][:, :], e.out[j][:, :], e.side[1][j][:, :], ALU.add))
            ch.do(split(eng, ch, add[0][:, m, :], add[1][:, m, :], e.out[j][:, :]))
            eng.sem_inc(e.out_ready, 1)
        return act, dve
    return epi, ((0, 1) if add is None else (0, 4))


def epi_glu(x):
    def epi(e):
        gate = [e.ph.sb(f"gate{j}", (P, e.n)) for j in range(2)]
        gate_ready = e.ph.sem("gate_ready")

        def act(eng, m, j, i, ch):
            eng.activation(sview(gate[j][:, :], e.n), pview(e.ps[j], e.n), ACT.Sigmoid).then_inc(gate_ready, 1)

        def dve(eng, m, j, i, ch):
            eng.wait_ge(gate_ready, m + 1)
            eng.sem_inc(e.psum_free, 1)
            eng.wait_ge(e.side_landed[0][j], 16 * (i + 1))
            ch.do(eng.tensor_tensor(gate[j][:, :], e.side[0][j][:, :], gate[j][:, :], ALU.mult))
            ch.do(split(eng, ch, x[0][:, m, :], x[1][:, m, :], gate[j][:, :]))
            eng.sem_inc(e.out_ready, 1)
        return act, dve
    return epi, (0, 3)


def epi_residual_norm(x, g, acc):
    def epi(e):
        sq = [e.ph.sb(f"sq{j}", (P, e.n)) for j in range(2)]
        v = e.ph.sb("v", (P, e.n))
        sum_ready, squared = e.ph.sem("sum_ready"), e.ph.sem("squared")

        def act(eng, m, j, i, ch):
            eng.wait_ge(sum_ready, m + 1)
            eng.activation(sq[j][:, :], e.out[j][:, :], ACT.Square).then_inc(squared, 1)

        def dve(eng, m, j, i, ch):
            eng.wait_ge(e.side_landed[0][j], 16 * (i + 1))
            ch.do(eng.tensor_tensor(sview(e.out[j][:, :], e.n), pview(e.ps[j], e.n),
                                    sview(e.side[0][j][:, :], e.n), ALU.add))
            eng.sem_inc(e.psum_free, 1)
            eng.sem_inc(sum_ready, 1)
            if x is not None:
                ch.do(eng.tensor_scalar(v[:, :], e.out[j][:, :], g[:, bass.ds(m, 1)], None, ALU.mult))
                ch.do(split(eng, ch, x[0][:, m, :], x[1][:, m, :], v[:, :]))
            eng.wait_ge(squared, m + 1)
            if isinstance(m, int) and m == 0:
                ch.do(eng.tensor_copy(acc[:, :], sq[j][:, :]))
            else:
                ch.do(eng.tensor_tensor(acc[:, :], acc[:, :], sq[j][:, :], ALU.add))
            eng.sem_inc(e.out_ready, 1)
        return act, dve
    return epi, (0, 5 if x is not None else 2)


class Order:

    def __init__(self, *names):
        self.names = names

    def at(self, i, name):
        return i * len(self.names) + self.names.index(name) + 1


def hgrn(nc, c, t, pin, x, mod):
    MT = 6 * DT
    MS, MB = MT // HH, 4
    CP = NC - 1
    MID = CH // 2 - 1
    VF = Order("decay", "key", "cum", "centred", "g_a", "g_b", "q_in", "k_in", "k_out")
    VB = Order("masked", "mask_tail", "k_rows", "scaled", "gated", "high", "low")
    AF = Order("sigmoid", "log", "grow", "shrink", "g", "v_rows")
    AB = Order("k_rows", "silu", "square", "raw", "log_square", "root")
    PF = Order("v_turned", "scores")
    PB = Order("k_turned", "out", "norm")
    with Phase(nc, "hgrn") as ph:
        def w(name, n=T1):
            return ph.sb(name, (P, n))
        q, f, v, og = w("q"), w("f"), w("v"), w("og")
        fp, k, sums, so = w("fp"), w("k"), w("sums"), w("so")
        e1, e2, ki, ko = w("e1"), w("e2"), w("ki"), w("ko")
        qi, gg = [w(f"qi{j}") for j in range(2)], [w(f"gg{j}", NC) for j in range(2)]
        raw, square, root = w("raw"), w("square"), w("root")
        gx, warm = w("gx", NC), w("warm", 1)
        cond, mb, mw = ph.sb("cond", (P, DT, 2)), w("mod_bias", MT), [w(f"mod_w{j}", DT * P) for j in range(MB)]
        vt = ph.sb("vt", (P, 9, P))
        kt = ph.sb("kt", (P, 8, 4, P))
        st = ph.sb("st", (P, 9, P))
        S = ph.sb("S", (P, NC, P))
        pa = ph.ps("turned_and_kv", (P, 4, 512))
        po = ph.ps("scores_and_out", (P, 1536))
        pm = ph.ps("modulations", (P, 512))
        flat = pa[:, :, :].rearrange("p b x -> p (b x)")
        sum3, k3 = (a[:, :].rearrange("p (c t) -> p c t", t=CH) for a in (sums, ki))
        ko3 = ko[:, :].rearrange("p (c t) -> p c t", t=CH)
        landed = {n: ph.sem(f"{n}_landed") for n in "qfvo"}
        vf, vb = ph.sem("vector_front"), ph.sem("vector_back")
        af, ab = ph.sem("scalar_front"), ph.sem("scalar_back")
        pf, pb = ph.sem("tensor_front"), ph.sem("tensor_back")
        kv_full, kv_used, zeroed = ph.sem("kv_full"), ph.sem("kv_used"), ph.sem("zeroed")
        cond_in, cond_ready, mod_step = ph.sem("cond_in"), ph.sem("cond_ready"), ph.sem("mod_step")
        mod_in, mod_used = [ph.sem(f"mod_w_in{j}") for j in range(MB)], ph.sem("mod_w_used")

        def steps(eng, step):
            with eng.Fori(0, HH // 2 - 1) as i:
                step(2 * i, 0, False)
                step(2 * i + 1, 1, False)
            step(HH - 2, 0, False)
            step(HH - 1, 1, True)

        with nc.Block() as block:
            @block.sync
            def _(sp):
                def load(n, buf, sec, h):
                    sp.dma_start(buf[:, :], pin[h + sec * DT]).then_inc(landed[n], 16)
                def tile(n, j):
                    sp.dma_start(mw[j][:, :], t["w_mod"][n]).then_inc(mod_in[j], 16)

                def tiles(n, first, count):
                    for u in range(first, first + count):
                        sp.wait_ge(mod_used, n + u - MB + 1)
                        tile(n + u, u % MB)

                def f_next(h):
                    sp.wait_ge(vf, VF.at(h, "cum"))
                    load("f", f, 2, h + 1)

                def q_v_next(h):
                    sp.wait_ge(vf, VF.at(h, "q_in"))
                    load("q", q, 1, h + 1)
                    sp.wait_ge(pf, PF.at(h, "v_turned"))
                    load("v", v, 3, h + 1)

                def o_next(h):
                    sp.wait_ge(ab, AB.at(h, "silu"))
                    load("o", og, 4, h + 1)
                load("f", f, 2, 0)
                load("q", q, 1, 0)
                load("v", v, 3, 0)
                load("o", og, 4, 0)
                sp.dma_start(cond[:, :, :], t["cond"]).then_inc(cond_in, 16)
                sp.dma_start(mb[:, :], t["b_mod"]).then_inc(cond_in, 16)
                for u in range(MB):
                    tile(u, u)
                f_next(0)
                q_v_next(0)
                with sp.Fori(0, HH // 2 - 1) as i:
                    for j in range(2):
                        h = 2 * i + j
                        tiles(2 * MS * i, MS * j + MB, 2)
                        o_next(h)
                        f_next(h + 1)
                        tiles(2 * MS * i, MS * j + MB + 2, MS - 2)
                        q_v_next(h + 1)
                tiles(MS * (HH - 2), MB, 2)
                o_next(HH - 2)
                tiles(MS * (HH - 2), MB + 2, 2 * MS - MB - 2)

            @block.scalar
            def _(act):
                def gate(h):
                    act.wait_ge(landed["f"], 16 * (h + 1))
                    act.activation(f[:, :], f[:, :], ACT.Sigmoid).then_inc(af, 1)

                def log(h):
                    act.wait_ge(vf, VF.at(h, "decay"))
                    act.activation(f[:, :], fp[:, :], ACT.Ln).then_inc(af, 1)

                def exponentials(h, j):
                    act.wait_ge(vf, VF.at(h, "g_b"))
                    act.activation(e1[:, :], fp[:, :], ACT.Exp).then_inc(af, 1)
                    act.activation(e2[:, :], fp[:, :], ACT.Exp, scale=-1.0).then_inc(af, 1)
                    act.activation(gg[j][:, 0:CP], gx[:, 0:CP], ACT.Exp).then_inc(af, 1)

                def v_rows(h):
                    act.wait_ge(pf, PF.at(h, "v_turned"))
                    act.activation(vt[:, 0:8, :].rearrange("p b x -> p (b x)"), flat[:, 0:1024], ACT.Copy)
                    act.activation(vt[0:CH, 8, :], flat[0:CH, 1024:1152], ACT.Copy).then_inc(af, 1)

                def k_rows(h):
                    act.wait_ge(pb, PB.at(h, "k_turned"))
                    for u in range(2):
                        r = CH * u
                        ins = act.activation(kt[r:r + CH, :, u, :],
                                             flat[r:r + CH, 0:1024].rearrange("p (b x) -> p b x", x=P), ACT.Copy)
                    ins.then_inc(ab, 1)

                def step(h, j, last):
                    if not last:
                        gate(h + 1)
                    k_rows(h)
                    if not last:
                        log(h + 1)
                    act.wait_ge(landed["o"], 16 * (h + 1))
                    act.wait_ge(vb, VB.at(h, "mask_tail"))
                    act.activation(so[:, :], og[:, :], ACT.Silu).then_inc(ab, 1)
                    act.activation(warm[:, :], c["eps"][:, :], ACT.Exp)
                    act.wait_ge(pb, PB.at(h, "out"))
                    act.activation(square[:, :], po[:, 0:T1], ACT.Square).then_inc(ab, 1)
                    act.activation(raw[:, :], po[:, 0:T1], ACT.Copy).then_inc(ab, 1)
                    if not last:
                        exponentials(h + 1, 1 - j)
                    act.wait_ge(pb, PB.at(h, "norm"))
                    inverse_root(act, sview(root[:, :], T1), pview(po, T1), c["eps"][:, 0:1], 1.0 / P,
                                 ab, AB.at(h, "raw"))
                    if not last:
                        v_rows(h + 1)
                act.wait_ge(cond_in, 32)
                act.activation(cond[:, :, :], cond[:, :, :], ACT.Silu).then_inc(cond_ready, 1)
                gate(0)
                log(0)
                exponentials(0, 0)
                v_rows(0)
                steps(act, step)

            @block.tensor
            def _(pe):
                def turn_v(h):
                    pe.wait_ge(landed["v"], 16 * (h + 1))
                    for b in range(9):
                        n = min(P, T1 - b * P)
                        mm = pe.transpose(flat[0:n, b * P:(b + 1) * P], v[:, b * P:b * P + n], c["ident"][:, :])
                    mm.then_inc(pf, 1)

                def scores(h, j):
                    pe.wait_ge(vf, VF.at(h, "k_in"))
                    for b in range(9):
                        n = min(P, T1 - b * P)
                        mm = pe.matmul(po[0:n, b * P:b * P + n], ki[:, b * P:b * P + n], qi[j][:, b * P:b * P + n],
                                       start=True, stop=True)
                    mm.then_inc(pf, 1)

                def modulations(h, j, place):
                    for u in range(2):
                        n = MS * h + 2 * place + u
                        k = MS * j + 2 * place + u
                        pe.wait_ge(mod_in[k % MB], (h - j) * (8 * 2 * MS // MB) + 16 * (k // MB + 1))
                        for kt_ in range(DT):
                            mm = pe.matmul(pm[:, bass.ds(2 * n, 2)], mw[k % MB][:, kt_ * P:(kt_ + 1) * P], cond[:, kt_, :],
                                           start=kt_ == 0, stop=kt_ == DT - 1)
                        mm.then_inc(mod_used, 1)

                def step(h, j, last):
                    pe.wait_ge(vf, VF.at(h, "k_out"))
                    pe.wait_ge(af, AF.at(h, "v_rows"))
                    for b in range(8):
                        mm = pe.transpose(flat[:, b * P:(b + 1) * P], ko[:, b * P:(b + 1) * P], c["ident"][:, :])
                    mm.then_inc(pb, 1)
                    modulations(h, j, 0)
                    pe.wait_ge(ab, AB.at(h, "k_rows"))
                    pe.wait_ge(vb, VB.at(h, "k_rows"))
                    for i in range(CP // 4):
                        if i >= 4:
                            pe.wait_ge(kv_used, h * CP + 4 * (i - 3))
                        for u in range(4):
                            mm = pe.matmul(pa[:, i % 4, P * u:P * (u + 1)], kt[:, i, u, :], vt[:, i, :],
                                           start=True, stop=True)
                        mm.then_inc(kv_full, 1)
                    pe.wait_ge(vb, VB.at(h, "mask_tail"))
                    for i in range(NC):
                        b, u = divmod(i, 4)
                        n = min(P, T1 - b * P)
                        if u == 0:
                            mm = pe.matmul(po[:, b * P:b * P + n], vt[0:n, b, :], st[0:n, b, 0:n],
                                           start=True, stop=True, skip_group_check=True)
                        if i == 0:
                            continue
                        pe.wait_ge(kv_used, h * CP + i)
                        mm = pe.matmul(po[:, CH * i:CH * (i + 1)], S[:, i, :], qi[j][:, CH * i:CH * (i + 1)],
                                       start=False, stop=True, skip_group_check=True)
                    mm.then_inc(pb, 1)
                    if not last:
                        turn_v(h + 1)
                    modulations(h, j, 1)
                    pe.wait_ge(ab, AB.at(h, "raw"))
                    for b, c0, n in pieces(T1):
                        mm = pe.matmul(po[:, 512 * b:512 * b + n], c["ones"][:, :], square[:, c0:c0 + n],
                                       start=True, stop=True)
                    mm.then_inc(pb, 1)
                    modulations(h, j, 2)
                    if not last:
                        pe.wait_ge(ab, AB.at(h, "log_square"))
                        scores(h + 1, 1 - j)
                turn_v(0)
                scores(0, 0)
                pe.wait_ge(cond_ready, 1)
                steps(pe, step)

            @block.vector
            def _(dve):
                def decay(h):
                    ch = Chain(dve, vf, h * len(VF.names))
                    dve.wait_ge(af, AF.at(h, "sigmoid"))
                    ch.do(dve.tensor_scalar(fp[:, :], f[:, :], c["one_minus_lb"][:, bass.ds(h, 1)],
                                            c["lb"][:, bass.ds(h, 1)], ALU.mult, ALU.add))
                    ch.do(dve.tensor_scalar(k[:, :], fp[:, :], -1.0, 1.0, ALU.mult, ALU.add))
                    return ch

                def sums_of(h, ch):
                    dve.wait_ge(af, AF.at(h, "log"))
                    ch.do(dve.tensor_tensor_scan(sums[:, :], c["chunk_mask"][:, :], f[:, :], 0.0,
                                                 ALU.mult, ALU.add))
                    ch.inc(dve.tensor_tensor(fp[:, :].rearrange("p (c t) -> p c t", t=CH), sum3,
                                             sum3[:, :, MID:MID + 1].broadcast_to([P, NC, CH]), ALU.subtract))
                    ch.do(dve.tensor_tensor(gx[:, 0:CP], sum3[:, 0:CP, CH - 1], sum3[:, 0:CP, MID], ALU.subtract))
                    ch.do(dve.tensor_tensor(gx[:, 0:CP], gx[:, 0:CP], sum3[:, 1:NC, MID], ALU.add))

                def operands(h, j, ch, prev):
                    dve.wait_ge(landed["q"], 16 * (h + 1))
                    dve.wait_ge(af, AF.at(h, "grow"))
                    ch.inc(dve.tensor_tensor(qi[j][:, :], q[:, :], e1[:, :], ALU.mult))
                    dve.wait_ge(af, AF.at(h, "g"))
                    ch.do(dve.tensor_tensor(ki[:, :], k[:, :], e2[:, :], ALU.mult))
                    if prev is not None:
                        dve.wait_ge(pb, PB.at(prev, "k_turned"))
                    ch.do(dve.tensor_tensor(ko3[:, 0:CP, :], k3[:, 0:CP, :],
                                            gg[j][:, 0:CP].unsqueeze(2).broadcast_to([P, CP, CH]), ALU.mult))

                def step(h, j, last):
                    back = Chain(dve, vb, h * len(VB.names))
                    dve.wait_ge(pf, PF.at(h, "scores"))
                    dve.sem_inc(zeroed, 1)
                    back.inc(dve.copy_predicated(st[:, 0:8, :], c["causal"][:, 0:8, :].bitcast(mybir.dt.int32),
                                                 po[:, 0:1024].rearrange("p (b t) -> p b t", t=P)))
                    back.do(dve.copy_predicated(st[0:CH, 8, 0:CH], c["causal"][0:CH, 8, 0:CH].bitcast(mybir.dt.int32),
                                                po[0:CH, 1024:T1]))
                    dve.wait_ge(pb, PB.at(h, "k_turned"))
                    for u in range(2, 4):
                        r = CH * u
                        ins = dve.tensor_copy(kt[r:r + CH, :, u, :],
                                              flat[r:r + CH, 0:1024].rearrange("p (b x) -> p b x", x=P))
                    back.inc(ins)
                    if not last:
                        front = decay(h + 1)
                    for i in range(CP):
                        if i % 4 == 0:
                            dve.wait_ge(kv_full, h * (CP // 4) + i // 4 + 1)
                        dve.scalar_tensor_tensor(
                            out=S[:, i + 1, :], in0=S[:, i, :], scalar=gg[j][:, i:i + 1],
                            in1=pa[:, i // 4 % 4, P * (i % 4):P * (i % 4 + 1)],
                            op0=ALU.mult, op1=ALU.add).then_inc(kv_used, 1)
                        dve.wait_ge(kv_used, h * CP + i + 1)
                    if not last:
                        sums_of(h + 1, front)
                        operands(h + 1, 1 - j, front, h)
                    dve.wait_ge(ab, AB.at(h, "root"))
                    back.do(dve.scalar_tensor_tensor(out=raw[:, :], in0=raw[:, :], scalar=c["hgrn_g"][:, 0:1],
                                                     in1=root[:, :], op0=ALU.mult, op1=ALU.mult))
                    back.do(dve.tensor_tensor(raw[:, :], raw[:, :], so[:, :], ALU.mult))
                    back.do(split(dve, back, x[0][:, h, :], x[1][:, h, :], raw[:, :]))
                dve.memset(S[:, 0, :], 0.0).then_inc(zeroed, 1)
                dve.memset(st[:, :, :], 0.0).then_inc(zeroed, 1)
                dve.memset(kt[:, :, :, :], 0.0).then_inc(zeroed, 1)
                dve.wait_ge(zeroed, 3)
                front = decay(0)
                sums_of(0, front)
                operands(0, 0, front, None)
                steps(dve, step)
                dve.wait_ge(mod_used, MT)
                ch = Chain(dve, mod_step)
                ch.do(dve.tensor_tensor(mod[:, :, :], pm[:, 0:2 * MT].rearrange("p (m s) -> p m s", s=2),
                                        mb[:, :].unsqueeze(2).broadcast_to([P, MT, 2]), ALU.add))
                for m in (DT, 4 * DT):
                    ch.do(dve.tensor_scalar(mod[:, m:m + DT, :], mod[:, m:m + DT, :], 1.0, None, ALU.add))


def split_y(nc, yc, yt, x):
    with Phase(nc, "split_y") as ph:
        a = [ph.sb(f"a{j}", (P, T1)) for j in range(2)]
        b = [ph.sb(f"b{j}", (P, T1)) for j in range(2)]
        landed = [ph.sem(f"landed{j}") for j in range(2)]
        stored = [ph.sem(f"stored{j}") for j in range(2)]
        moved, moved_high, step = ph.sem("moved"), ph.sem("moved_high"), ph.sem("step")
        with nc.Block() as block:
            @block.sync
            def _(sp):
                for m in range(DT):
                    if m >= 2:
                        sp.wait_ge(moved, m - 1)
                    sp.dma_start(a[m % 2][:, :], yc[m]).then_inc(landed[m % 2], 16)
                    if m >= 1:
                        sp.wait_ge(moved, m)
                        sp.dma_start(yt[m - 1], b[(m - 1) % 2][:, :]).then_inc(stored[(m - 1) % 2], 16)
                sp.wait_ge(moved, DT)
                sp.dma_start(yt[DT - 1], b[(DT - 1) % 2][:, :]).then_inc(stored[(DT - 1) % 2], 16)
                for j in range(2):
                    sp.wait_ge(stored[j], 16 * DT // 2)

            @block.scalar
            def _(act):
                for m in range(DT):
                    act.wait_ge(landed[m % 2], 16 * (m // 2 + 1))
                    if m >= 2:
                        act.wait_ge(stored[m % 2], 16 * (m // 2))
                        act.wait_ge(step, m - 1)
                    act.activation(b[m % 2][:, :].rearrange("p (c t) -> p c t", t=TAU),
                                   a[m % 2][:, :].rearrange("p (t c) -> p c t", t=TAU), ACT.Copy).then_inc(moved, 1)
                    act.wait_ge(moved, m + 1)
                    act.activation(x[0][:, m, :], b[m % 2][:, :], ACT.Copy).then_inc(moved_high, 1)

            @block.vector
            def _(dve):
                for m in range(DT):
                    dve.wait_ge(moved_high, m + 1)
                    dve.tensor_tensor(x[1][:, m, :], b[m % 2][:, :], x[0][:, m, :].bitcast(F32),
                                      ALU.subtract).then_inc(step, 1)


def s5(nc, c, t, pin, up, yc):
    NP, NQ = NPAIR, 8
    with Phase(nc, "s5") as outer:
        ca = [outer.sb(n, (P, NP, TAU + 1, SG)) for n in ("ca_re", "ca_im")]
        win = outer.sb("win", (P, 2, NP, P))
        toep = outer.sb("toeplitz", (P, 2, NP, P))
        m8 = outer.sb("m8", (P, NP))
        rot = outer.sb("rot", (P, 2, NP))
        U = outer.sb("u", (P, G, NCH))
        urow = up.rearrange("m p x -> (m p) x").rearrange("(g h) (t c) -> t h g c", h=SG, t=TAU)
        with Phase(nc, "s5w") as ph:
            def small(n, k=1):
                return ph.sb(n, (P, NP * k))
            lr, li, dt = small("lr"), small("li"), small("dt")
            br, bi, cr, ci = (ph.sb(n, (P, NP, SG)) for n in ("br", "bi", "cr", "ci"))
            th, kk, r, ab, co, si, mag = (small(n) for n in ("th", "kk", "r", "ab", "co", "si", "mag"))
            x1, x2, x3, x4 = (small(n) for n in ("x1", "x2", "x3", "x4"))
            pw = ph.sb("powers", (P, 2, TAU + 1, NP))
            bb = [ph.sb(n, (P, NP, 5 * SG)) for n in ("bb_re", "bb_im")]
            b_re, b_im = (ph.sb(n, (P, NP, SG)) for n in ("scaled_b_re", "scaled_b_im"))
            wt = [U[:, :, :].rearrange("p g c -> p (g c)")[:, NP * P * q:NP * P * (q + 1)].rearrange(
                "p (n k h) -> p n k h", n=NP, k=TAU) for q in range(2)]
            before, after = ([toep[:, q, :, :].rearrange("p a b -> p (a b)")[:, T1 * k:T1 * (k + 1)]
                              for k in range(2)] for q in range(2))
            t1, t2 = (ph.sb(n, (P, NP, SG)) for n in ("t1", "t2"))
            skip, skip_diag = ph.sb("skip", (SS, NP)), ph.sb("skip_diag", (SS, NP, 2 * SG))
            pst = ph.ps("turn", (P, 4, 512))
            psk = ph.ps("kernel", (P, 4, 512))
            landed, step, sc = ph.sem("landed"), ph.sem("vector_step"), ph.sem("scalar_step")
            zeroed, w_ready, ker_ready = ph.sem("zeroed"), ph.sem("w_ready"), ph.sem("kernel_ready")
            turned, turned_out = ph.sem("turned"), ph.sem("turned_out")
            made, made_even, made_odd = ph.sem("made"), ph.sem("made_even_out"), ph.sem("made_odd_out")
            in_ = [ph.sem(f"u_tile_in{k}") for k in range(2)]
            out_ = [ph.sem(f"u_tile_stored{k}") for k in range(2)]
            moved, b_ready, spread, u_in = ph.sem("moved"), ph.sem("b_ready"), ph.sem("b_spread"), ph.sem("u_in")
            loads = ((lr, "lam_re"), (li, "lam_im"), (dt, "log_dt"), (br, "b_re"), (bi, "b_im"), (cr, "c_re"),
                     (ci, "c_im"), (skip, "ssm_d"))
            with nc.Block() as block:
                @block.sync
                def _(sp):
                    for buf, n in loads:
                        sp.dma_start(buf[:], t[n]).then_inc(landed, 16)
                    for m in range(DT + 1):
                        if m < DT:
                            if m >= 2:
                                sp.wait_ge(moved, m - 1)
                            sp.dma_start(before[m % 2], pin[m]).then_inc(in_[m % 2], 16)
                        if m:
                            sp.wait_ge(moved, m)
                            sp.dma_start(up[m - 1], after[(m - 1) % 2]).then_inc(out_[(m - 1) % 2], 16)
                    for k in range(2):
                        sp.wait_ge(out_[k], 16 * DT // 2)
                    sp.wait_ge(turned, 16)
                    for k in range(TAU):
                        sp.dma_start(U[SG * k:SG * k + SG, :, :], urow[k]).then_inc(u_in, 16)
                    sp.wait_ge(u_in, 16 * TAU)

                @block.scalar
                def _(act):
                    act.wait_ge(landed, 16 * len(loads))
                    act.activation(dt[:, :], dt[:, :], ACT.Exp).then_inc(sc, 1)
                    act.wait_ge(step, 2)
                    act.activation(mag[:, :], x1[:, :], ACT.Exp).then_inc(sc, 1)
                    act.wait_ge(step, 11)
                    act.activation(si[:, :], r[:, :], ACT.Sin).then_inc(sc, 1)
                    act.activation(co[:, :], ab[:, :], ACT.Sin).then_inc(sc, 1)
                    for m in range(DT):
                        act.wait_ge(in_[m % 2], 16 * (m // 2 + 1))
                        if m >= 2:
                            act.wait_ge(out_[m % 2], 16 * (m // 2))
                        act.activation(after[m % 2].rearrange("p (t c) -> p c t", t=TAU),
                                       before[m % 2].rearrange("p (c t) -> p c t", t=TAU), ACT.Copy).then_inc(moved, 1)
                    act.wait_ge(b_ready, 1)
                    for b, v in zip(bb, (b_re, b_im)):
                        act.activation(b[0:SS, :, SG:2 * SG], v[0:SS, :, :], ACT.Copy).then_inc(spread, 1)
                        act.activation(b[SS:P, :, 3 * SG:4 * SG], v[SS:P, :, :], ACT.Copy).then_inc(spread, 1)
                    act.wait_ge(w_ready, 1)
                    for n in range(16):
                        act.wait_ge(turned, n + 1)
                        part, q = divmod(n, 8)
                        act.activation(win[:, part, 4 * q:4 * q + 4, :].rearrange("p a b -> p (a b)"),
                                       pst[:, n % 4, :], ACT.Copy).then_inc(turned_out, 1)
                    act.wait_ge(zeroed, 4)
                    for n in range(8):
                        act.wait_ge(made, n + 1)
                        for j in range(4):
                            ins = act.activation(toep[32 * j:32 * j + 32, 1, 4 * n:4 * n + 4, 32 * j:P],
                                                 psk[32:64, n % 4, :].rearrange("p (a b) -> p a b", b=P)[
                                                     :, :, 0:P - 32 * j], ACT.Copy)
                        ins.then_inc(made_odd, 1)

                @block.vector
                def _(dve):
                    ch = Chain(dve, step)
                    tt, ts = dve.tensor_tensor, dve.tensor_scalar
                    for b in bb:
                        dve.memset(b[:, :, :], 0.0).then_inc(zeroed, 1)
                    dve.wait_ge(zeroed, 2)
                    dve.wait_ge(sc, 1)
                    ch.do(tt(th[:, :], li[:, :], dt[:, :], ALU.mult))
                    ch.do(tt(x1[:, :], lr[:, :], dt[:, :], ALU.mult))
                    big = 1.5 * 2.0 ** 23
                    ch.do(ts(kk[:, :], th[:, :], float(1 / (2 * np.pi)), big, ALU.mult, ALU.add))
                    ch.do(ts(kk[:, :], kk[:, :], big, None, ALU.subtract))
                    src = th
                    for part in (6.28125, 0.0019350051879882812, 3.019915981956752e-07):
                        ch.do(dve.scalar_tensor_tensor(out=r[:, :], in0=kk[:, :], scalar=-part, in1=src[:, :],
                                                       op0=ALU.mult, op1=ALU.add))
                        src = r
                    ch.do(ts(r[:, :], r[:, :], 3.1415925, -3.1415925, ALU.min, ALU.max))
                    ch.do(ts(ab[:, :], r[:, :], -1.0, None, ALU.mult))
                    ch.do(tt(ab[:, :], r[:, :], ab[:, :], ALU.max))
                    ch.do(ts(ab[:, :], ab[:, :], -1.0, float(np.pi / 2), ALU.mult, ALU.add))
                    assert ch.n == 11
                    dve.wait_ge(sc, 4)
                    ch.inc(dve.memset(pw[:, 0, 0, :], 1.0))
                    ch.inc(dve.memset(pw[:, 1, 0, :], 0.0))
                    ch.inc(tt(pw[:, 0, 1, :], mag[:, :], co[:, :], ALU.mult))
                    ch.do(tt(pw[:, 1, 1, :], mag[:, :], si[:, :], ALU.mult))

                    def cmul(ore, oim, are, aim, bre, bim, u, v):
                        ch.inc(tt(u, are, bre, ALU.mult))
                        ch.do(tt(v, aim, bim, ALU.mult))
                        ch.do(tt(ore, u, v, ALU.subtract))
                        ch.inc(tt(u, are, bim, ALU.mult))
                        ch.do(tt(v, aim, bre, ALU.mult))
                        ch.do(tt(oim, u, v, ALU.add))

                    a1, b1 = pw[:, 0, 1, :], pw[:, 1, 1, :]
                    for j in range(2, TAU + 1):
                        cmul(pw[:, 0, j, :], pw[:, 1, j, :], pw[:, 0, j - 1, :], pw[:, 1, j - 1, :], a1, b1,
                             x1[:, :], x2[:, :])
                    cmul(rot[:, 0, :], rot[:, 1, :], co[:, :], si[:, :], co[:, :], si[:, :], x1[:, :], x2[:, :])
                    ch.do(tt(m8[:, :], mag[:, :], mag[:, :], ALU.mult))
                    for _ in range(2):
                        cmul(x3[:, :], x4[:, :], rot[:, 0, :], rot[:, 1, :], rot[:, 0, :], rot[:, 1, :],
                             x1[:, :], x2[:, :])
                        ch.inc(dve.tensor_copy(rot[:, 0, :], x3[:, :]))
                        ch.inc(dve.tensor_copy(rot[:, 1, :], x4[:, :]))
                        ch.do(tt(m8[:, :], m8[:, :], m8[:, :], ALU.mult))
                    ch.inc(tt(x1[:, :], lr[:, :], lr[:, :], ALU.mult))
                    ch.do(tt(x2[:, :], li[:, :], li[:, :], ALU.mult))
                    ch.do(tt(x1[:, :], x1[:, :], x2[:, :], ALU.add))
                    ch.do(dve.reciprocal(r[:, :], x1[:, :]))
                    ch.inc(ts(kk[:, :], a1, -1.0, None, ALU.add))
                    ch.do(tt(x2[:, :], b1, li[:, :], ALU.mult))
                    ch.do(tt(x1[:, :], kk[:, :], lr[:, :], ALU.mult))
                    ch.do(tt(x1[:, :], x1[:, :], x2[:, :], ALU.add))
                    ch.do(tt(x3[:, :], x1[:, :], r[:, :], ALU.mult))
                    ch.inc(tt(x1[:, :], b1, lr[:, :], ALU.mult))
                    ch.do(tt(x2[:, :], kk[:, :], li[:, :], ALU.mult))
                    ch.do(tt(x1[:, :], x1[:, :], x2[:, :], ALU.subtract))
                    ch.do(tt(x4[:, :], x1[:, :], r[:, :], ALU.mult))
                    wide = lambda v, n: v.unsqueeze(2).broadcast_to([P, NP, n])
                    bre, bim = b_re[:, :, :], b_im[:, :, :]
                    cmul(bre, bim, wide(x3[:, :], SG), wide(x4[:, :], SG), br[:, :, :], bi[:, :, :],
                         t1[:, :, :], t2[:, :, :])
                    dve.sem_inc(b_ready, 1)
                    for k in range(TAU):
                        cmul(wt[0][:, :, k, :], wt[1][:, :, k, :], wide(pw[:, 0, TAU - 1 - k, :], SG),
                             wide(pw[:, 1, TAU - 1 - k, :], SG), bre, bim, t1[:, :, :], t2[:, :, :])
                    dve.sem_inc(w_ready, 1)
                    ch.do(ts(pw[:, 1, :, :], pw[:, 1, :, :], -1.0, None, ALU.mult))
                    for k in range(TAU + 1):
                        re, im = wide(pw[:, 0, k, :], SG), wide(pw[:, 1, k, :], SG)
                        ch.inc(tt(t1[:, :, :], re, cr[:, :, :], ALU.mult))
                        ch.do(tt(t2[:, :, :], im, ci[:, :, :], ALU.mult))
                        ch.do(tt(ca[0][:, :, k, :], t1[:, :, :], t2[:, :, :], ALU.add))
                        ch.inc(tt(t1[:, :, :], im, cr[:, :, :], ALU.mult))
                        ch.do(tt(t2[:, :, :], re, ci[:, :, :], ALU.mult))
                        ch.do(tt(ca[1][:, :, k, :], t1[:, :, :], t2[:, :, :], ALU.subtract))
                    for q in range(2):
                        rows_ = slice(32 * q, 32 * q + 32)
                        ch.do(tt(skip_diag[rows_, :, :], c["ident"][rows_, rows_].unsqueeze(1).broadcast_to([32, NP, 32]),
                                 skip[rows_, :].unsqueeze(2).broadcast_to([32, NP, 32]), ALU.mult))
                    dve.sem_inc(ker_ready, 1)
                    for k in range(2):
                        dve.wait_ge(out_[k], 16 * DT // 2)
                    dve.memset(toep[:, :, :, :], 0.0).then_inc(zeroed, 1)
                    dve.wait_ge(zeroed, 3)
                    dve.sem_inc(zeroed, 1)
                    for n in range(8):
                        dve.wait_ge(made, n + 1)
                        for j in range(4):
                            ins = dve.tensor_copy(
                                toep[32 * j:32 * j + 32, 0, 4 * n:4 * n + 4, 32 * j:P],
                                psk[0:32, n % 4, :].rearrange("p (a b) -> p a b", b=P)[:, :, 0:P - 32 * j])
                        ins.then_inc(made_even, 1)

                @block.tensor
                def _(pe):
                    pe.wait_ge(w_ready, 1)
                    for n in range(16):
                        part, q = divmod(n, 8)
                        if n >= 4:
                            pe.wait_ge(turned_out, n - 3)
                        for u in range(4):
                            mm = pe.transpose(pst[:, n % 4, P * u:P * u + P],
                                              wt[part][:, 4 * q + u, :, :].rearrange("p a b -> p (a b)"),
                                              c["ident"][:, :])
                        mm.then_inc(turned, 1)
                    pe.wait_ge(ker_ready, 1)
                    pe.wait_ge(spread, 4)
                    for n in range(8):
                        if n >= 4:
                            pe.wait_ge(made_even, n - 3)
                            pe.wait_ge(made_odd, n - 3)
                        for u in range(4):
                            pair = 4 * n + u
                            o = psk[0:SS, n % 4, P * u:P * u + P]
                            for part in range(2):
                                b = bb[part][:, pair, :]
                                a = ca[part][:, pair, :, :].rearrange("p a b -> p (a b)")
                                pe.matmul(o, b[:, SG:5 * SG], a[:, 0:P], start=part == 0, stop=False,
                                          skip_group_check=True)
                                pe.matmul(o[:, SG:P], b[:, 0:4 * SG], a[:, 0:P - SG], start=False, stop=False,
                                          skip_group_check=True)
                            mm = pe.matmul(o[:, 0:2 * SG], c["ident"][0:SS, 0:SS], skip_diag[:, pair, :], start=False,
                                           stop=True, skip_group_check=True)
                        mm.then_inc(made, 1)
        with Phase(nc, "s5m") as ph:
            rounds = NP // NQ
            w_re, w_im = ([ph.sb(f"w_{n}{k}", (P, NQ, NCH)) for k in range(2)] for n in ("re", "im"))
            er, ei, t1, t2, sr, si, dec = (
                ph.sb(n, (P, NQ, NCH)) for n in ("er", "ei", "t1", "t2", "sr", "si", "dec"))
            yv = ph.sb("yv", (P, 2, NQ, NCH))
            psv = ph.ps("v", (P, 4, 512))
            psy = ph.ps("y", (P, 4, 512))
            step, zeroed = ph.sem("vector_step"), ph.sem("zeroed")
            v_full, v_used, states = ph.sem("v_full"), ph.sem("v_used"), ph.sem("states")
            y_full, gelu = ph.sem("y_full"), ph.sem("gelu")
            stored = [ph.sem(f"stored{q}") for q in range(2)]
            trips = ((0, 3), (3, 6), (6, 8))
            NT = len(trips)
            rows = yc.rearrange("m p x -> (m p) x").rearrange("(g h) (t c) -> t h g c", h=SG, t=TAU)
            with nc.Block() as block:
                @block.sync
                def _(sp):
                    for n in range(rounds):
                        for par in range(2):
                            sp.wait_ge(gelu, NT * (2 * n + par + 1))
                            for k in range(TAU):
                                dst = rows[k][:, 2 * NQ * n + par:2 * NQ * (n + 1):2, :]
                                sp.dma_start(dst, yv[SG * k:SG * k + SG, par, :, :]).then_inc(stored[par], 16)
                    for par in range(2):
                        sp.wait_ge(stored[par], 16 * TAU * rounds)

                @block.tensor
                def _(pe):
                    def inputs(n, trip):
                        f = NT * n + trip
                        a, b = trips[trip]
                        if f >= 2:
                            pe.wait_ge(v_used, f - 1)
                        for pair in range(a, b):
                            pp = NQ * n + pair
                            for part in range(2):
                                for par in range(2):
                                    o = psv[SS * par:SS * par + SS, 2 * (f % 2) + part,
                                            NCH * (pair - a):NCH * (pair - a + 1)]
                                    mm = pe.matmul(o, win[:, part, pp, SS * par:SS * par + SS],
                                                   U[:, 2 * pp + par, :], start=True, stop=True)
                        mm.then_inc(v_full, 1)

                    def outputs(n, par):
                        r0 = SS * par
                        for trip, (a, b) in enumerate(trips):
                            g = NT * (2 * n + par) + trip
                            if g >= 4:
                                pe.wait_ge(gelu, g - 3)
                            for pair in range(a, b):
                                pp = NQ * n + pair
                                o = psy[:, g % 4, NCH * (pair - a):NCH * (pair - a + 1)]
                                pe.matmul(o, toep[:, par, pp, :], U[:, 2 * pp + par, :], start=True, stop=False)
                                for part, s in ((0, sr), (1, si)):
                                    w = ca[part][r0:r0 + SS, pp, :, :].rearrange("p a b -> p (a b)")
                                    mm = pe.matmul(o, w[:, SG:], s[r0:r0 + SS, pair, :], start=False,
                                                   stop=part == 1)
                            mm.then_inc(y_full, 1)
                    for trip in range(NT):
                        inputs(0, trip)
                    for n in range(rounds):
                        if n + 1 < rounds:
                            inputs(n + 1, 0)
                            inputs(n + 1, 1)
                        pe.wait_ge(states, n + 1)
                        outputs(n, 0)
                        if n + 1 < rounds:
                            inputs(n + 1, 2)
                        outputs(n, 1)

                @block.scalar
                def _(act):
                    for n in range(rounds):
                        for par in range(2):
                            for trip, (a, b) in enumerate(trips):
                                g = NT * (2 * n + par) + trip
                                act.wait_ge(y_full, g + 1)
                                if n and trip == 0:
                                    act.wait_ge(stored[par], 16 * TAU * n)
                                act.activation(yv[:, par, a:b, :],
                                               psy[:, g % 4, 0:NCH * (b - a)].rearrange("p (a c) -> p a c", c=NCH),
                                               ACT.Gelu_apprx_tanh).then_inc(gelu, 1)

                @block.vector
                def _(dve):
                    ch = Chain(dve, step)
                    tt = dve.tensor_tensor

                    def turns(n):
                        lo, hi = NQ * n, NQ * (n + 1)
                        wr, wi = w_re[n % 2], w_im[n % 2]
                        ch.inc(dve.memset(wr[:, :, 0:1], 1.0))
                        ch.inc(dve.memset(wi[:, :, 0:1], 0.0))
                        ch.inc(dve.tensor_copy(wr[:, :, 1:2], rot[:, 0, lo:hi].unsqueeze(2)))
                        ch.inc(dve.tensor_copy(wi[:, :, 1:2], rot[:, 1, lo:hi].unsqueeze(2)))
                        ch.do(dve.tensor_copy(dec[:, :, :], m8[:, lo:hi].unsqueeze(2).broadcast_to([P, NQ, NCH])))
                        ch.do(dve.memset(dec[:, :, 0:1], 0.0))
                        k = 1
                        while k < NCH - 1:
                            m = min(k, NCH - 1 - k)
                            s = slice(1, m + 1)
                            d = slice(k + 1, k + 1 + m)
                            wk = [w[:, :, k:k + 1].broadcast_to([P, NQ, m]) for w in (wr, wi)]
                            u, v = t1[:, :, 0:m], t2[:, :, 0:m]
                            ch.inc(tt(u, wr[:, :, s], wk[0], ALU.mult))
                            ch.do(tt(v, wi[:, :, s], wk[1], ALU.mult))
                            ch.do(tt(wr[:, :, d], u, v, ALU.subtract))
                            ch.inc(tt(u, wr[:, :, s], wk[1], ALU.mult))
                            ch.do(tt(v, wi[:, :, s], wk[0], ALU.mult))
                            ch.do(tt(wi[:, :, d], u, v, ALU.add))
                            k *= 2

                    def turned_back(n):
                        for trip, (a, b) in enumerate(trips):
                            f = NT * n + trip
                            dve.wait_ge(v_full, f + 1)
                            vr, vi = (psv[:, 2 * (f % 2) + part, 0:NCH * (b - a)].rearrange(
                                "p (a c) -> p a c", c=NCH) for part in range(2))
                            s = slice(a, b)
                            wr, wi = w_re[n % 2][:, s, :], w_im[n % 2][:, s, :]
                            ch.inc(tt(t1[:, s, :], vr, wr, ALU.mult))
                            ch.inc(tt(t2[:, s, :], vi, wi, ALU.mult))
                            ch.inc(tt(er[:, s, :], vi, wr, ALU.mult))
                            ch.do(tt(ei[:, s, :], vr, wi, ALU.mult))
                            dve.sem_inc(v_used, 1)
                            ch.inc(tt(ei[:, s, :], er[:, s, :], ei[:, s, :], ALU.subtract))
                            dve.wait_ge(step, ch.n)
                            ch.do(tt(er[:, s, :], t1[:, s, :], t2[:, s, :], ALU.add))

                    def states_of(n):
                        wr, wi = w_re[n % 2], w_im[n % 2]
                        for e in (er, ei):
                            flat = e[:, :, :].rearrange("p a c -> p (a c)")
                            ch.do(dve.tensor_tensor_scan(flat, dec[:, :, :].rearrange("p a c -> p (a c)"), flat, 0.0,
                                                         ALU.mult, ALU.add))
                        w = slice(0, NCH - 1)
                        ch.inc(tt(t1[:, :, w], er[:, :, w], wr[:, :, w], ALU.mult))
                        ch.do(tt(t2[:, :, w], ei[:, :, w], wi[:, :, w], ALU.mult))
                        if n:
                            dve.wait_ge(y_full, 2 * NT * n)
                        ch.do(tt(sr[:, :, 1:], t1[:, :, w], t2[:, :, w], ALU.subtract))
                        ch.inc(tt(t1[:, :, w], ei[:, :, w], wr[:, :, w], ALU.mult))
                        ch.do(tt(t2[:, :, w], er[:, :, w], wi[:, :, w], ALU.mult))
                        ch.do(tt(si[:, :, 1:], t1[:, :, w], t2[:, :, w], ALU.add))
                        dve.sem_inc(states, 1)
                    dve.memset(sr[:, :, 0:1], 0.0).then_inc(zeroed, 1)
                    dve.memset(si[:, :, 0:1], 0.0).then_inc(zeroed, 1)
                    dve.wait_ge(zeroed, 2)
                    for n in range(rounds):
                        turns(n)
                        turned_back(n)
                        states_of(n)


def epi_conv(rms, conv, x, off):
    def epi(e):
        raw = [e.ph.sb(f"raw{j}", (P, T1 + 2)) for j in range(2)]
        cv = [e.ph.sb(f"conv{j}", (P, T1)) for j in range(2)]
        gate = e.ph.sb("gate", (P, T1))
        conv_ready, gate_ready, zeroed = e.ph.sem("conv_ready"), e.ph.sem("gate_ready"), e.ph.sem("zeroed")

        def act(eng, m, j, i, ch):
            if j == 0:
                eng.wait_ge(conv_ready, i + 1)
                eng.activation(gate[:, :], cv[0][:, :], ACT.Silu).then_inc(gate_ready, 1)

        def dve(eng, m, j, i, ch):
            if isinstance(m, int) and m == j:
                eng.memset(raw[j][:, 0:2], 0.0).then_inc(zeroed, 1)
                eng.wait_ge(zeroed, m + 1)
            ch.do(eng.tensor_tensor(sview(raw[j][:, 2:], T1), pview(e.ps[j], T1), sview(rms[:, :], T1), ALU.mult))
            eng.sem_inc(e.psum_free, 1)
            col = lambda k: conv[:, bass.ds(m + off, 1), k]
            ch.do(eng.tensor_scalar(cv[j][:, :], raw[j][:, 2:], col(2), col(3), ALU.mult, ALU.add))
            for k in (1, 0):
                ch.do(eng.scalar_tensor_tensor(out=cv[j][:, :], in0=raw[j][:, k:k + T1], scalar=col(k),
                                               in1=cv[j][:, :], op0=ALU.mult, op1=ALU.add))
            if j == 0:
                eng.sem_inc(conv_ready, 1)
            else:
                eng.wait_ge(gate_ready, i + 1)
                ch.do(eng.tensor_tensor(cv[1][:, :], gate[:, :], cv[1][:, :], ALU.mult))
                ch.do(split(eng, ch, x[0][:, i, :], x[1][:, i, :], cv[1][:, :]))
            eng.sem_inc(e.out_ready, 1)
        return act, dve
    return epi, (0, 5.5)


def epi_residual():
    def epi(e):
        def act(eng, m, j, i, ch):
            pass

        def dve(eng, m, j, i, ch):
            eng.wait_ge(e.side_landed[0][j], 16 * (i + 1))
            ch.do(eng.tensor_tensor(sview(e.out[j][:, :], e.n), pview(e.ps[j], e.n),
                                    sview(e.side[0][j][:, :], e.n), ALU.add))
            eng.sem_inc(e.psum_free, 1)
            eng.sem_inc(e.out_ready, 1)
        return act, dve
    return epi, (0, 1)


def epi_gated_residual(mod, n):
    def epi(e):
        scaled = [e.ph.sb(f"scaled{j}", (P, n)) for j in range(2)]
        scaled_ready = e.ph.sem("scaled_ready")

        def act(eng, m, j, i, ch):
            eng.wait_ge(e.side_landed[0][j], 16 * (i + 1))
            eng.activation(scaled[j][:, :], e.side[0][j][:, :], ACT.Copy, scale=ALPHA).then_inc(scaled_ready, 1)

        def dve(eng, m, j, i, ch):
            eng.wait_ge(scaled_ready, m + 1)
            for s, (a, b) in enumerate(((0, SEQ), (SEQ, n))[:1 if n == SEQ else 2]):
                ins = eng.scalar_tensor_tensor(out=e.out[j][:, a:b], in0=e.ps[j][:, a:b],
                                               scalar=mod[:, bass.ds(m + 2 * DT, 1), s],
                                               in1=scaled[j][:, a:b], op0=ALU.mult, op1=ALU.add)
                ch.do(ins)
            eng.sem_inc(e.psum_free, 1)
            eng.sem_inc(e.out_ready, 1)
        return act, dve
    return epi, (0, 1 if n == SEQ else 2)


def modulate(act, sem, done, mod, m, x, v, h, n):
    for s, (a, b) in enumerate(((0, SEQ), (SEQ, n))):
        act.activation(h[:, a:b], v[:, a:b], ACT.Identity, bias=mod[:, m, s:s + 1],
                       scale=mod[:, DT + m, s:s + 1]).then_inc(sem, 1)
    act.wait_ge(sem, done + 2)
    act.activation(x[0][:, m, :], h[:, :], ACT.Copy).then_inc(sem, 1)


def finish_first(nc, c, hd, ctx, x1, rms, mod, x):
    with Phase(nc, "finish") as ph:
        NB = 4
        a = [ph.sb(f"a{j}", (P, T1)) for j in range(NB)]
        v = [ph.sb(f"v{j}", (P, T2)) for j in range(NB)]
        h = [ph.sb(f"h{j}", (P, T2)) for j in range(2)]
        landed = [ph.sem(f"landed{j}") for j in range(NB)]
        stored = [ph.sem(f"stored{j}") for j in range(NB)]
        normed, modulated, low = ph.sem("normed"), ph.sem("modulated"), ph.sem("low")
        with nc.Block() as block:
            @block.sync
            def _(sp):
                def load(m):
                    j = m % NB
                    sp.dma_start(a[j][:, :], hd[m]).then_inc(landed[j], 16)
                    sp.dma_start(v[j][:, SEQ:], ctx[m]).then_inc(landed[j], 16)
                for m in range(NB):
                    load(m)
                for m in range(DT):
                    sp.wait_ge(normed, m + 1)
                    sp.dma_start(x1[m], v[m % NB][:, :]).then_inc(stored[m % NB], 16)
                    if m + NB < DT:
                        sp.wait_ge(modulated, 3 * m + 2)
                        sp.wait_ge(stored[m % NB], 16 * (m // NB + 1))
                        load(m + NB)
                for j in range(NB):
                    sp.wait_ge(stored[j], 16 * DT // NB)

            @block.vector
            def _(dve):
                for m in range(DT + 1):
                    if m:
                        k = m - 1
                        dve.wait_ge(modulated, 3 * m)
                        dve.tensor_tensor(x[1][:, k, :], h[k % 2][:, :], x[0][:, k, :].bitcast(F32),
                                          ALU.subtract).then_inc(low, 1)
                    if m == DT:
                        break
                    j = m % NB
                    dve.wait_ge(landed[j], 32 * (m // NB + 1))
                    dve.scalar_tensor_tensor(out=v[j][:, 0:SEQ], in0=a[j][:, META:META + SEQ],
                                             scalar=c["final_g"][:, m:m + 1], in1=rms[:, META:META + SEQ],
                                             op0=ALU.mult, op1=ALU.mult).then_inc(normed, 1)

            @block.scalar
            def _(act):
                for m in range(DT):
                    act.wait_ge(normed, m + 1)
                    act.wait_ge(landed[m % NB], 32 * (m // NB + 1))
                    if m >= 2:
                        act.wait_ge(low, m - 1)
                    modulate(act, modulated, 3 * m, mod, m, x, v[m % NB], h[m % 2], T2)


def layer_norm(nc, name, c, vd, n, g, b, out, mod=None, x=None):
    with Phase(nc, name) as ph:
        v = ph.sb("v", (P, DT, n))
        mean, root, h = ph.sb("mean", (P, n)), ph.sb("root", (P, n)), [ph.sb(f"h{j}", (P, n)) for j in range(2)]
        modulated, low = ph.sem("modulated"), ph.sem("low")
        sq = [ph.sb(f"sq{j}", (P, n)) for j in range(2)]
        ps = ph.ps("mean_sum", (P, 1536))
        pq = ph.ps("square_sum", (P, 1536))
        landed = [ph.sem(f"landed{m}") for m in range(DT)]
        summed, centred, squared, sq_used, rooted = (ph.sem(s) for s in ("summed", "centred", "squared", "sq_used",
                                                                         "rooted"))
        step, done, stored = ph.sem("step"), ph.sem("done"), ph.sem("stored")
        with nc.Block() as block:
            @block.sync
            def _(sp):
                for m in range(DT):
                    sp.dma_start(v[:, m, :], vd[m]).then_inc(landed[m], 16)
                for m in range(DT):
                    sp.wait_ge(done, m + 1)
                    sp.dma_start(out[m], v[:, m, :]).then_inc(stored, 16)
                sp.wait_ge(stored, 16 * DT)

            @block.tensor
            def _(pe):
                for m in range(DT):
                    pe.wait_ge(landed[m], 16)
                    for bk, c0, w in pieces(n):
                        mm = pe.matmul(ps[:, 512 * bk:512 * bk + w], c["ones"][:, :], v[:, m, c0:c0 + w],
                                       start=m == 0, stop=m == DT - 1)
                mm.then_inc(summed, 1)
                for m in range(DT):
                    pe.wait_ge(squared, m + 1)
                    for bk, c0, w in pieces(n):
                        mm = pe.matmul(pq[:, 512 * bk:512 * bk + w], c["ones"][:, :], sq[m % 2][:, c0:c0 + w],
                                       start=m == 0, stop=m == DT - 1)
                    mm.then_inc(sq_used, 1)

            @block.scalar
            def _(act):
                act.wait_ge(summed, 1)
                act.activation(mean[:, :], ps[:, 0:n], ACT.Copy, scale=1.0 / D).then_inc(summed, 1)
                for m in range(DT):
                    act.wait_ge(centred, m + 1)
                    if m >= 2:
                        act.wait_ge(sq_used, m - 1)
                    act.activation(sq[m % 2][:, :], v[:, m, :], ACT.Square).then_inc(squared, 1)
                act.wait_ge(sq_used, DT)
                inverse_root(act, root[:, :], pq[:, 0:n], c["eps"][:, 0:1], 1.0 / D, rooted)
                for m in range(DT if x is not None else 0):
                    act.wait_ge(done, m + 1)
                    if m >= 2:
                        act.wait_ge(low, m - 1)
                    modulate(act, modulated, 3 * m, mod, m, x, v[:, m, :], h[m % 2], n)

            @block.vector
            def _(dve):
                ch = Chain(dve, step)
                dve.wait_ge(summed, 2)
                for m in range(DT):
                    dve.wait_ge(landed[m], 16)
                    dve.tensor_tensor(v[:, m, :], v[:, m, :], mean[:, :], ALU.subtract).then_inc(centred, 1)
                dve.wait_ge(rooted, 2)
                dve.wait_ge(centred, DT)
                for m in range(DT + 1):
                    if m < DT:
                        ch.do(dve.scalar_tensor_tensor(out=v[:, m, :], in0=v[:, m, :], scalar=g[:, m:m + 1],
                                                       in1=root[:, :], op0=ALU.mult, op1=ALU.mult))
                        dve.tensor_scalar(v[:, m, :], v[:, m, :], b[:, m:m + 1], None, ALU.add).then_inc(done, 1)
                    if m and x is not None:
                        k = m - 1
                        dve.wait_ge(modulated, 3 * m)
                        dve.tensor_tensor(x[1][:, k, :], h[k % 2][:, :], x[0][:, k, :].bitcast(F32),
                                          ALU.subtract).then_inc(low, 1)


def pool_and_gate(nc, c, t, z, x):
    NCK = T2 // P
    PAD, W = 8, 8 + SEQ + 16 + CTX + 8
    with Phase(nc, "mixer") as ph:
        a, ga, inv = ph.sb("a", (P, T2)), ph.sb("ga", (P, T2)), ph.sb("inv", (P, T2))
        pad = ph.sb("pad", (P, W))
        s = [ph.sb(f"s{k}", (P, W)) for k in range(4)]
        d, sga = ph.sb("d", (P, T2)), ph.sb("silu_a", (P, T2))
        pw, scale = ph.sb("pool_w", (P, 4, P)), ph.sb("pool_scale", (P, 4))
        u, v, gb = ph.sb("u", (P, T2)), ph.sb("v", (P, T2)), ph.sb("gb", (P, T2))
        vt = ph.sb("vt", (P, NCK, P))
        st, mv, root = ph.sb("stats", (P, NCK, 6)), ph.sb("mean_var", (P, NCK, 2)), ph.sb("root", (P, NCK))
        sw, sb_ = ph.sb("sgu_w", (P, 4, P)), ph.sb("sgu_b", (P, 4, P))
        f, sgb = ph.sb("f", (P, NCK, P)), ph.sb("silu_b", (P, T2))
        ps = ph.ps("pooled", (P, 1536))
        pt = ph.ps("turned_and_mixed", (P, 1536))
        small, a_in, ga_in, v_in, u_in, gb_in = (ph.sem(n) for n in (
            "small_in", "a_in", "gate_a_in", "v_in", "u_in", "gate_b_in"))
        silu_a, silu_b, pooled, mixed, turned = (ph.sem(n) for n in ("silu_a_ready", "silu_b_ready", "pool_made",
                                                                     "gate_made", "turned"))
        step, zeroed, rooted = ph.sem("step"), ph.sem("zeroed"), ph.sem("rooted")
        diffed, a_done, stats, normed, b_done, v_used = (ph.sem(n) for n in ("diffed", "pool_done", "stats_ready",
                                                                             "normed", "gate_done", "v_used"))
        flat = lambda q: q[:, :, :].rearrange("p a b -> p (a b)")
        seqs = ((PAD, 0, SEQ), (PAD + SEQ + 16, SEQ, CTX))
        with nc.Block() as block:
            @block.sync
            def _(sp):
                for dst, n in ((pw, "pool_w"), (scale, "pool_scale"), (sw, "sgu_w"), (sb_, "sgu_b")):
                    sp.dma_start(dst[:], t[n]).then_inc(small, 16)
                for g in range(4):
                    if g:
                        sp.wait_ge(turned, g)
                    sp.dma_start(v[:, :], z[12 + g]).then_inc(v_in, 16)
                    if g:
                        sp.wait_ge(diffed, g)
                    sp.dma_start(a[:, :], z[g]).then_inc(a_in, 16)
                    sp.dma_start(inv[:, :], t["inv_count"][g]).then_inc(a_in, 16)
                    if g:
                        sp.wait_ge(silu_a, g)
                    sp.dma_start(ga[:, :], z[4 + g]).then_inc(ga_in, 16)
                    if g:
                        sp.wait_ge(silu_b, g)
                    sp.dma_start(gb[:, :], z[16 + g]).then_inc(gb_in, 16)
                    if g:
                        sp.wait_ge(b_done, g)
                    sp.dma_start(u[:, :], z[8 + g]).then_inc(u_in, 16)

            @block.scalar
            def _(act):
                for g in range(4):
                    act.wait_ge(stats, g + 1)
                    act.activation(root[:, :], mv[:, :, 1], ACT.Sqrt, bias=c["eps"][:, 0:1]).then_inc(rooted, 1)
                    act.wait_ge(ga_in, 16 * (g + 1))
                    if g:
                        act.wait_ge(a_done, g)
                    act.activation(sga[:, :], ga[:, :], ACT.Silu).then_inc(silu_a, 1)
                    act.wait_ge(gb_in, 16 * (g + 1))
                    if g:
                        act.wait_ge(b_done, g)
                    act.activation(sgb[:, :], gb[:, :], ACT.Silu).then_inc(silu_b, 1)

            @block.tensor
            def _(pe):
                def turn(g):
                    pe.wait_ge(v_in, 16 * (g + 1))
                    if g:
                        pe.wait_ge(v_used, g)
                    for b in range(NCK):
                        mm = pe.transpose(pt[:, P * b:P * b + P], v[:, P * b:P * b + P], c["ident"][:, :])
                    mm.then_inc(turned, 1)
                pe.wait_ge(small, 64)
                turn(0)
                for g in range(4):
                    pe.wait_ge(diffed, g + 1)
                    for bk, c0, w in pieces(T2):
                        mm = pe.matmul(ps[:, c0:c0 + w], pw[:, g, :], d[:, c0:c0 + w], start=True, stop=True)
                    mm.then_inc(pooled, 1)
                    pe.wait_ge(normed, g + 1)
                    for b in range(NCK):
                        mm = pe.matmul(pt[:, P * b:P * b + P], vt[:, b, :], sw[:, g, :], start=True, stop=True)
                    mm.then_inc(mixed, 1)
                    if g < 3:
                        turn(g + 1)

            @block.vector
            def _(dve):
                ch = Chain(dve, step)
                tt = dve.tensor_tensor
                for b in [pad] + s:
                    dve.memset(b[:, :], 0.0).then_inc(zeroed, 1)
                dve.wait_ge(zeroed, 5)
                dve.wait_ge(small, 64)
                for g in range(4):
                    dve.wait_ge(turned, g + 1)
                    for b in range(NCK):
                        ch.inc(dve.bn_stats(st[:, b, :], pt[:, P * b:P * b + P]))
                    dve.wait_ge(step, ch.n)
                    for b in range(NCK):
                        ch.inc(dve.bn_aggr(mv[:, b, :], st[:, b, :]))
                    dve.wait_ge(step, ch.n)
                    dve.sem_inc(stats, 1)
                    dve.wait_ge(a_in, 32 * (g + 1))
                    for p0, c0, n in seqs:
                        ch.inc(dve.tensor_copy(pad[:, p0:p0 + n], a[:, c0:c0 + n]))
                    dve.wait_ge(step, ch.n)
                    ch.do(tt(s[0][:, 1:W], pad[:, 0:W - 1], pad[:, 1:W], ALU.add))
                    for k in range(1, g + 1):
                        q = 2 ** (k - 1)
                        lo, hi = 2 ** k, W - 2 ** k
                        ch.do(tt(s[k][:, lo:hi], s[k - 1][:, lo - q:hi - q], s[k - 1][:, lo + q:hi + q], ALU.add))
                    for p0, c0, n in seqs:
                        ch.inc(tt(d[:, c0:c0 + n], s[g][:, p0:p0 + n], inv[:, c0:c0 + n], ALU.mult))
                    dve.wait_ge(step, ch.n)
                    ch.do(tt(d[:, :], d[:, :], a[:, :], ALU.subtract))
                    dve.sem_inc(diffed, 1)
                    dve.wait_ge(rooted, g + 1)
                    ch.do(dve.reciprocal(root[:, :], root[:, :]))
                    for b in range(NCK):
                        ch.inc(dve.tensor_scalar(vt[:, b, :], pt[:, P * b:P * b + P], mv[:, b, 0:1],
                                                 root[:, b:b + 1], ALU.subtract, ALU.mult))
                    dve.wait_ge(step, ch.n)
                    dve.sem_inc(normed, 1)
                    dve.wait_ge(pooled, g + 1)
                    dve.wait_ge(silu_a, g + 1)
                    ch.do(dve.scalar_tensor_tensor(out=d[:, :], in0=ps[:, 0:T2], scalar=scale[:, g:g + 1],
                                                   in1=sga[:, :], op0=ALU.mult, op1=ALU.mult))
                    ch.do(split(dve, ch, x[0][:, g, :], x[1][:, g, :], d[:, :]))
                    dve.sem_inc(a_done, 1)
                    dve.wait_ge(mixed, g + 1)
                    ch.do(tt(f[:, :, :], pt[:, 0:T2].rearrange("p (a b) -> p a b", b=P),
                             sb_[:, g:g + 1, :].broadcast_to([P, NCK, P]), ALU.add))
                    dve.sem_inc(v_used, 1)
                    dve.wait_ge(u_in, 16 * (g + 1))
                    ch.do(tt(flat(f), flat(f), u[:, :], ALU.mult))
                    dve.wait_ge(silu_b, g + 1)
                    ch.do(tt(flat(f), flat(f), sgb[:, :], ALU.mult))
                    ch.do(split(dve, ch, x[0][:, 4 + g, :], x[1][:, 4 + g, :], flat(f)))
                    dve.sem_inc(b_done, 1)


def fourier(nc, c, t, z, x):
    LT, HT = SEQ // P, SEQ // P // 2
    with Phase(nc, "fnet") as ph:
        fin, fg = [ph.sb(f"f_in{j}", (P, SEQ)) for j in range(2)], [ph.sb(f"gate{j}", (P, SEQ)) for j in range(2)]
        dd = ph.sb("dft_features", (P, 2 * P))
        dl = ph.sb("dft_tokens", (P, 2, HT, SEQ))
        pq = [ph.sb(f"pq{j}", (P, LT, 2 * P)) for j in range(2)]
        eo = [[ph.sb(f"{n}{j}", (P, HT, 2 * P)) for n in ("sum", "difference")] for j in range(2)]
        sp_ = ph.sb("spectrum", (P, 4, SEQ))
        w = ph.sb("fnet_w", (P, 4, 512))
        sg = [ph.sb(f"silu{j}", (P, SEQ)) for j in range(2)]
        y = ph.sb("y", (P, SEQ))
        p1 = ph.ps("features", (P, 4, 512))
        p2 = [ph.ps(f"tokens{j}", (P, 1024)) for j in range(2)]
        const, tokens_in = ph.sem("constants"), ph.sem("dft_tokens_in")
        landed, g_landed = ([ph.sem(f"{n}{j}") for j in range(2)] for n in ("f_in_landed", "gate_landed"))
        first, first_out, second, second_out = (ph.sem(n) for n in ("first", "first_out", "second", "second_out"))
        silu, step, done = ph.sem("silu"), ph.sem("step"), ph.sem("done")
        folded = ph.sem("folded")
        with nc.Block() as block:
            @block.sync
            def _(sp):
                sp.dma_start(dd[:, :], t["dft_features"]).then_inc(const, 16)
                sp.dma_start(w[:, :, :], t["fnet_w"]).then_inc(const, 16)
                for h in range(2):
                    sp.dma_start(fin[h][:, :], z[h]).then_inc(landed[h], 16)
                sp.dma_start(dl[:, :, :, :], t["dft_tokens"]).then_inc(tokens_in, 16)
                for h in range(2, 4):
                    sp.wait_ge(first, 4 * (h - 1))
                    sp.dma_start(fin[h % 2][:, :], z[h]).then_inc(landed[h % 2], 16)
                for m in range(4):
                    if m >= 2:
                        sp.wait_ge(silu, m - 1)
                    sp.dma_start(fg[m % 2][:, :], z[4 + m]).then_inc(g_landed[m % 2], 16)

            @block.tensor
            def _(pe):
                pe.wait_ge(const, 32)

                def features(h):
                    pe.wait_ge(landed[h % 2], 16 * (h // 2 + 1))
                    for b in range(4):
                        if h:
                            pe.wait_ge(first_out, 4 * (h - 1) + b + 1)
                        for u in range(2):
                            q = 2 * b + u
                            mm = pe.matmul(p1[:, b, 256 * u:256 * u + 256], fin[h % 2][:, P * q:P * q + P],
                                           dd[:, :], start=True, stop=True)
                        mm.then_inc(first, 1)
                features(0)
                for h in range(4):
                    if h + 1 < 4:
                        features(h + 1)
                    pe.wait_ge(folded, h + 1)
                    pe.wait_ge(tokens_in, 16)
                    if h >= 2:
                        pe.wait_ge(second_out, h - 1)
                    for b in range(2):
                        for n in range(2 * HT):
                            part, q = divmod(n, HT)
                            mm = pe.matmul(p2[h % 2][:, 512 * b:512 * b + 512],
                                           eo[h % 2][b][:, q, P * part:P * part + P],
                                           dl[:, part, q, 512 * b:512 * b + 512], start=n == 0, stop=n == 2 * HT - 1)
                    mm.then_inc(second, 1)
                for m in range(4):
                    pe.wait_ge(second_out, 4 if m < 2 else 4 + m - 1)
                    for b in range(2):
                        for k in range(4):
                            mm = pe.matmul(p2[m % 2][:, 512 * b:512 * b + 512], w[:, k, P * m:P * m + P],
                                           sp_[:, k, 512 * b:512 * b + 512], start=k == 0, stop=k == 3)
                    mm.then_inc(second, 1)

            @block.scalar
            def _(act):
                for h in range(4):
                    for b in range(4):
                        act.wait_ge(first, 4 * h + b + 1)
                        if h >= 2:
                            act.wait_ge(folded, h - 1)
                        act.activation(pq[h % 2][:, 2 * b:2 * b + 2, :].rearrange("p a b -> p (a b)"), p1[:, b, :],
                                       ACT.Copy).then_inc(first_out, 1)
                for m in range(4):
                    act.wait_ge(g_landed[m % 2], 16 * (m // 2 + 1))
                    if m >= 2:
                        act.wait_ge(done, m - 1)
                    act.activation(sg[m % 2][:, :], fg[m % 2][:, :], ACT.Silu).then_inc(silu, 1)

            @block.vector
            def _(dve):
                ch = Chain(dve, step)
                def fold(h):
                    dve.wait_ge(first_out, 4 * (h + 1))
                    if h >= 2:
                        dve.wait_ge(second, h - 1)
                    lo, hi = pq[h % 2][:, 0:HT, :], pq[h % 2][:, HT:LT, :]
                    dve.tensor_tensor(eo[h % 2][0][:, :, :], lo, hi, ALU.add)
                    dve.tensor_tensor(eo[h % 2][1][:, :, :], lo, hi, ALU.subtract).then_inc(folded, 1)
                fold(0)
                for h in range(4):
                    if h + 1 < 4:
                        fold(h + 1)
                    dve.wait_ge(second, h + 1)
                    dve.tensor_copy(sp_[:, h, :].rearrange("p (k b) -> p b k", b=2),
                                    p2[h % 2][:, :].rearrange("p (b k) -> p b k", b=2)).then_inc(second_out, 1)
                for m in range(4):
                    dve.wait_ge(second, 4 + m + 1)
                    dve.wait_ge(silu, m + 1)
                    dve.tensor_tensor(y[:, :], p2[m % 2][:, :], sg[m % 2][:, :], ALU.mult).then_inc(second_out, 1)
                    dve.wait_ge(second_out, 4 + m + 1)
                    ch.do(split(dve, ch, x[0][:, m, :], x[1][:, m, :], y[:, :]))
                    dve.sem_inc(done, 1)


def mla_operands(nc, c, t, z, zk, qc, kc, vc, room):
    QT = QL // P
    with Phase(nc, "mla") as ph:
        cq = room[0][:, 0:QT * SEQ].rearrange("p (k n) -> p k n", k=QT)
        wq = room[1][:, 0:QT * NH * P].rearrange("p (k h m) -> p k h m", k=QT, h=NH)
        ckv, kr = ph.sb("ckv", (P, T2)), ph.sb("kr", (P, T2))
        wk, wv = ph.sb("wk", (P, NH, NOPE)), ph.sb("wv", (P, NH * VD))
        qn, kn = ph.sb("q_norm", (P, QT)), ph.sb("kv_norm", (P, 1))
        turn = ph.sb("turn", (P, T2))
        sq = [ph.sb(f"sq{k}", (P, SEQ)) for k in range(QT)] + [ph.sb("sq_kv", (P, T2))]
        root, rk, tmp = sq[0], sq[2], sq[2]
        pq = [ph.ps(f"q{j}", (P, 1024)) for j in range(2)]
        pk = ph.ps("k", (P, 1536))
        pv = ph.ps("v", (P, 512))
        landed, squared, summed, rooted, normed = (ph.sem(n) for n in ("landed", "squared", "summed", "rooted",
                                                                       "normed"))
        q_made, q_low, q_high, k_made, k_out = (ph.sem(n) for n in ("q_made", "q_plain_out", "q_turned_out",
                                                                    "k_made", "k_out"))
        v_made, v_out, step, kr_done, kr_copied = (ph.sem(n) for n in ("v_made", "v_out", "step", "kr_done",
                                                                       "kr_copied"))
        loads = ((cq[:, 0, :], z[8]), (cq[:, 1, :], z[9]), (ckv[:, :], zk[0]), (kr[:, :], zk[1]),
                 (wq[:, :, :, :], t["w_q_up"]), (wk[:, :, :], t["w_k_up"]), (wv[:, :], t["w_v_up"]),
                 (qn[:, :], t["q_norm"]), (kn[:, :], t["kv_norm"]), (turn[:, :], t["rope"]))
        A, B = slice(NOPE, NOPE + ROPE), slice(NOPE + ROPE, P)
        with nc.Block() as block:
            @block.sync
            def _(sp):
                for dst, src in loads:
                    sp.dma_start(dst, src).then_inc(landed, 16)

            @block.tensor
            def _(pe):
                pe.wait_ge(squared, 3)
                for b, c0, w in pieces(SEQ):
                    for k in range(QT):
                        pe.matmul(pq[0][:, c0:c0 + w], c["ones"][:, :], sq[k][:, c0:c0 + w], start=k == 0,
                                  stop=k == QT - 1)
                for b, c0, w in pieces(T2):
                    mm = pe.matmul(pk[:, c0:c0 + w], c["ones"][:, :], sq[2][:, c0:c0 + w], start=True, stop=True)
                mm.then_inc(summed, 1)
                pe.wait_ge(normed, 3)
                for h in range(NH):
                    if h >= 2:
                        pe.wait_ge(q_low, h - 1)
                        pe.wait_ge(q_high, h - 1)
                    for b, c0, w in pieces(SEQ):
                        for k in range(QT):
                            mm = pe.matmul(pq[h % 2][:, c0:c0 + w], wq[:, k, h, :], cq[:, k, c0:c0 + w],
                                           start=k == 0, stop=k == QT - 1)
                    mm.then_inc(q_made, 1)
                    if h:
                        pe.wait_ge(k_out, h)
                    for b, c0, w in pieces(T2):
                        mm = pe.matmul(pk[0:NOPE, c0:c0 + w], wk[:, h, :], ckv[:, c0:c0 + w], start=True, stop=True)
                    mm.then_inc(k_made, 1)
                for b in range(T2 // P):
                    if b:
                        pe.wait_ge(v_out, b)
                    pe.matmul(pv[:, :], ckv[:, P * b:P * b + P], wv[:, :], start=True, stop=True).then_inc(v_made, 1)

            @block.scalar
            def _(act):
                act.wait_ge(landed, 16 * len(loads))
                for k in range(QT):
                    act.activation(sq[k][:, :], cq[:, k, :], ACT.Square).then_inc(squared, 1)
                act.activation(sq[2][:, :], ckv[:, :], ACT.Square).then_inc(squared, 1)
                act.wait_ge(summed, 1)
                inverse_root(act, root[:, :], pq[0][:, :], c["eps"][:, 0:1], 1.0 / QL, rooted)
                inverse_root(act, rk[:, :], pk[:, 0:T2], c["eps"][:, 0:1], 1.0 / KVL, rooted, 2)
                for h in range(NH):
                    act.wait_ge(q_made, h + 1)
                    act.activation(qc[0:NOPE, h, :], pq[h % 2][0:NOPE, :], ACT.Copy).then_inc(q_low, 1)
                    act.wait_ge(k_made, h + 1)
                    act.activation(kc[0:NOPE, h, :], pk[0:NOPE, 0:T2], ACT.Copy).then_inc(k_out, 1)
                    if h == 0:
                        act.wait_ge(kr_done, 1)
                    act.activation(kc[A, h, :], kr[A, :], ACT.Copy).then_inc(kr_copied, 1)
                for b in range(T2 // P):
                    act.wait_ge(v_made, b + 1)
                    act.activation(vc[:, b, :].rearrange("p (h v) -> p h v", h=NH)[:, :, 0:VD],
                                   pv[:, :].rearrange("p (h v) -> p h v", h=NH), ACT.Copy).then_inc(v_out, 1)

            @block.vector
            def _(dve):
                ch = Chain(dve, step)
                tt = dve.tensor_tensor
                dve.memset(vc[:, :, :].rearrange("p b (h v) -> p (b h) v", v=VD + 1)[:, :, VD:VD + 1], 1.0)
                dve.memset(kc[NOPE + ROPE:NOPE + ROPE + 1, :, :], 1.0)
                dve.wait_ge(landed, 16 * len(loads))
                dve.wait_ge(rooted, 4)
                for k in range(QT):
                    dve.scalar_tensor_tensor(out=cq[:, k, :], in0=cq[:, k, :], scalar=qn[:, k:k + 1], in1=root[:, :],
                                             op0=ALU.mult, op1=ALU.mult).then_inc(normed, 1)
                dve.scalar_tensor_tensor(out=ckv[:, :], in0=ckv[:, :], scalar=kn[:, 0:1], in1=rk[:, :],
                                         op0=ALU.mult, op1=ALU.mult).then_inc(normed, 1)
                dve.wait_ge(normed, 3)
                ch.inc(tt(tmp[A, :], kr[B, :], turn[B, :], ALU.mult))
                ch.do(tt(kr[A, :], kr[A, :], turn[A, :], ALU.mult))
                ch.do(tt(kr[A, :], kr[A, :], tmp[A, :], ALU.add))
                dve.sem_inc(kr_done, 1)
                for h in range(NH):
                    dve.wait_ge(q_made, h + 1)
                    ps = pq[h % 2]
                    ch.inc(tt(tmp[A, 0:SEQ], ps[B, :], turn[B, 0:SEQ], ALU.mult))
                    ch.do(tt(qc[A, h, :], ps[A, :], turn[A, 0:SEQ], ALU.mult))
                    ch.do(tt(qc[A, h, :], qc[A, h, :], tmp[A, 0:SEQ], ALU.add))
                    dve.sem_inc(q_high, 1)


def attention(nc, c, z, qc, kc, vc, x, room):
    NQT, NKT = SEQ // P, T2 // P
    KD, V1, HQ = NOPE + ROPE, VD + 1, NQT // 2
    SCORE_RING, PROB_RING = 3, 6
    BACK = (2, 5, 8)
    scale = float(KD) ** -0.5
    with Phase(nc, "attn") as ph:
        pt = [ph.sb(f"probs{j}", (P, 512)) for j in range(PROB_RING)]
        mx = ph.sb("max", (P, KD + NH * NQT))
        rr = ph.sb("inverse_sum", (P, HQ))
        zero = ph.sb("zeros", (1, P + HQ * V1), mybir.dt.bfloat16)
        o = room[0][:, :].rearrange("p (q n) -> p q n", q=NQT)
        dg = room[1][:, :].rearrange("p (m n) -> p m n", m=4)
        y = ph.sb("y", (P, SEQ))
        pa = ph.ps("scores", (P, 1536))
        pb = [ph.ps(f"turned_scores{j}", (P, 512)) for j in range(SCORE_RING)]
        pc = [ph.ps(f"values{j}", (P, 512)) for j in range(2)]
        zeroed, scored, maxed, rows_made, rows_out = (ph.sem(n) for n in (
            "zeroed", "scored", "maxed", "rows_made", "rows_out"))
        turned, exped, used, summed, normal = (ph.sem(n) for n in ("turned", "exponentials", "probs_used", "summed",
                                                                  "normal"))
        step, landed, back, back_used, silu = (ph.sem(n) for n in ("step", "landed", "back", "back_used", "silu"))
        with nc.Block() as block:
            @block.sync
            def _(sp):
                for m in range(4):
                    sp.dma_start(dg[:, m, :], z[10 + m]).then_inc(landed, 16)

            @block.tensor
            def _(pe):
                def scores(h, q):
                    i = h * NQT + q
                    if q == 0 and h:
                        pe.wait_ge(rows_out, h)
                    elif q:
                        pe.wait_ge(maxed, i)
                    for b, c0, w in pieces(T2):
                        mm = pe.matmul(pa[:, c0:c0 + w], qc[0:KD, h, P * q:P * q + P], kc[0:KD, h, c0:c0 + w],
                                       start=True, stop=True)
                    mm.then_inc(scored, 1)

                def turn_maxima(h):
                    pe.wait_ge(maxed, NQT * (h + 1))
                    for q in range(NQT):
                        i = h * NQT + q
                        mm = pe.matmul(pa[0:KD + 1, P * q:P * q + P], mx[:, i:i + KD + 1], c["ident"][:, :],
                                       start=True, stop=True)
                    mm.then_inc(rows_made, 1)

                def turned_scores(h, k):
                    if k == 0:
                        pe.wait_ge(rows_out, h + 1)
                    for b in range(2):
                        u = 2 * (h * NKT + k) + b
                        if u >= SCORE_RING:
                            pe.wait_ge(exped, u - SCORE_RING + 1)
                        pe.matmul(pb[u % SCORE_RING][:, :], kc[0:KD + 1, h, P * k:P * k + P],
                                  qc[0:KD + 1, h, 512 * b:512 * b + 512], start=True, stop=True).then_inc(turned, 1)

                def values(h, k):
                    for b in range(2):
                        u = 2 * (h * NKT + k) + b
                        if k == 0:
                            if h:
                                pe.wait_ge(normal, 2 * (h - 1) + b + 1)
                            pe.matmul(pc[b][:, 0:HQ * V1], zero[:, 0:P], zero[:, P:P + HQ * V1],
                                      start=True, stop=False, skip_group_check=True)
                        pe.wait_ge(exped, u + 1)
                        for q in range(HQ):
                            mm = pe.matmul(pc[b][:, V1 * q:V1 * (q + 1)], pt[u % PROB_RING][:, P * q:P * q + P],
                                           vc[:, k, V1 * h:V1 * (h + 1)], start=False,
                                           stop=k == NKT - 1 and q == HQ - 1, skip_group_check=True)
                        mm.then_inc(used, 1)
                pe.wait_ge(zeroed, 2)
                for q in range(NQT):
                    scores(0, q)
                turn_maxima(0)

                def back_turn(m):
                    pe.wait_ge(normal, 4 * (m + 1))
                    if m:
                        pe.wait_ge(back_used, m)
                    for q in range(NQT):
                        mm = pe.transpose(pa[:, P * q:P * q + P], o[:, q, P * m:P * m + P], c["ident"][:, :])
                    mm.then_inc(back, 1)
                for h in range(NH):
                    for k in range(NKT):
                        if h + 1 < NH and k < NQT:
                            scores(h + 1, k)
                        if h + 1 == NH and k in BACK:
                            if k == BACK[0]:
                                pe.wait_ge(rows_out, NH)
                            back_turn(BACK.index(k))
                        if h + 1 < NH and k == NQT:
                            turn_maxima(h + 1)
                        turned_scores(h, k)
                        if k:
                            values(h, k - 1)
                        elif h:
                            values(h - 1, NKT - 1)
                values(NH - 1, NKT - 1)
                back_turn(3)

            @block.scalar
            def _(act):
                def rows(h):
                    act.wait_ge(rows_made, h + 1)
                    act.activation(qc[KD:KD + 1, h, :], pa[KD:KD + 1, 0:SEQ], ACT.Copy,
                                   scale=-1.0).then_inc(rows_out, 1)
                act.wait_ge(landed, 64)
                for m in range(4):
                    act.activation(dg[:, m, :], dg[:, m, :], ACT.Silu).then_inc(silu, 1)
                rows(0)
                for h in range(NH):
                    for k in range(NKT):
                        if h + 1 < NH and k == NQT:
                            rows(h + 1)
                        for b in range(2):
                            u = 2 * (h * NKT + k) + b
                            act.wait_ge(turned, u + 1)
                            if u >= PROB_RING:
                                act.wait_ge(used, u - PROB_RING + 1)
                            act.activation(pt[u % PROB_RING][:, :], pb[u % SCORE_RING][:, :], ACT.Exp,
                                           scale=scale).then_inc(exped, 1)

            @block.vector
            def _(dve):
                ch = Chain(dve, step)

                def maximum(h, q):
                    i = h * NQT + q
                    dve.wait_ge(scored, i + 1)
                    dve.tensor_reduce(mx[:, KD + i:KD + i + 1], pa[:, 0:T2], AX.X, ALU.max).then_inc(maxed, 1)

                def normalise(h):
                    for b in range(2):
                        dve.wait_ge(used, 2 * (h * NKT + NKT - 1) + b + 1)
                        sums = pc[b][:, 0:HQ * V1].rearrange("p (q v) -> p q v", v=V1)
                        ch.do(dve.reciprocal(rr[:, :], sums[:, :, VD]))
                        ins = dve.tensor_tensor(o[:, HQ * b:HQ * (b + 1), VD * h:VD * (h + 1)], sums[:, :, 0:VD],
                                                rr[:, :].unsqueeze(2).broadcast_to([P, HQ, VD]), ALU.mult)
                        ins.then_inc(normal, 1)
                        dve.wait_ge(normal, 2 * h + b + 1)

                def gated(m):
                    dve.wait_ge(back, m + 1)
                    dve.wait_ge(silu, m + 1)
                    ch.do(dve.tensor_tensor(y[:, :], pa[:, 0:SEQ], dg[:, m, :], ALU.mult))
                    dve.sem_inc(back_used, 1)
                    ch.do(split(dve, ch, x[0][:, m, :], x[1][:, m, :], y[:, :]))
                dve.memset(mx[:, 0:KD], 0.0).then_inc(zeroed, 1)
                dve.memset(zero[:, :], 0.0).then_inc(zeroed, 1)
                for q in range(NQT):
                    maximum(0, q)
                for h in range(NH):
                    for k in range(NKT):
                        if h + 1 < NH and k < NQT:
                            maximum(h + 1, k)
                        if h and k == 1:
                            normalise(h - 1)
                        if h + 1 == NH and k in BACK:
                            gated(BACK.index(k))
                normalise(NH - 1)
                gated(3)


def setup(nc, ph, t, c):
    shapes = {"ident": (P, P), "chunk_mask": (P, T1), "causal": (P, 9, P), "mix_g": (P, DT), "ffn_g": (P, DT),
              "final_g": (P, DT), "hgrn_g": (P, 1), "ab_g": (P, DT), "ab_b": (P, DT), "cd_g": (P, DT),
              "cd_b": (P, DT), "lb_logits": (P, 2, HH), "conv": (P, 2 * FT, 4)}
    for n, sh in shapes.items():
        c[n] = ph.sb(n, sh)
    for n, sh in {"ones": (P, P), "eps": (P, 1), "lb": (P, HH), "one_minus_lb": (P, HH)}.items():
        c[n] = ph.sb(n, sh)
    with Phase(nc, "setup") as s:
        m, e0, e1 = (s.sb(n, (P, HH)) for n in ("m", "e0", "e1"))
        landed, step, ex = s.sem("landed"), s.sem("step"), s.sem("exponentials")
        with nc.Block() as block:
            @block.sync
            def _(sp):
                for n, sh in shapes.items():
                    sp.dma_start(c[n][:], t[n]).then_inc(landed, 16)
                sp.wait_ge(landed, 16 * len(shapes))

            @block.vector
            def _(dve):
                ch = Chain(dve, step)
                dve.memset(c["ones"][:, :], 1.0)
                dve.memset(c["eps"][:, :], EPS)
                dve.wait_ge(landed, 16 * len(shapes))
                l0, l1 = c["lb_logits"][:, 0, :], c["lb_logits"][:, 1, :]
                ch.do(dve.tensor_tensor(m[:, :], l0, l1, ALU.max))
                ch.inc(dve.tensor_tensor(e0[:, :], l0, m[:, :], ALU.subtract))
                ch.inc(dve.tensor_tensor(e1[:, :], l1, m[:, :], ALU.subtract))
                dve.wait_ge(ex, 2)
                ch.do(dve.tensor_tensor(e1[:, :], e0[:, :], e1[:, :], ALU.add))
                ch.do(dve.reciprocal(e1[:, :], e1[:, :]))
                ch.do(dve.tensor_tensor(c["lb"][:, :], e0[:, :], e1[:, :], ALU.mult))
                ch.do(dve.tensor_scalar(c["one_minus_lb"][:, :], c["lb"][:, :], -1.0, 1.0, ALU.mult, ALU.add))

            @block.scalar
            def _(act):
                act.wait_ge(step, 3)
                act.activation(e0[:, :], e0[:, :], ACT.Exp).then_inc(ex, 1)
                act.activation(e1[:, :], e1[:, :], ACT.Exp).then_inc(ex, 1)


def build(nc, t):
    def scratch(name, tiles, n):
        return nc.dram_tensor(name, (tiles, P, n), F32, kind="Internal").ap()
    t["p"] = scratch("p", 7 * DT, T1)
    t["y_glu"] = scratch("y_glu", DT, T1)
    t["mb"] = scratch("mb", DT, T1)
    t["h"] = scratch("h", DT, T1)
    c = {}

    def pair(ph, name, tiles, n):
        return [ph.sb(f"{name}_{part}", (P, tiles, n), F32R) for part in ("high", "low")]

    own = lambda s, a, m: a[m]
    root = Phase(nc, "all")
    setup(nc, root, t, c)
    mods = root.sb("modulations", (P, 6 * DT, 2))
    mod, mod2 = mods[:, 0:3 * DT, :], mods[:, 3 * DT:, :]
    with Phase(nc, "mix") as outer:
        rms = outer.sb("inverse_rms", (P, T1))
        acc = outer.sb("squares", (P, T1))
        xa = pair(outer, "z", DT, T1)
        prepare_input(nc, c, t["xt"], xa, acc)
        inverse_rms(nc, "mix_rms", acc, rms, D, c, T1)
        epi, steps = epi_scale_store(rms)
        dense(nc, "w_in", t["w_in"], 7 * DT, DT, xa, T1, epi, store=lambda m: t["p"][m], steps=steps)
    with Phase(nc, "yb") as outer:
        xb = pair(outer, "yb", DT, T1)
        hgrn(nc, c, t, t["p"], xb, mods)
        epi, steps = epi_gate(None)
        dense(nc, "hgrn_proj", t["w_hgrn_proj"], DT, DT, xb, T1, epi, sides=(t["p"],),
              side_at=lambda s, a, m: a[m + 6 * DT], store=lambda m: t["mb"][m], steps=steps)
    with Phase(nc, "first_norms") as norms:
        rms = norms.sb("inverse_rms", (P, T1))
        t["u_chunks"] = scratch("u_chunks", DT, T1)
        t["y_chunks"] = scratch("y_chunks", DT, T1)
        s5(nc, c, t, t["p"], t["u_chunks"], t["y_chunks"])
        with Phase(nc, "first") as outer:
            xa, xb = pair(outer, "operand_a", DT, T1), pair(outer, "operand_b", DT, T1)
            stage = [outer.sb(f"weights{j}", (P, DT * P)) for j in range(2)]
            split_y(nc, t["y_chunks"], t["y_glu"], xa)
            epi, steps = epi_glu(xb)
            dense(nc, "glu", t["w_glu"], DT, DT, xa, T1, epi, sides=(t["y_glu"],), side_at=own, steps=steps,
                  stage=stage, following=t["w_ssm_proj"])
            epi, steps = epi_gate(xa)
            dense(nc, "ssm_proj", t["w_ssm_proj"], DT, DT, xb, T1, epi, sides=(t["p"], t["mb"]),
                  side_at=lambda s, a, m: a[m + 5 * DT] if s == 0 else a[m], steps=steps, stage=stage, warm=True,
                  following=t["w_out"])
            epi, steps = epi_residual_norm(xb, c["ffn_g"], rms)
            dense(nc, "w_out", t["w_out"], DT, DT, xa, T1, epi, sides=(t["xt"],), side_at=own,
                  store=lambda m: t["h"][m], steps=steps, stage=stage, warm=True, following=t["w_up"])
            inverse_rms(nc, "ffn_rms", rms, rms, D, c, T1)
            f0, last = 0, 2
            for n, k in enumerate((8, 8, 6)):
                epi, steps = epi_conv(rms, c["conv"], xa, 2 * f0)
                dense(nc, f"up{n}", t["w_up"], 2 * k, DT, xb, T1, epi, steps=steps, off=2 * f0, stage=stage, warm=True,
                      following=t[f"w_down{n}"])
                epi, steps = epi_residual() if n < last else epi_residual_norm(None, None, rms)
                dense(nc, f"down{n}", t[f"w_down{n}"], DT, k, xa, T1, epi, sides=(t["h"],), side_at=own,
                      store=lambda m: t["h"][m], steps=steps, stage=stage, warm=True,
                      following=t["w_up"][2 * (f0 + k):] if n < last else None)
                f0 += k
        t["x1"], t["x2"] = scratch("x1", DT, T2), scratch("x2", DT, T2)
        t["v"], t["abz"] = scratch("v", DT, T2), scratch("abz", 20, T2)
        t["v_out"] = scratch("v_out", DT, SEQ)
        t["cdz"], t["cdk"] = scratch("cdz", 14, SEQ), scratch("cdk", 2, T2)
        with Phase(nc, "abx") as inner:
            xa = pair(inner, "operand", DT, T2)
            inverse_rms(nc, "final_rms", rms, rms, D, c, T1)
            finish_first(nc, c, t["h"], t["ctx"], t["x1"], rms, mod, xa)
            epi, steps = epi_scale_store(None)
            dense(nc, "ab_in", t["ab_w_in"], 20, DT, xa, T2, epi, store=lambda m: t["abz"][m], steps=steps)
    with Phase(nc, "abm") as inner:
        xb = pair(inner, "operand", DT, T2)
        pool_and_gate(nc, c, t, t["abz"], xb)
        epi, steps = epi_gated_residual(mod, T2)
        dense(nc, "ab_out", t["ab_w_out"], DT, DT, xb, T2, epi, sides=(t["x1"],), side_at=own,
              store=lambda m: t["v"][m], steps=steps)
    with Phase(nc, "cdx") as inner:
        xa = pair(inner, "operand", DT, T2)
        stage = [inner.sb(f"weights{j}", (P, DT * P)) for j in range(2)]
        layer_norm(nc, "ab_norm", c, t["v"], T2, c["ab_g"], c["ab_b"], t["x2"], mod2, xa)
        epi, steps = epi_scale_store(None)
        dense(nc, "cd_in", t["cd_w_in"], 14, DT, xa, SEQ, epi, store=lambda m: t["cdz"][m], steps=steps,
              stage=stage, following=t["cd_w_kv"])
        epi, steps = epi_scale_store(None)
        dense(nc, "cd_kv", t["cd_w_kv"], 2, DT, xa, T2, epi, store=lambda m: t["cdk"][m], steps=steps,
              stage=stage, warm=True)
    with Phase(nc, "cdm") as inner:
        xv = pair(inner, "attended", 4, SEQ)
        with Phase(nc, "qkv") as q:
            qc, kc = q.sb("queries", (P, NH, SEQ)), q.sb("keys", (P, NH, T2))
            vc = q.sb("values", (P, T2 // P, NH * (VD + 1)))
            room = [q.sb(f"room{j}", (P, 4 * SEQ)) for j in range(2)]
            mla_operands(nc, c, t, t["cdz"], t["cdk"], qc, kc, vc, room)
            attention(nc, c, t["cdz"], qc, kc, vc, xv, room)
        with Phase(nc, "cdo") as o:
            xf = pair(o, "spectrum", 4, SEQ)
            fourier(nc, c, t, t["cdz"], xf)
            epi, steps = epi_gated_residual(mod2, SEQ)
            dense(nc, "cd_out", t["cd_w_out"], DT, DT, [Halves(xf[j], xv[j]) for j in range(2)], SEQ, epi,
                  sides=(t["x2"],), side_at=lambda s, a, m: a[m][:, 0:SEQ], store=lambda m: t["v_out"][m],
                  steps=steps)
    layer_norm(nc, "cd_norm", c, t["v_out"], SEQ, c["cd_g"], c["cd_b"], t["out"])


def columns(v):
    return np.ascontiguousarray(np.asarray(v).reshape(-1, P).T)


def weight_tiles(w):
    k, m = w.shape
    return np.ascontiguousarray(w.reshape(k // P, P, m // P, P).transpose(2, 1, 0, 3)).reshape(m // P, P, -1)


def layout(a):
    f = np.float32
    o = {}
    xt = np.zeros((DT, P, T1), f)
    xt[:, :, :META] = a["meta_tokens"].T.reshape(DT, P, META)
    xt[:, :, META:META + SEQ] = a["x"][0].T.reshape(DT, P, SEQ)
    o["xt"] = xt
    for n, k in (("mix_g", "mix_norm_g"), ("ffn_g", "ffn_norm_g"), ("final_g", "final_norm_g"),
                 ("hgrn_g", "hgrn_norm_g")):
        o[n] = columns(a[k])
    o["lb_logits"] = np.ascontiguousarray(a["hgrn_lb_logits"].reshape(2, HH, P).transpose(2, 0, 1))
    for n, k in (("w_in", "w_in"), ("w_hgrn_proj", "w_hgrn_proj"), ("w_glu", "ssm_w_glu"),
                 ("w_ssm_proj", "w_ssm_proj"), ("w_out", "w_out")):
        o[n] = weight_tiles(a[k][0])

    def pairs(v, lead):
        v = np.asarray(v).reshape((NPAIR, 2, SS) + lead)
        return np.ascontiguousarray(np.moveaxis(v, 0, 2)).reshape((P, NPAIR) + lead)
    o["lam_re"], o["lam_im"] = pairs(a["ssm_lambda_re"][0], ()), pairs(a["ssm_lambda_im"][0], ())
    o["log_dt"] = pairs(np.broadcast_to(a["ssm_log_dt"][0][:, None], (G, SS)), ())
    o["b_re"], o["b_im"] = pairs(a["ssm_b_re"][0], (SG,)), pairs(a["ssm_b_im"][0], (SG,))
    o["c_re"], o["c_im"] = (pairs(a[n][0].transpose(0, 2, 1), (SG,)) for n in ("ssm_c_re", "ssm_c_im"))
    d = a["ssm_d"][0].reshape(NPAIR, 2, SG).transpose(1, 2, 0)
    o["ssm_d"] = np.ascontiguousarray(np.broadcast_to(d[:, None], (2, 2, SG, NPAIR))).reshape(SS, NPAIR)
    ctx = a["ctx_2"][0].T.reshape(DT, P, CTX)
    o["ctx"] = np.ascontiguousarray(ctx)
    order = np.arange(2 * FT).reshape(2, FT).T.reshape(-1)
    o["w_up"] = np.ascontiguousarray(weight_tiles(a["w_up"][0])[order])
    cw = np.concatenate([a["conv_w"][0], a["conv_b"][0][None]])
    o["conv"] = np.ascontiguousarray(cw.reshape(4, 2 * FT, P)[:, order].transpose(2, 1, 0))
    for n, (r0, r1) in enumerate(((0, 1024), (1024, 2048), (2048, FF))):
        o[f"w_down{n}"] = weight_tiles(a["w_down"][0][r0:r1])
    o["cond"] = np.ascontiguousarray(np.stack([columns(a["c_2"][0]), columns(a["c_ctx_2"])], -1))
    o["w_mod"] = np.concatenate([weight_tiles(a[f"{n}_w_mod_2"][0]) for n in ("ab", "cd")])
    o["b_mod"] = np.concatenate([columns(a[f"{n}_b_mod_2"][0]) for n in ("ab", "cd")], 1)
    for n in ("ab", "cd"):
        o[f"{n}_g"], o[f"{n}_b"] = columns(a[f"{n}_ln_g_2"][0]), columns(a[f"{n}_ln_b_2"][0])
        o[f"{n}_w_out"] = weight_tiles(a[f"{n}_w_out_2"][0])
    o["ab_w_in"] = weight_tiles(a["ab_w_in_2"][0])
    o["pool_w"] = np.ascontiguousarray(a["ab_pool_w_2"][0].transpose(1, 0, 2))
    o["pool_scale"] = columns(a["ab_pool_scale_2"][0])
    inv = []
    for w in POOLS:
        row = []
        for n in (SEQ, CTX):
            p = np.arange(n)
            row.append(1.0 / (np.minimum(p + w - w // 2, n) - np.maximum(p - w // 2, 0)))
        inv.append(np.tile(np.concatenate(row), (P, 1)))
    o["inv_count"] = np.stack(inv).astype(f)
    o["sgu_w"] = np.ascontiguousarray(a["ab_sgu_w_2"][0].transpose(2, 0, 1))
    o["sgu_b"] = np.ascontiguousarray(np.broadcast_to(a["ab_sgu_b_2"][0][None], (P, 4, P)))
    w = a["cd_w_in_2"][0]
    swap = np.concatenate([np.arange(8, 16), np.arange(0, 8), np.arange(24, 32), np.arange(16, 24)])
    kr = w[:, 1408:1440]
    o["cd_w_in"] = weight_tiles(np.concatenate([w[:, 0:1280], w[:, 1440:]], 1))
    o["cd_w_kv"] = weight_tiles(np.concatenate([w[:, 1280:1408], kr, kr, kr, kr[:, swap]], 1))
    wq = a["cd_w_q_up_2"][0].reshape(QL // P, P, NH, NOPE + ROPE)
    o["w_q_up"] = np.ascontiguousarray(np.concatenate([wq, wq[..., NOPE + swap]], -1).transpose(1, 0, 2, 3))
    wkv = a["cd_w_kv_up_2"][0].reshape(KVL, NH, NOPE + VD)
    o["w_k_up"] = np.ascontiguousarray(wkv[..., :NOPE])
    o["w_v_up"] = np.ascontiguousarray(wkv[..., NOPE:]).reshape(KVL, NH * VD)
    o["q_norm"], o["kv_norm"] = columns(a["cd_q_norm_2"][0]), columns(a["cd_kv_norm_2"][0])
    inv_f = 10000.0 ** (-np.arange(0, 16, 2) / 16)
    pos = np.arange(SEQ)
    ang = np.concatenate([np.outer(inv_f, pos // 64)] * 2 + [np.outer(inv_f, pos % 64)] * 2)
    sign = np.where(np.arange(ROPE) % 16 < 8, -1.0, 1.0)[:, None]
    rope = np.zeros((P, T2), f)
    rope[NOPE:NOPE + ROPE] = 1.0
    rope[NOPE:NOPE + ROPE, :SEQ] = np.cos(ang)
    rope[NOPE + ROPE:, :SEQ] = np.sin(ang) * sign
    o["rope"] = rope
    p = np.outer(np.arange(P), np.arange(P)) % P * (2 * np.pi / P)
    o["dft_features"] = (np.concatenate([np.cos(p), np.sin(p)], 1) / np.sqrt(P)).astype(f)
    p = np.outer(np.arange(SEQ), np.arange(SEQ)) % SEQ * (2 * np.pi / SEQ)
    d = (np.stack([np.cos(p), -np.sin(p)]) / np.sqrt(SEQ)).astype(f)
    d = d[:, :SEQ // 2].reshape(2, SEQ // 2, SEQ // 2, 2).transpose(0, 1, 3, 2)
    o["dft_tokens"] = np.ascontiguousarray(d.reshape(2, SEQ // 2 // P, P, SEQ).transpose(2, 0, 1, 3))
    o["fnet_w"] = np.ascontiguousarray(a["cd_fnet_w_2"][0].reshape(4, P, 512).transpose(1, 0, 2))
    o["ident"] = np.eye(P, dtype=f)
    o["chunk_mask"] = np.tile((np.arange(T1) % CH != 0).astype(f), (P, 1))
    s, u = np.arange(P)[:, None], np.arange(P)[None, :]
    o["causal"] = np.ascontiguousarray(np.broadcast_to(((s // CH == u // CH) & (s <= u))[:, None, :], (P, 9, P)))
    o["causal"] = o["causal"].astype(f)
    return o


def kernel(**inputs):
    import concourse.bacc as bacc
    from concourse.bass_utils import run_bass_kernel_spmd
    arrays = layout({k: np.asarray(v) for k, v in inputs.items()})
    nc = bacc.Bacc("TRN2", target_bir_lowering=False, num_devices=1)
    t = {n: nc.dram_tensor(n, v.shape, F32, kind="ExternalInput").ap() for n, v in arrays.items()}
    t["out"] = nc.dram_tensor("out", (DT, P, SEQ), F32, kind="ExternalOutput").ap()
    build(nc, t)
    r = run_bass_kernel_spmd(nc, [arrays], core_ids=[0])
    y = r.results[0]["out"]
    return np.ascontiguousarray(y.reshape(D, SEQ).T).reshape(1, SEQ, D)
```
